# Optimizing a Trainium2 kernel written in Bass

```python
import math
import jax
import jax.numpy as jnp
from jax import lax
import numpy as np
import jax, jax.numpy as jnp

D_MODEL = 1024
BATCH = 1
SEQ = 256
DEPTH = 1

HEAD_DIM = 64
NSA_HEADS = 8
NSA_GROUPS = 2
NSA_REP = NSA_HEADS // NSA_GROUPS
CMP_BLOCK = 32
CMP_STRIDE = 16
CMP_HIDDEN = 256
SEL_BLOCK = 64
SEL_TOPK = 16
NSA_WINDOW = 512
NSA_QBLOCK = 128
SWA_HEADS = 8
SWA_KV_HEADS = 2
SWA_REP = SWA_HEADS // SWA_KV_HEADS
SWA_WINDOW = 128
SWA_QBLOCK = 128
D_FF = 4 * D_MODEL
NUM_BUCKETS = 32
MAX_DISTANCE = 1024
N_BIAS_HEADS = NSA_HEADS + SWA_HEADS
RMS_EPS = 1e-6

NSA_Q_DIM = NSA_HEADS * HEAD_DIM
NSA_KV_DIM = NSA_GROUPS * HEAD_DIM
SWA_Q_DIM = SWA_HEADS * HEAD_DIM
SWA_KV_DIM = SWA_KV_HEADS * HEAD_DIM
IN_SIZES = (NSA_Q_DIM,) + (NSA_KV_DIM,) * 6 + (3 * NSA_HEADS, SWA_Q_DIM, SWA_KV_DIM, SWA_KV_DIM, D_MODEL, D_MODEL)
IN_DIM = int(sum(IN_SIZES))
IN_OFFSETS = tuple(int(o) for o in np.cumsum(IN_SIZES)[:-1])


def rms_norm(x, g):
    xf = x.astype(jnp.float32)
    y = xf * lax.rsqrt(jnp.mean(xf * xf, axis=-1, keepdims=True) + RMS_EPS)
    return (y * g.astype(jnp.float32)).astype(x.dtype)

def t5_bucket(dist):
    max_exact = NUM_BUCKETS // 2
    d = jnp.maximum(dist, 0)
    df = jnp.maximum(d, 1).astype(jnp.float32)
    large = max_exact + (jnp.log(df / max_exact) / math.log(MAX_DISTANCE / max_exact)
                         * (NUM_BUCKETS - max_exact)).astype(jnp.int32)
    large = jnp.minimum(large, NUM_BUCKETS - 1)
    return jnp.where(d < max_exact, d, large)

def masked_softmax(s, mask):
    s = jnp.where(mask, s.astype(jnp.float32), -jnp.inf)
    m = jnp.max(s, axis=-1, keepdims=True)
    m = jnp.where(jnp.isfinite(m), m, 0.0)
    e = jnp.exp(s - m)
    return e / jnp.maximum(jnp.sum(e, axis=-1, keepdims=True), 1e-30)

def compress_kv(kv, pos, w1, w2):
    b, s, g, d = kv.shape
    n_cmp = (s - CMP_BLOCK) // CMP_STRIDE + 1
    kb = kv.reshape(b, s // CMP_STRIDE, CMP_STRIDE, g, d)
    blocks = jnp.concatenate([kb[:, o:o + n_cmp] for o in range(CMP_BLOCK // CMP_STRIDE)], axis=2)
    blocks = blocks + pos[None, None, :, None, :]
    flat = blocks.transpose(0, 1, 3, 2, 4).reshape(b, n_cmp, g, CMP_BLOCK * d)
    return jax.nn.gelu(flat @ w1) @ w2

def nsa_attention(q, kc, vc, k_slc, v_slc, k_win, v_win, gates, bias_tab):
    b, s, g, r, d = q.shape
    scale = d ** -0.5
    n_cmp = kc.shape[1]
    n_sel = s // SEL_BLOCK
    topk = min(SEL_TOPK, n_sel)
    n_chunks = s // NSA_QBLOCK
    ratio = SEL_BLOCK // CMP_STRIDE
    pad_front = CMP_BLOCK // CMP_STRIDE - 1
    pad_back = n_sel * ratio - n_cmp
    ks_blk = k_slc.reshape(b, n_sel, SEL_BLOCK, g, d).transpose(0, 3, 1, 2, 4)
    vs_blk = v_slc.reshape(b, n_sel, SEL_BLOCK, g, d).transpose(0, 3, 1, 2, 4)
    kw = jnp.pad(k_win, ((0, 0), (NSA_WINDOW, 0), (0, 0), (0, 0)))
    vw = jnp.pad(v_win, ((0, 0), (NSA_WINDOW, 0), (0, 0), (0, 0)))
    cmp_end = jnp.arange(n_cmp) * CMP_STRIDE + CMP_BLOCK - 1
    b_idx = jnp.arange(b)[:, None, None, None]
    g_idx = jnp.arange(g)[None, :, None, None]
    win_off = jnp.arange(NSA_QBLOCK + NSA_WINDOW) - NSA_WINDOW
    sel_off = jnp.arange(SEL_BLOCK)
    blk_ids = jnp.arange(n_sel)

    def chunk(args):
        qc, gc, ci = args
        t = ci * NSA_QBLOCK + jnp.arange(NSA_QBLOCK)
        sc = jnp.einsum('bqgrd,bngd->bgrqn', qc, kc).astype(jnp.float32) * scale
        pc = masked_softmax(sc, cmp_end[None, :] <= t[:, None])
        oc = jnp.einsum('bgrqn,bngd->bqgrd', pc.astype(vc.dtype), vc)
        pg = jnp.pad(pc.sum(axis=2), ((0, 0), (0, 0), (0, 0), (pad_front, pad_back)))
        ps = sum(pg[..., o:o + n_sel * ratio:ratio] for o in range(ratio + pad_front))
        cur = t // SEL_BLOCK
        valid = blk_ids[None, :] <= cur[:, None]
        forced = (blk_ids[None, :] == 0) | (blk_ids[None, :] == cur[:, None]) | (blk_ids[None, :] == cur[:, None] - 1)
        score = jnp.where(valid, jnp.where(forced, jnp.inf, ps), -jnp.inf)
        _, idx = lax.top_k(score, topk)
        kg = ks_blk[b_idx, g_idx, idx]
        vg = vs_blk[b_idx, g_idx, idx]
        pos = idx[..., None] * SEL_BLOCK + sel_off
        tq = t[None, None, :, None, None]
        bias_s = bias_tab[t5_bucket(tq - pos), g_idx[..., None]]
        ss = jnp.einsum('bqgrd,bgqjkd->bgrqjk', qc, kg).astype(jnp.float32) * scale + jnp.moveaxis(bias_s, -1, 2)
        n_keys = topk * SEL_BLOCK
        mask_s = (pos <= tq).reshape(b, g, 1, NSA_QBLOCK, n_keys)
        p_s = masked_softmax(ss.reshape(b, g, r, NSA_QBLOCK, n_keys), mask_s)
        o_s = jnp.einsum('bgrqn,bgqnd->bqgrd', p_s.astype(vg.dtype), vg.reshape(b, g, NSA_QBLOCK, n_keys, d))
        kwc = lax.dynamic_slice_in_dim(kw, ci * NSA_QBLOCK, NSA_QBLOCK + NSA_WINDOW, axis=1)
        vwc = lax.dynamic_slice_in_dim(vw, ci * NSA_QBLOCK, NSA_QBLOCK + NSA_WINDOW, axis=1)
        spos = ci * NSA_QBLOCK + win_off
        dist = t[:, None] - spos[None, :]
        mask_w = (dist >= 0) & (dist < NSA_WINDOW) & (spos[None, :] >= 0)
        bias_w = jnp.transpose(bias_tab[t5_bucket(dist)], (2, 3, 0, 1))
        sw = jnp.einsum('bqgrd,bkgd->bgrqk', qc, kwc).astype(jnp.float32) * scale + bias_w
        p_w = masked_softmax(sw, mask_w)
        o_w = jnp.einsum('bgrqk,bkgd->bqgrd', p_w.astype(vwc.dtype), vwc)
        gs = jax.nn.sigmoid(gc.astype(jnp.float32)).astype(qc.dtype)
        return gs[..., 0:1] * oc + gs[..., 1:2] * o_s + gs[..., 2:3] * o_w

    q_ch = q.reshape(b, n_chunks, NSA_QBLOCK, g, r, d).swapaxes(0, 1)
    g_ch = gates.reshape(b, n_chunks, NSA_QBLOCK, g, r, 3).swapaxes(0, 1)
    out = lax.map(chunk, (q_ch, g_ch, jnp.arange(n_chunks)))
    return out.swapaxes(0, 1).reshape(b, s, g * r * d)

def swa_sink_attention(q, k, v, sinks, bias_tab):
    b, s, g, r, d = q.shape
    scale = d ** -0.5
    nb = s // SWA_QBLOCK
    qb = q.reshape(b, nb, SWA_QBLOCK, g, r, d)
    kb = k.reshape(b, nb, SWA_QBLOCK, g, d)
    vb = v.reshape(b, nb, SWA_QBLOCK, g, d)
    pad = ((0, 0), (1, 0), (0, 0), (0, 0), (0, 0))
    kk = jnp.concatenate([jnp.pad(kb, pad)[:, :-1], kb], axis=2)
    vv = jnp.concatenate([jnp.pad(vb, pad)[:, :-1], vb], axis=2)
    qi = jnp.arange(SWA_QBLOCK)[:, None]
    ki = jnp.arange(2 * SWA_QBLOCK)[None, :]
    dist = qi - ki + SWA_QBLOCK
    band = (dist >= 0) & (dist < SWA_WINDOW)
    first = (jnp.arange(nb) > 0)[:, None, None] | (ki >= SWA_QBLOCK)[None]
    mask = (band[None] & first)[None, :, None, None]
    bias = jnp.transpose(bias_tab[t5_bucket(dist)], (2, 3, 0, 1))
    sc = jnp.einsum('bnqgrd,bnkgd->bngrqk', qb, kk).astype(jnp.float32) * scale + bias
    sc = jnp.where(mask, sc, -jnp.inf)
    sink = sinks.astype(jnp.float32)[None, None, :, :, None, None]
    m = jnp.maximum(jnp.max(sc, axis=-1, keepdims=True), sink)
    e = jnp.exp(sc - m)
    p = e / (jnp.sum(e, axis=-1, keepdims=True) + jnp.exp(sink - m))
    o = jnp.einsum('bngrqk,bnkgd->bnqgrd', p.astype(vv.dtype), vv)
    return o.reshape(b, s, g * r * d)

def first_inputs(seed: int = 0) -> dict:
    key = jax.random.key(seed)
    ks = jax.random.split(key, 20)
    nrm = lambda k, shape, scale: jax.random.normal(k, shape, jnp.float32) * scale
    gain = lambda k: 1.0 + nrm(k, (DEPTH, D_MODEL), 0.05)
    cin = CMP_BLOCK * HEAD_DIM
    return {
        'x': nrm(ks[0], (BATCH, SEQ, D_MODEL), 1.0),
        'norm_mix_pre': gain(ks[1]),
        'norm_mix_post': gain(ks[2]),
        'norm_mlp_pre': gain(ks[3]),
        'norm_mlp_post': gain(ks[4]),
        'w_in': nrm(ks[5], (DEPTH, D_MODEL, IN_DIM), D_MODEL ** -0.5),
        'cmp_pos_k': nrm(ks[6], (DEPTH, CMP_BLOCK, HEAD_DIM), 0.5),
        'cmp_w1_k': nrm(ks[7], (DEPTH, cin, CMP_HIDDEN), cin ** -0.5),
        'cmp_w2_k': nrm(ks[8], (DEPTH, CMP_HIDDEN, HEAD_DIM), CMP_HIDDEN ** -0.5),
        'cmp_pos_v': nrm(ks[9], (DEPTH, CMP_BLOCK, HEAD_DIM), 0.5),
        'cmp_w1_v': nrm(ks[10], (DEPTH, cin, CMP_HIDDEN), cin ** -0.5),
        'cmp_w2_v': nrm(ks[11], (DEPTH, CMP_HIDDEN, HEAD_DIM), CMP_HIDDEN ** -0.5),
        'attn_sinks': nrm(ks[12], (DEPTH, SWA_HEADS), 0.5),
        'rel_bias': nrm(ks[13], (NUM_BUCKETS, N_BIAS_HEADS), 0.5),
        'w_up_nsa': nrm(ks[14], (DEPTH, NSA_Q_DIM, D_MODEL), NSA_Q_DIM ** -0.5),
        'w_up_swa': nrm(ks[15], (DEPTH, SWA_Q_DIM, D_MODEL), SWA_Q_DIM ** -0.5),
        'w_out': nrm(ks[16], (DEPTH, D_MODEL, D_MODEL), D_MODEL ** -0.5),
        'w_mlp_in': nrm(ks[17], (DEPTH, D_MODEL, D_FF), D_MODEL ** -0.5),
        'w_mlp_out': nrm(ks[18], (DEPTH, D_FF, D_MODEL), D_FF ** -0.5),
    }

def first_block(x, norm_mix_pre, norm_mix_post, norm_mlp_pre, norm_mlp_post, w_in,
              cmp_pos_k, cmp_w1_k, cmp_w2_k, cmp_pos_v, cmp_w1_v, cmp_w2_v,
              attn_sinks, rel_bias, w_up_nsa, w_up_swa, w_out, w_mlp_in, w_mlp_out):
    b, s, _ = x.shape
    bias_nsa = rel_bias[:, :NSA_HEADS].reshape(NUM_BUCKETS, NSA_GROUPS, NSA_REP)
    bias_swa = rel_bias[:, NSA_HEADS:].reshape(NUM_BUCKETS, SWA_KV_HEADS, SWA_REP)
    h = x
    for l in range(DEPTH):
        u = rms_norm(h, norm_mix_pre[l])
        (q_n, kc_n, vc_n, ks_n, vs_n, kw_n, vw_n, g_n,
         q_s, k_s, v_s, gate_a, gate_b) = jnp.split(u @ w_in[l], IN_OFFSETS, axis=-1)
        kvr = lambda t_: t_.reshape(b, s, NSA_GROUPS, HEAD_DIM)
        kc = compress_kv(kvr(kc_n), cmp_pos_k[l], cmp_w1_k[l], cmp_w2_k[l])
        vc = compress_kv(kvr(vc_n), cmp_pos_v[l], cmp_w1_v[l], cmp_w2_v[l])
        o_a = nsa_attention(q_n.reshape(b, s, NSA_GROUPS, NSA_REP, HEAD_DIM), kc, vc,
                            kvr(ks_n), kvr(vs_n), kvr(kw_n), kvr(vw_n),
                            g_n.reshape(b, s, NSA_GROUPS, NSA_REP, 3), bias_nsa)
        o_b = swa_sink_attention(q_s.reshape(b, s, SWA_KV_HEADS, SWA_REP, HEAD_DIM),
                                 k_s.reshape(b, s, SWA_KV_HEADS, HEAD_DIM),
                                 v_s.reshape(b, s, SWA_KV_HEADS, HEAD_DIM),
                                 attn_sinks[l].reshape(SWA_KV_HEADS, SWA_REP), bias_swa)
        y = jax.nn.sigmoid(gate_a) * (o_a @ w_up_nsa[l]) + jax.nn.sigmoid(gate_b) * (o_b @ w_up_swa[l])
        h = h + rms_norm(y @ w_out[l], norm_mix_post[l])
        u = rms_norm(h, norm_mlp_pre[l])
        f = jnp.square(jax.nn.relu(u @ w_mlp_in[l])) @ w_mlp_out[l]
        h = h + rms_norm(f, norm_mlp_post[l])
    return h


DEPTH_2 = 2

N_A_LAYERS = DEPTH_2 // 2
N_B_LAYERS = DEPTH_2 - N_A_LAYERS
POOL_WINDOWS = (2, 4, 8, 16)
N_POOL_GROUPS = len(POOL_WINDOWS)
POOL_GROUP = D_MODEL // N_POOL_GROUPS
HEAD_DIM_2 = 128
N_HEADS = D_MODEL // HEAD_DIM_2
MOBA_BLOCK = 256
MOBA_TOPK = 3
Q_CHUNK = 64
D_FF_2 = ((8 * D_MODEL // 3 + 255) // 256) * 256
ROPE_THETA = 10000.0
EPS = 1e-6
N_SUBLAYERS = 3
N_MOD = 3 * N_SUBLAYERS
MACARON_WEIGHT = 0.5


def rms_norm_2(x, g):
    xf = x.astype(jnp.float32)
    y = xf * lax.rsqrt(jnp.mean(xf * xf, axis=-1, keepdims=True) + EPS)
    return (y * g.astype(jnp.float32)).astype(x.dtype)

def modulate(h, shift, scale):
    return h * (1.0 + scale[:, None, :]) + shift[:, None, :]

def swiglu(h, w_in, w_out):
    gu = h @ w_in
    g, u = jnp.split(gu, 2, axis=-1)
    return (jax.nn.silu(g) * u) @ w_out

def rope_tables(T):
    pos = jnp.arange(T, dtype=jnp.float32)
    inv = ROPE_THETA ** (-jnp.arange(0, HEAD_DIM_2, 2, dtype=jnp.float32) / HEAD_DIM_2)
    ang = pos[:, None] * inv[None, :]
    return jnp.cos(ang), jnp.sin(ang)

def rope(x, cos, sin):
    half = HEAD_DIM_2 // 2
    xf = x.astype(jnp.float32)
    x1, x2 = xf[..., :half], xf[..., half:]
    c = cos[None, :, None, :]
    s = sin[None, :, None, :]
    return jnp.concatenate([x1 * c - x2 * s, x2 * c + x1 * s], axis=-1).astype(x.dtype)

def pool_mixer(h, w_pool, pool_scale):
    B, T, _ = h.shape
    hg = h.astype(jnp.float32).reshape(B, T, N_POOL_GROUPS, POOL_GROUP)
    cs = jnp.cumsum(hg, axis=1)
    t = jnp.arange(T)
    outs = []
    for gi, w in enumerate(POOL_WINDOWS):
        c_g = cs[:, :, gi]
        prev = jnp.pad(c_g, ((0, 0), (w, 0), (0, 0)))[:, :T]
        cnt = jnp.minimum(t + 1, w).astype(jnp.float32)[None, :, None]
        outs.append((c_g - prev) / cnt - hg[:, :, gi])
    pooled = jnp.stack(outs, axis=2).astype(h.dtype)
    y = jnp.einsum('btgc,gcd->btgd', pooled, w_pool).reshape(B, T, D_MODEL)
    return y * pool_scale

def shared_kv(h, c_silu, kv_norm, kv_ada_w, kv_ada_b, w_kv, k_norm, cos, sin):
    B, T, _ = h.shape
    shift, scale = jnp.split(c_silu @ kv_ada_w + kv_ada_b, 2, axis=-1)
    hn = modulate(rms_norm_2(h, kv_norm), shift, scale)
    k, v = jnp.split(hn @ w_kv, 2, axis=-1)
    k = rope(rms_norm_2(k.reshape(B, T, N_HEADS, HEAD_DIM_2), k_norm), cos, sin)
    v = v.reshape(B, T, N_HEADS, HEAD_DIM_2)
    nb = -(-T // MOBA_BLOCK)
    pad = nb * MOBA_BLOCK - T
    k = jnp.pad(k.transpose(0, 2, 1, 3), ((0, 0), (0, 0), (0, pad), (0, 0)))
    v = jnp.pad(v.transpose(0, 2, 1, 3), ((0, 0), (0, 0), (0, pad), (0, 0)))
    k_blocks = k.reshape(B, N_HEADS, nb, MOBA_BLOCK, HEAD_DIM_2)
    v_blocks = v.reshape(B, N_HEADS, nb, MOBA_BLOCK, HEAD_DIM_2)
    k_mean = jnp.mean(k_blocks.astype(jnp.float32), axis=3).astype(k.dtype)
    return k_blocks, v_blocks, k_mean

def moba_attention(q, k_blocks, v_blocks, k_mean):
    B, H, T, _ = q.shape
    nb = k_blocks.shape[2]
    topk = min(MOBA_TOPK, nb)
    n_chunks = T // Q_CHUNK
    bi = jnp.arange(B)[:, None, None, None]
    hi = jnp.arange(H)[None, :, None, None]
    sm_scale = HEAD_DIM_2 ** -0.5

    def chunk(ci):
        q0 = ci * Q_CHUNK
        qc = lax.dynamic_slice_in_dim(q, q0, Q_CHUNK, axis=2)
        n = q0 // MOBA_BLOCK
        gate = jnp.einsum('bhqd,bhnd->bhqn', qc, k_mean).astype(jnp.float32)
        gate = jnp.where(jnp.arange(nb) < n, gate, -jnp.inf)
        _, idx = lax.top_k(gate, topk)
        valid = jnp.arange(topk) < n
        k_sel = k_blocks[bi, hi, idx]
        v_sel = v_blocks[bi, hi, idx]
        s_sel = jnp.einsum('bhqd,bhqkjd->bhqkj', qc, k_sel).astype(jnp.float32) * sm_scale
        s_sel = jnp.where(valid[:, None], s_sel, -jnp.inf).reshape(B, H, Q_CHUNK, topk * MOBA_BLOCK)
        k_own = lax.dynamic_index_in_dim(k_blocks, n, axis=2, keepdims=False)
        v_own = lax.dynamic_index_in_dim(v_blocks, n, axis=2, keepdims=False)
        s_own = jnp.einsum('bhqd,bhkd->bhqk', qc, k_own).astype(jnp.float32) * sm_scale
        qpos = q0 + jnp.arange(Q_CHUNK)
        kpos = n * MOBA_BLOCK + jnp.arange(MOBA_BLOCK)
        s_own = jnp.where(kpos[None, :] <= qpos[:, None], s_own, -jnp.inf)
        p = jax.nn.softmax(jnp.concatenate([s_sel, s_own], axis=-1), axis=-1).astype(v_blocks.dtype)
        p_sel = p[..., :topk * MOBA_BLOCK].reshape(B, H, Q_CHUNK, topk, MOBA_BLOCK)
        p_own = p[..., topk * MOBA_BLOCK:]
        return (jnp.einsum('bhqkj,bhqkjd->bhqd', p_sel, v_sel)
                + jnp.einsum('bhqk,bhkd->bhqd', p_own, v_own))

    outs = lax.map(chunk, jnp.arange(n_chunks))
    return outs.transpose(1, 2, 0, 3, 4).reshape(B, H, T, HEAD_DIM_2)

def second_inputs(seed: int = 0) -> dict:
    key = jax.random.key(seed)
    ks = jax.random.split(key, 20)
    f32 = jnp.float32
    D = D_MODEL
    nrm = lambda k, shape, s: (jax.random.normal(k, shape, f32) * s)
    return {
        "x": nrm(ks[0], (BATCH, SEQ, D), 1.0),
        "c": nrm(ks[1], (BATCH, D), 1.0),
        "ada_w": nrm(ks[2], (DEPTH_2, D, N_MOD * D), 0.1 * D ** -0.5),
        "ada_b": nrm(ks[3], (DEPTH_2, N_MOD * D), 0.05),
        "norm_g": 1.0 + nrm(ks[4], (DEPTH_2, N_SUBLAYERS, D), 0.05),
        "ffn_w_in": nrm(ks[5], (DEPTH_2, 2, D, 2 * D_FF_2), D ** -0.5),
        "ffn_w_out": nrm(ks[6], (DEPTH_2, 2, D_FF_2, D), D_FF_2 ** -0.5),
        "pool_w": nrm(ks[7], (N_A_LAYERS, N_POOL_GROUPS, POOL_GROUP, POOL_GROUP), POOL_GROUP ** -0.5),
        "pool_scale": 1.0 + nrm(ks[8], (N_A_LAYERS, D), 0.1),
        "kv_norm": 1.0 + nrm(ks[9], (D,), 0.05),
        "kv_ada_w": nrm(ks[10], (D, 2 * D), 0.1 * D ** -0.5),
        "kv_ada_b": nrm(ks[11], (2 * D,), 0.05),
        "w_kv": nrm(ks[12], (D, 2 * D), D ** -0.5),
        "k_norm": 1.0 + nrm(ks[13], (HEAD_DIM_2,), 0.05),
        "w_q": nrm(ks[14], (N_B_LAYERS, D, D), D ** -0.5),
        "q_norm": 1.0 + nrm(ks[15], (N_B_LAYERS, HEAD_DIM_2), 0.05),
        "w_o": nrm(ks[16], (N_B_LAYERS, D, D), D ** -0.5),
    }

def second_block(x, c, ada_w, ada_b, norm_g, ffn_w_in, ffn_w_out, pool_w, pool_scale,
              kv_norm, kv_ada_w, kv_ada_b, w_kv, k_norm, w_q, q_norm, w_o):
    B, T, D = x.shape
    c_silu = jax.nn.silu(c)
    cos, sin = rope_tables(T)
    kv = None
    for layer in range(DEPTH_2):
        mods = jnp.split(c_silu @ ada_w[layer] + ada_b[layer], N_MOD, axis=-1)
        sh, sc, g = mods[0], mods[1], mods[2]
        h = modulate(rms_norm_2(x, norm_g[layer, 0]), sh, sc)
        x = x + MACARON_WEIGHT * (1.0 + g)[:, None, :] * swiglu(h, ffn_w_in[layer, 0], ffn_w_out[layer, 0])
        sh, sc, g = mods[3], mods[4], mods[5]
        h = modulate(rms_norm_2(x, norm_g[layer, 1]), sh, sc)
        if layer < N_A_LAYERS:
            y = pool_mixer(h, pool_w[layer], pool_scale[layer])
        else:
            j = layer - N_A_LAYERS
            k_blocks, v_blocks, k_mean = kv
            q = (h @ w_q[j]).reshape(B, T, N_HEADS, HEAD_DIM_2)
            q = rope(rms_norm_2(q, q_norm[j]), cos, sin).transpose(0, 2, 1, 3)
            att = moba_attention(q, k_blocks, v_blocks, k_mean)
            y = att.transpose(0, 2, 1, 3).reshape(B, T, D) @ w_o[j]
        x = x + (1.0 + g)[:, None, :] * y
        sh, sc, g = mods[6], mods[7], mods[8]
        h = modulate(rms_norm_2(x, norm_g[layer, 2]), sh, sc)
        x = x + MACARON_WEIGHT * (1.0 + g)[:, None, :] * swiglu(h, ffn_w_in[layer, 1], ffn_w_out[layer, 1])
        if layer == N_A_LAYERS - 1:
            kv = shared_kv(x, c_silu, kv_norm, kv_ada_w, kv_ada_b, w_kv, k_norm, cos, sin)
    return x


def setup_inputs(seed=0):
    out = dict(first_inputs(seed))
    for name, value in second_inputs(seed + 1).items():
        if name != "x":
            out[name + "_2"] = value
    return out


def reference(
    x, norm_mix_pre, norm_mix_post, norm_mlp_pre, norm_mlp_post, w_in, cmp_pos_k, cmp_w1_k,
    cmp_w2_k, cmp_pos_v, cmp_w1_v, cmp_w2_v, attn_sinks, rel_bias, w_up_nsa, w_up_swa, w_out,
    w_mlp_in, w_mlp_out, c_2, ada_w_2, ada_b_2, norm_g_2, ffn_w_in_2, ffn_w_out_2, pool_w_2,
    pool_scale_2, kv_norm_2, kv_ada_w_2, kv_ada_b_2, w_kv_2, k_norm_2, w_q_2, q_norm_2, w_o_2,
):
    x = first_block(
        x, norm_mix_pre, norm_mix_post, norm_mlp_pre, norm_mlp_post, w_in, cmp_pos_k, cmp_w1_k,
        cmp_w2_k, cmp_pos_v, cmp_w1_v, cmp_w2_v, attn_sinks, rel_bias, w_up_nsa, w_up_swa,
        w_out, w_mlp_in, w_mlp_out,
    )
    return second_block(
        x, c_2, ada_w_2, ada_b_2, norm_g_2, ffn_w_in_2, ffn_w_out_2, pool_w_2, pool_scale_2,
        kv_norm_2, kv_ada_w_2, kv_ada_b_2, w_kv_2, k_norm_2, w_q_2, q_norm_2, w_o_2,
    )


_drawn_inputs = setup_inputs


def setup_inputs(seed=0):
    import zlib

    import numpy as np

    out = dict(_drawn_inputs(seed))
    spreads = {}
    factors = {'attn_sinks': 6.858, 'kv_norm_2': 4.908, 'k_norm_2': 8.0, 'q_norm_2': 8.0}
    for name, (base, spread) in spreads.items():
        noise = np.random.default_rng([zlib.crc32(name.encode()), seed]).standard_normal(out[name].shape)
        drawn = base * np.exp(spread * noise) if base else spread * noise
        out[name] = jnp.asarray(drawn.astype(out[name].dtype))
    for name, factor in factors.items():
        out[name] = (out[name] * factor).astype(out[name].dtype)
    return out
```

```python
from contextlib import ExitStack
import math

import numpy as np

import concourse.bass as bass
from concourse import mybir

F32 = mybir.dt.float32
F32R = mybir.dt.float32r
ALU = mybir.AluOpType
ACT = mybir.ActivationFunctionType
AX = mybir.AxisListType

P = 128
T = 256
D = 1024
KT = D // P
HD = 64
NH = 8
NCMP = 15
FF = 4096
FF2 = 2816
SLOT = 2048
NEG = -1.0e30
FLOOR = -1.0e29
EPS = 1e-6
NMOD = 20

MLP_N = FF // 256
FFN_N = FF2 // 256


def plan_slots():
    start, ring = {}, []

    def phase(name, positions):
        start[name] = len(ring)
        ring.extend(positions)

    phase("in", [n % 3 for n in range(16)])
    phase("cmp", [1, 2, 0, 1])
    phase("up", [2, 0, 1, 2])
    phase("out", [0, 1, 2, 0])
    order = [0, 2]
    for i in range(MLP_N):
        order.append(1)
        if i + 2 < MLP_N:
            order.append(0 if i % 2 == 0 else 2)
    phase("mlp", order)
    ffn = [0, 1] + [0, 1, 2] * (FFN_N - 1) + [2]
    phase("ffn0", ffn)
    phase("pool", [1])
    phase("ffn1", ffn)
    phase("kv", [0, 1, 2, 0, 1, 2, 0, 1])
    phase("ffn2", ffn)
    phase("wq", [0, 1, 2, 0])
    phase("wo", [1, 2, 0, 1])
    phase("ffn3", ffn)
    return start, ring


START, RING = plan_slots()


def before(n):
    for m in range(n - 1, -1, -1):
        if RING[m] == RING[n]:
            return m + 1
    return 0


def filled(n):
    return sum(32 if 0 <= m - START["up"] < 4 else 16 for m in range(n + 1) if RING[m] == RING[n])


ADA_SESSIONS = [[0, 1], [2, 3, 4], [5, 6], [7, 8], [9]]
ADA_BUF = []
ADA_ACC = []
ADA_START = []
for _s in ADA_SESSIONS:
    ADA_START.append(len(ADA_BUF))
    for _k in range(KT):
        for _a in range(len(_s)):
            ADA_BUF.append(_a % 2)
            ADA_ACC.append(_a)
PAIR_MODS = [(0, 1), (2, 3), (4, 5), (6, 7), (8, 17), (18, 19), (9, 10), (11, 12), (13, 14), (15, 16)]


def ada_before(m):
    for q in range(m - 1, -1, -1):
        if ADA_BUF[q] == ADA_BUF[m]:
            return q + 1
    return 0


def ada_filled(m):
    return 16 * sum(1 for q in range(m + 1) if ADA_BUF[q] == ADA_BUF[m])


def ada_acc_before(m):
    for q in range(m - 1, -1, -1):
        if ADA_ACC[q] == ADA_ACC[m]:
            return q + 1
    return 0


VEC = {"mix_pre": 0, "mix_post": 8, "mlp_pre": 16, "mlp_post": 24, "norm_g": 32, "pool_scale": 80,
       "kv_norm": 88, "c": 96, "k_norm": 104, "q_norm": 105}
NVEC = 106

CST = {}
_at = 0
for _n, _w in (("ident", 128), ("ones", 128), ("swap", 128), ("causal", 384), ("cos", 256), ("sin", 256),
               ("cmpmask", 32), ("poolrc", 64)):
    CST[_n] = (_at, _at + _w)
    _at += _w
NCST = _at


def shape_constants():
    c = np.zeros((P, NCST), np.float32)

    def put(name, a):
        lo, hi = CST[name]
        c[:, lo:hi] = a.reshape(P, hi - lo)

    q = np.arange(P)[:, None]
    put("ident", np.eye(P, dtype=np.float32))
    put("ones", np.ones((P, P), np.float32))
    put("swap", np.eye(P, dtype=np.float32)[:, (np.arange(P) + 64) % P])
    second = np.where(P + q - np.arange(T)[None] >= 0, 0.0, NEG)
    put("causal", np.concatenate([second[:, P:], second], 1).astype(np.float32))
    inv = (10000.0 ** (-(np.arange(0, P, 2) / float(P)))).astype(np.float32)
    ang = np.arange(T, dtype=np.float32)[:, None] * inv[None, :]
    cos, sin = np.cos(ang).T, np.sin(ang).T
    put("cos", np.concatenate([cos, cos], 0))
    put("sin", np.concatenate([-sin, sin], 0))
    end = np.arange(NCMP) * 16 + 31
    m = np.full((P, 2, 16), NEG, np.float32)
    for t in range(2):
        m[:, t, :NCMP] = np.where(end[None] <= t * P + q, 0.0, NEG)
    put("cmpmask", m)
    rc = np.stack([1.0 / np.minimum(np.arange(16) + 1, w) for w in (2, 4, 8, 16)]).astype(np.float32)
    put("poolrc", np.broadcast_to(rc[None], (P, 4, 16)))
    dist = 255 - np.arange(384)
    d = np.maximum(dist, 0)
    df = np.maximum(d, 1).astype(np.float32)
    large = 16 + (np.log(df / np.float32(16)) / np.float32(math.log(64)) * np.float32(16)).astype(np.int32)
    bucket = np.where(d < 16, d, np.minimum(large, 31))
    onehot = (bucket[None] == np.arange(32)[:, None]).astype(np.float32)
    mask = np.zeros((16, 384), np.float32)
    mask[:8] = np.where(dist < 0, NEG, 0.0)
    mask[8:] = np.where((dist < 0) | (dist >= 128), NEG, 0.0)
    return c, onehot, mask


NAMES = ["x", "norm_mix_pre", "norm_mix_post", "norm_mlp_pre", "norm_mlp_post", "w_in", "cmp_pos_k", "cmp_w1_k",
         "cmp_w2_k", "cmp_pos_v", "cmp_w1_v", "cmp_w2_v", "attn_sinks", "rel_bias", "w_up_nsa", "w_up_swa",
         "w_out", "w_mlp_in", "w_mlp_out", "c_2", "ada_w_2", "ada_b_2", "norm_g_2", "ffn_w_in_2", "ffn_w_out_2",
         "pool_w_2", "pool_scale_2", "kv_norm_2", "kv_ada_w_2", "kv_ada_b_2", "w_kv_2", "k_norm_2", "w_q_2",
         "q_norm_2", "w_o_2"]


def build(nc, A, cst_dram, onehot_dram, dmask_dram, bias_dram, out):
    with ExitStack() as ctx:
        def sb(name, shape, dt=F32):
            return ctx.enter_context(nc.sbuf_tensor(name, shape, dt))

        def sem(name):
            return ctx.enter_context(nc.semaphore(name))

        raw = sb("raw", [P, 3, SLOT])
        whi = sb("whi", [P, 3, SLOT], F32R)
        wlo = sb("wlo", [P, 3, SLOT], F32R)
        ada = sb("ada", [P, 2, SLOT])
        acc = sb("acc", [P, 3, SLOT])
        xT = sb("xT", [P, KT, T])
        full = sb("full", [P, KT, T])
        uhi = sb("uhi", [P, KT, T], F32R)
        ulo = sb("ulo", [P, KT, T], F32R)
        cst = sb("cst", [P, NCST])
        wide = sb("wide", [P, 4352])
        arena = sb("arena", [P, 5632])
        mix = sb("mix", [P, 2048])
        hsplit = sb("hsplit", [P, 2, 512], F32R)
        vec = sb("vec", [P, 112])
        adab = sb("adab", [P, NMOD * KT])
        mods = sb("mods", [P, NMOD, KT])
        scal = sb("scal", [P, 16, KT])
        csilu = sb("csilu", [P, KT])
        root = sb("root", [P, T])
        rstd = sb("rstd", [P, T])
        eps = sb("eps", [P, 1])
        sinks = sb("sinks", [P, 8])
        small = sb("small", [P, 3, 16])
        gate3 = sb("gate3", [P, 2, 24])
        wg = sb("wg", [P, KT, 24])
        posx = sb("posx", [P, 2, 16])
        h1 = sb("h1", [P, 2, 2, 32])
        kcT = sb("kcT", [P, 16])
        cmpS = sb("cmpS", [P, 3, 16])

        bank = [ctx.enter_context(nc.psum_tensor(f"bank{i}", [P, 512], F32)) for i in range(8)]

        def const(name):
            return cst[:, CST[name][0]:CST[name][1]]

        ident, ones = const("ident"), const("ones")
        SA = {"ffn0": 0, "pool": 1, "ffn1": 2, "kv": 3, "ffn2": 4, "moba": 5, "ffn3": 6}
        SC = {"ffn0": 7, "pool": 8, "ffn1": 9, "ffn2": 10, "moba": 11, "ffn3": 12}
        QSC = 13

        def cols(buf, a, *dims):
            n = int(np.prod(dims))
            v = buf[:, a:a + n]
            if len(dims) == 2:
                return v.rearrange("p (a b) -> p a b", a=dims[0])
            if len(dims) == 3:
                return v.rearrange("p (a b c) -> p a b c", a=dims[0], b=dims[1])
            return v

        gates = cols(wide, 0, 16, T)
        qn = cols(arena, 0, 4, T)
        qs = cols(arena, 1024, 4, T)
        kT = cols(arena, 2048, 3, T)
        vv = cols(arena, 2816, 3, 2, P)
        kvr = cols(arena, 3584, 2, T)
        kvx = cols(arena, 4096, 2, 2, T)
        vcs = arena[0:16, 5120:5248].rearrange("p (g d) -> p g d", g=2)
        w2 = cols(arena, 5248, 2, 2, HD)
        cmpE = cols(wide, 4096, 2, 8, 16)
        blk = cols(mix, 0, 2, 480)
        uhi_flat = uhi[:].rearrange("p a b -> p (a b)")
        ulo_flat = ulo[:].rearrange("p a b -> p (a b)")
        bparts = [(uhi_flat[:, 512 * a:512 * a + 480], ulo_flat[:, 512 * a:512 * a + 480]) for a in range(2)]
        vrows = cols(mix, 0, 4, P)
        onehot = mix[0:32, 512:896]
        dmask = mix[0:16, 896:1280]
        relb = mix[0:32, 1280:1296]
        bvec = mix[0:16, 1600:1984]
        bias = acc[:].rearrange("p a b -> p (a b)").rearrange("p (h c) -> p h c", h=16)
        prob = [mix[:, 384 * i:384 * i + 384] for i in range(3)]
        probT = [mix[:, 1152 + 384 * i:1536 + 384 * i] for i in range(2)]
        pcT = full[0:NCMP, :, :]
        act_g = mix[:, 0:512]
        hfull = mix[:, 512:1024]
        hhi, hlo = hsplit[:, 0, :], hsplit[:, 1, :]
        pool_a = cols(wide, 0, KT, 272)
        pool_b = cols(arena, 0, KT, 272)
        k2 = cols(wide, 0, KT, T)
        v2 = cols(wide, 2048, 2, D)
        q2 = cols(arena, 0, KT, T)
        tmp2 = cols(arena, 2048, KT, T)
        xin = full[:].rearrange("p a b -> p (a b)").rearrange("p (t d) -> p t d", t=2)

        loaded = [sem(f"loaded{i}") for i in range(3)]
        ada_loaded = [sem(f"ada_loaded{i}") for i in range(2)]
        consts_in = sem("consts_in")
        x_in = sem("x_in")
        hi_done = sem("hi_done")
        lo_done = sem("lo_done")
        pe_done = sem("pe_done")
        ada_used = sem("ada_used")
        ada_sum = sem("ada_sum")
        mods_done = sem("mods_done")
        vec_t = sem("vec_t")
        vec_done = sem("vec_done")
        c_ready = sem("c_ready")
        x_turned = sem("x_turned")
        x_ready = sem("x_ready")
        sq_ready = sem("sq_ready")
        ss_done = sem("ss_done")
        root_done = sem("root_done")
        rstd_done = sem("rstd_done")
        u_full = sem("u_full")
        u_hi = sem("u_hi")
        u_lo = sem("u_lo")
        in_taken = sem("in_taken")
        kvx_in = sem("kvx_in")
        gate_mm = sem("gate_mm")
        gate_done = sem("gate_done")
        blk_full = sem("blk_full")
        blk_hi = sem("blk_hi")
        blk_lo = sem("blk_lo")
        gelu_done = sem("gelu_done")
        ckv_mm = sem("ckv_mm")
        ckv_done = sem("ckv_done")
        bvec_mm = sem("bvec_mm")
        bvec_done = sem("bvec_done")
        bvec_out = sem("bvec_out")
        bias_in = sem("bias_in")
        cs_mm = sem("cs_mm")
        cs_dve = sem("cs_dve")
        cs_exp = sem("cs_exp")
        cs_prob = sem("cs_prob")
        cs_turned = sem("cs_turned")
        cs_done = sem("cs_done")
        s_mm = sem("s_mm")
        s_max = sem("s_max")
        s_exp = sem("s_exp")
        s_prob = sem("s_prob")
        s_turned = sem("s_turned")
        s_copied = sem("s_copied")
        s_pv = sem("s_pv")
        o_hi = sem("o_hi")
        o_lo = sem("o_lo")
        y_taken = sem("y_taken")
        y_full = sem("y_full")
        y_hi = sem("y_hi")
        y_lo = sem("y_lo")
        g_act = sem("g_act")
        h_full = sem("h_full")
        h_hi = sem("h_hi")
        h_lo = sem("h_lo")
        pool_full = sem("pool_full")
        pool_hi = sem("pool_hi")
        pool_lo = sem("pool_lo")
        v2_taken = sem("v2_taken")
        r_copy = sem("r_copy")
        r_ss = sem("r_ss")
        r_root = sem("r_root")
        r_swap = sem("r_swap")
        r_done = sem("r_done")
        out_turned = sem("out_turned")
        out_copied = sem("out_copied")
        out_dma = sem("out_dma")
        dve_own = sem("dve_own")
        act_own = sem("act_own")

        block = ctx.enter_context(nc.Block())

        def v8(buf, p):
            return buf[:, p, :].rearrange("p (k c) -> p k c", k=8)

        def pair_view(buf, p):
            return buf[:, p:p + 2, :].rearrange("p a b -> p (a b)").rearrange("p (k g d) -> p k g d", g=2, d=HD)

        QSLOTS = {0: (0, 0), 1: (0, 1), 3: (0, 0), 4: (0, 1)}

        def split_views(buf, n):
            if n in QSLOTS:
                return pair_view(buf, QSLOTS[n][0])[:, :, QSLOTS[n][1], :]
            return buf[:, RING[n], :]

        def raw_view(n):
            return raw[:, RING[n], :].rearrange("p (k d) -> p k d", d=HD) if n in QSLOTS else raw[:, RING[n], :]

        def v4(buf, p):
            return buf[:, p, :].rearrange("p (k c) -> p k c", k=4)

        def v2k(buf, p):
            return buf[:, p, :].rearrange("p (k c) -> p k c", k=2)

        def vrow(name):
            return slice(VEC[name], VEC[name] + 8)

        def const_loads():
            yield cst[:], cst_dram
            for name, key in (("mix_pre", "norm_mix_pre"), ("mix_post", "norm_mix_post"), ("mlp_pre", "norm_mlp_pre"),
                              ("mlp_post", "norm_mlp_post"), ("pool_scale", "pool_scale_2"), ("c", "c_2")):
                yield vrows[vrow(name), 0, :], A[key][0].rearrange("(r c) -> r c", c=P)
            yield vrows[32:80, 0, :], A["norm_g_2"].rearrange("l s (r c) -> (l s r) c", c=P)
            yield vrows[vrow("kv_norm"), 0, :], A["kv_norm_2"].rearrange("(r c) -> r c", c=P)
            yield vrows[104:105, 0, :], A["k_norm_2"].rearrange("(r c) -> r c", c=P)
            yield vrows[105:106, 0, :], A["q_norm_2"]
            ada_rows = A["ada_b_2"].rearrange("l (r c) -> (l r) c", c=P)
            yield vrows[0:80, 1, :], ada_rows[0:80]
            yield vrows[0:64, 2, :], ada_rows[80:144]
            yield vrows[64:80, 2, :], A["kv_ada_b_2"].rearrange("(r c) -> r c", c=P)
            yield vrows[0:16, 3, :], A["cmp_pos_k"][0].rearrange("(r i) d -> r (i d)", i=2)
            yield vrows[16:32, 3, :], A["cmp_pos_v"][0].rearrange("(r i) d -> r (i d)", i=2)
            yield relb, A["rel_bias"]
            yield onehot, onehot_dram
            yield dmask, dmask_dram
            yield wg[:], A["w_in"][0].rearrange("(k p) c -> p k c", p=P)[:, :, 1280:1304]
            yield w2[:, 0], A["cmp_w2_k"][0].rearrange("(m p) d -> p m d", p=P)
            yield w2[:, 1], A["cmp_w2_v"][0].rearrange("(m p) d -> p m d", p=P)
            yield sinks[:], A["attn_sinks"].partition_broadcast(P).rearrange("p a h -> p (a h)")

        N_CONSTS = len(list(const_loads()))

        ffn_phase = [("ffn0", 0, 0), ("ffn1", 0, 1), ("ffn2", 1, 0), ("ffn3", 1, 1)]
        units = [(b, t + 4 * g) for t in range(4) for g in range(2) for b in (0, 1)]
        units += [(2, t + 4 * g) for t in range(4) for g in range(2)]
        NU = len(units)
        H_BASE = {"mlp": 0, "ffn0": MLP_N, "ffn1": MLP_N + FFN_N, "ffn2": MLP_N + 2 * FFN_N, "ffn3": MLP_N + 3 * FFN_N}
        SESSION = {"in": 0, "mlp": 1, "ffn0": 2, "ffn1": 3, "ffn2": 4, "ffn3": None}

        def o_local(i):
            return 2 * i + 2 if not isinstance(i, int) or i < MLP_N - 1 else 2 * MLP_N - 1

        def i_local(i):
            return 2 * i - 1 if not isinstance(i, int) or i > 0 else 0

        @block.sync
        def _(sp):
            def load(n, pos, free, dst_view, src):
                if free is not None:
                    sp.wait_ge(lo_done, free)
                sp.dma_start(dst_view, src).then_inc(loaded[pos], 16)

            def slot(n, view, src):
                load(n, RING[n], before(n) or None, view(raw, RING[n]), src)

            def ada_src(pair, k):
                rows = bass.ds(k * P, P) if not isinstance(k, int) else slice(k * P, k * P + P)
                if pair == 4:
                    return A["ada_w_2"][:, rows, 8 * D:9 * D].rearrange("l p c -> p l c")
                if pair == 5:
                    return A["kv_ada_w_2"][rows, :].rearrange("p (a c) -> p a c", a=2)
                layer, at = (0, pair) if pair < 4 else (1, pair - 6)
                return A["ada_w_2"][layer, rows, 2 * at * D:2 * (at + 1) * D].rearrange("p (a c) -> p a c", a=2)

            def ada_load(s, a, k, k0):
                w = len(ADA_SESSIONS[s])
                m = ADA_START[s] + k0 * w + a
                free = ada_before(m)
                step = 0 if isinstance(k, int) else w
                if free:
                    sp.wait_ge(ada_used, free + step * (k - k0))
                sp.dma_start(ada[:, ADA_BUF[m], :].rearrange("p (a c) -> p a c", a=2),
                             ada_src(ADA_SESSIONS[s][a], k)).then_inc(ada_loaded[ADA_BUF[m]], 16)

            w_in = A["w_in"][0].rearrange("(k p) c -> p k c", p=P)
            q1, q2_ = 1304, 2072
            starts = [0, 256, 512, q1, q1 + 256, 768, 1024, q1 + 512] + [q2_ + 256 * j for j in range(8)]
            for n in range(16):
                slot(n, v8, w_in[:, :, starts[n]:starts[n] + 256])
                ada_load(0, n % 2, n // 2, n // 2)
            for n, name in enumerate(["cmp_w1_k", "cmp_w1_k", "cmp_w1_v", "cmp_w1_v"]):
                src = A[name][0].rearrange("(s k p) c -> s p k c", p=P, k=8)[n % 2]
                slot(START["cmp"] + n, v8, src)
            for n in range(4):
                w = A["w_up_nsa" if n < 2 else "w_up_swa"][0].rearrange("(g t d) c -> g d t c", g=2, d=HD)
                s = START["up"] + n
                c0 = 512 * (n % 2)
                sp.wait_ge(lo_done, before(s))
                sp.dma_start(v4(raw, RING[s])[0:HD], w[0][:, :, c0:c0 + 512]).then_inc(loaded[RING[s]], 16)
                sp.dma_start(v4(raw, RING[s])[HD:P], w[1][:, :, c0:c0 + 512]).then_inc(loaded[RING[s]], 16)
            w_out = A["w_out"][0].rearrange("(k p) c -> p k c", p=P)
            for n in range(4):
                slot(START["out"] + n, v8, w_out[:, :, 256 * n:256 * n + 256])

            mi = A["w_mlp_in"][0]
            mo = A["w_mlp_out"][0]
            b = START["mlp"]

            def mlp_load_in(i, i0):
                n = b + i_local(i0)
                c = bass.ds(i * 256, 256) if not isinstance(i, int) else slice(i * 256, i * 256 + 256)
                load(n, RING[n], before(n) + 2 * (i - i0), v8(raw, RING[n]), mi[:, c].rearrange("(k p) c -> p k c", p=P))

            def mlp_load_out(i, i0):
                n = b + o_local(i0)
                r = bass.ds(i * 256, 256) if not isinstance(i, int) else slice(i * 256, i * 256 + 256)
                load(n, RING[n], before(n) + 2 * (i - i0), v2k(raw, RING[n]), mo[r, :].rearrange("(k p) c -> p k c", p=P))

            def mlp_pair(j, j0, last=False):
                i, i0 = 2 * j, 2 * j0
                mlp_load_out(i, i0)
                ada_load(1, 0, j, j0)
                if not last:
                    mlp_load_in(i + 2, i0 + 2)
                ada_load(1, 1, j, j0)
                mlp_load_out(i + 1, i0 + 1)
                ada_load(1, 2, j, j0)
                if not last:
                    mlp_load_in(i + 3, i0 + 3)

            mlp_load_in(0, 0)
            mlp_load_in(1, 1)
            mlp_pair(0, 0)
            mlp_pair(1, 1)
            with sp.Fori(2, MLP_N // 2 - 1) as j:
                mlp_pair(j, 2)
            mlp_pair(MLP_N // 2 - 1, MLP_N // 2 - 1, last=True)

            def ffn(name, layer, sub):
                b = START[name]
                wi, wo = A["ffn_w_in_2"][layer, sub], A["ffn_w_out_2"][layer, sub]
                s = SESSION[name]

                def body(i, i0, with_ada):
                    n = b + 3 * i0 - 1
                    for q in range(2):
                        if not isinstance(i, int):
                            c = bass.ds(i * 256 + q * FF2, 256)
                        else:
                            c = slice(i * 256 + q * FF2, i * 256 + q * FF2 + 256)
                        load(n + q, q, before(n + q) + 3 * (i - i0), v8(raw, q), wi[:, c].rearrange("(k p) c -> p k c", p=P))
                        if q == 0 and with_ada:
                            ada_load(s, 0, i - 1, i0 - 1)
                    r = bass.ds((i - 1) * 256, 256) if not isinstance(i, int) else slice((i - 1) * 256, i * 256)
                    load(n + 2, 2, before(n + 2) + 3 * (i - i0), v2k(raw, 2), wo[r, :].rearrange("(k p) c -> p k c", p=P))
                    if with_ada and len(ADA_SESSIONS[s]) > 1:
                        ada_load(s, 1, i - 1, i0 - 1)

                for q in range(2):
                    slot(b + q, v8, wi[:, q * FF2:q * FF2 + 256].rearrange("(k p) c -> p k c", p=P))
                body(1, 1, s is not None)
                body(2, 2, s is not None)
                with sp.Fori(3, KT + 1) as i:
                    body(i, 3, s is not None)
                with sp.Fori(KT + 1, FFN_N) as i:
                    body(i, KT + 1, False)
                slot(b + 3 * FFN_N - 1, v2k, wo[FF2 - 256:FF2, :].rearrange("(k p) c -> p k c", p=P))

            ffn(*ffn_phase[0])
            slot(START["pool"], v8, A["pool_w_2"][0].rearrange("g (k p) c -> p (g k) c", p=P))
            ffn(*ffn_phase[1])
            w_kv = A["w_kv_2"].rearrange("(k p) c -> p k c", p=P)
            for n in range(8):
                slot(START["kv"] + n, v8, w_kv[:, :, 256 * n:256 * n + 256])
            ffn(*ffn_phase[2])
            for name, key in (("wq", "w_q_2"), ("wo", "w_o_2")):
                w = A[key][0].rearrange("(k p) c -> p k c", p=P)
                for n in range(4):
                    slot(START[name] + n, v8, w[:, :, 256 * n:256 * n + 256])
            ffn(*ffn_phase[3])
            for t in range(2):
                sp.wait_ge(out_copied, 2 * (t + 1))
                sp.dma_start(out[0, t * P:(t + 1) * P, :], xin[:, t, :]).then_inc(out_dma, 16)
            sp.wait_ge(out_dma, 32)

        @block.gpsimd
        def _(pool):
            pool.wait_ge(bvec_done, 1)
            pool.dma_start(bias_dram.rearrange("q h c -> h q c"),
                           bvec.unsqueeze(1).to_broadcast([16, P, 384])).then_inc(bvec_out, 16)
            pool.wait_ge(in_taken, 3)
            for g in range(2):
                src = kvr[g * HD:(g + 1) * HD]
                pool.dma_start(kvx[0:HD, :, g, :], src).then_inc(kvx_in, 16)
                pool.dma_start(kvx[HD:P, :, g, 0:T - 1], src[:, :, 1:T]).then_inc(kvx_in, 16)
            pool.wait_ge(bvec_out, 16)
            pool.wait_ge(ada_sum, 1)
            second = bass.AP(bias_dram.tensor, 127, [[16 * 384 - 1, P], [384, 16], [1, T]])
            first = bass.AP(bias_dram.tensor, 127 + P, [[16 * 384 - 1, P], [384, 16], [1, P]])
            pool.dma_start(bias[:, :, 0:P], first).then_inc(bias_in, 16)
            pool.dma_start(bias[:, :, P:384], second).then_inc(bias_in, 16)

        @block.tensor
        def _(pe):
            def mm3(o, wh, wl, xh, xl, start, stop, skip=False):
                nc.tensor.matmul(o, wh, xh, start=start, stop=False, skip_group_check=skip)
                nc.tensor.matmul(o, wh, xl, start=False, stop=False, skip_group_check=skip)
                return nc.tensor.matmul(o, wl, xh, start=False, stop=stop, skip_group_check=skip)

            def dense8(n, pos, o, pre=None, lo_at=None):
                pe.wait_ge(lo_done, lo_at if lo_at is not None else n + 1)
                wh, wl = v8(whi, pos), v8(wlo, pos)
                for m in range(2):
                    for k in range(KT):
                        if pre is not None and m == 0:
                            pe.wait_ge(u_lo, pre + k + 1)
                        ins = mm3(o[:, m * T:(m + 1) * T], wh[:, k, m * P:(m + 1) * P], wl[:, k, m * P:(m + 1) * P],
                                  uhi[:, k, :], ulo[:, k, :], k == 0, k == KT - 1)
                ins.then_inc(pe_done, 1)

            def norm_sum(e):
                for k in range(KT):
                    if k % 2 == 0:
                        pe.wait_ge(sq_ready, 4 * e + k // 2 + 1)
                    ins = nc.tensor.matmul(bank[6][:, 0:T], ones, full[:, k, :], start=k == 0, stop=k == KT - 1)
                ins.then_inc(ss_done, 1)

            def ada_reduce(s):
                w = len(ADA_SESSIONS[s])
                pe.wait_ge(ada_used, ADA_START[s] + KT * w)
                for a in range(w):
                    for j in range(16):
                        ins = nc.tensor.matmul(bank[7][:, 16 * a + j:16 * a + j + 1], acc[:, a, j * P:(j + 1) * P],
                                               ones[:, 0:1], start=True, stop=True)
                ins.then_inc(ada_sum, 1)

            pe.wait_ge(consts_in, 16 * N_CONSTS)
            nc.tensor.transpose(bank[6][:, 0:NVEC], vrows[0:NVEC, 0, :], ident[0:NVEC, 0:NVEC])
            nc.tensor.transpose(bank[6][:, 128:208], vrows[0:80, 1, :], ident[0:80, 0:80])
            nc.tensor.transpose(bank[6][:, 208:288], vrows[0:80, 2, :], ident[0:80, 0:80])
            nc.tensor.transpose(bank[6][:, 288:320], vrows[0:32, 3, :], ident[0:32, 0:32]).then_inc(vec_t, 1)
            nc.tensor.matmul(bank[7][0:16, 0:384], relb, onehot, start=True, stop=True).then_inc(bvec_mm, 1)
            pe.wait_ge(x_in, 16)
            for k in range(KT):
                for t in range(2):
                    ins = nc.tensor.transpose(bank[k // 2][:, (k % 2) * T + t * P:(k % 2) * T + (t + 1) * P],
                                              xin[:, t, k * P:(k + 1) * P], ident)
            ins.then_inc(x_turned, 1)
            norm_sum(0)

            pool6 = [0, 1, 2, 3, 4, 5]

            def q_pair(n):
                pe.wait_ge(lo_done, n + 2)
                p = RING[n]
                for t in range(4):
                    o = bank[pool6[(n + t // 2) % 6]][:, (t % 2) * T:(t % 2 + 1) * T]
                    for k in range(KT):
                        if n == 0 and t == 0:
                            pe.wait_ge(u_lo, k + 1)
                        wh, wl = pair_view(whi, p)[:, 4 * k + t, :, :], pair_view(wlo, p)[:, 4 * k + t, :, :]
                        wh, wl = wh.rearrange("p g d -> p (g d)"), wl.rearrange("p g d -> p (g d)")
                        ins = mm3(o, wh, wl, uhi[:, k, :], ulo[:, k, :], k == 0, k == KT - 1)
                ins.then_inc(pe_done, 2)

            def k_and_v(n):
                pe.wait_ge(lo_done, n + 1)
                wh, wl = v8(whi, RING[n]), v8(wlo, RING[n])
                o = bank[pool6[n % 6]]
                for k in range(KT):
                    mm3(o[:, 0:T], wh[:, k, 0:P], wl[:, k, 0:P], uhi[:, k, :], ulo[:, k, :], k == 0, k == KT - 1)
                for t in range(2):
                    for k in range(KT):
                        ins = mm3(o[:, T + t * P:T + (t + 1) * P], uhi[:, k, t * P:(t + 1) * P],
                                  ulo[:, k, t * P:(t + 1) * P], wh[:, k, P:2 * P], wl[:, k, P:2 * P], k == 0, k == KT - 1)
                ins.then_inc(pe_done, 1)

            n = 0
            while n < 16:
                if n >= 5:
                    pe.wait_ge(in_taken, n - 4)
                if n in (0, 3):
                    q_pair(n)
                    n += 2
                    continue
                if n in (5, 6, 7):
                    k_and_v(n)
                else:
                    dense8(n, RING[n], bank[pool6[n % 6]])
                n += 1
            for t in range(2):
                for k in range(KT):
                    ins = nc.tensor.matmul(bank[6][:, 256 + 24 * t:280 + 24 * t], full[:, k, t * P:(t + 1) * P], wg[:, k, :],
                                           start=k == 0, stop=k == KT - 1)
            ins.then_inc(gate_mm, 1)
            pe.wait_ge(bvec_done, 1)
            ada_reduce(0)

            pe.wait_ge(in_taken, 16)
            for a in range(2):
                pe.wait_ge(blk_lo, a + 1)
                if a == 1:
                    pe.wait_ge(mods_done, 1)
                    pe.wait_ge(gate_done, 1)
                for s in range(2):
                    n = START["cmp"] + 2 * a + s
                    pe.wait_ge(lo_done, n + 1)
                    for m in range(2):
                        for kk in range(8):
                            ii = 8 * s + kk
                            ins = mm3(bank[4 + 2 * a + m][:, 0:30], v8(whi, RING[n])[:, kk, m * P:(m + 1) * P],
                                      v8(wlo, RING[n])[:, kk, m * P:(m + 1) * P], bparts[a][0][:, ii * 30:ii * 30 + 30],
                                      bparts[a][1][:, ii * 30:ii * 30 + 30], ii == 0, ii == 15)
                    ins.then_inc(pe_done, 1)
            pe.wait_ge(gelu_done, 1)
            for g in range(2):
                for m in range(2):
                    nc.tensor.matmul(bank[4][g * HD:(g + 1) * HD, 32:32 + NCMP], w2[:, 0, m, :],
                                     h1[:, 0, m, g * NCMP:(g + 1) * NCMP], start=m == 0, stop=m == 1)
            pe.wait_ge(gelu_done, 2)
            for g in range(2):
                for m in range(2):
                    ins = nc.tensor.matmul(bank[6][0:NCMP, 64 + g * HD:64 + (g + 1) * HD],
                                           h1[:, 1, m, g * NCMP:(g + 1) * NCMP], w2[:, 1, m, :], start=m == 0, stop=m == 1)
            ins.then_inc(ckv_mm, 1)

            pe.wait_ge(ckv_done, 1)
            for h in range(NH):
                g, t = h // 4, h % 4
                for qt in range(2):
                    c = qt * 64 + t * 16
                    ins = nc.tensor.matmul(bank[4 + g][:, c:c + NCMP],
                                           qn[g * HD:(g + 1) * HD, t, qt * P:(qt + 1) * P], kcT[g * HD:(g + 1) * HD, 0:NCMP],
                                           start=True, stop=True)
            ins.then_inc(cs_mm, 1)
            pe.wait_ge(cs_prob, 1)
            for h in range(NH):
                for qt in range(2):
                    b = [2, 3, 6, 7][h // 2]
                    c = (h % 2) * T + qt * P
                    ins = nc.tensor.transpose(bank[b][0:NCMP, c:c + P], cmpE[:, qt, h, 0:NCMP], ident)
            ins.then_inc(cs_turned, 1)

            def attention(count, base, q_of, k_of, v_of, o_of, before_pv, start_of, stop_of):
                for u in range(count + 3):
                    if u < count:
                        w = base + u
                        if w >= 2:
                            pe.wait_ge(s_max, w - 1)
                        sc = bank[4 + w % 2]
                        q, k = q_of(u), k_of(u)
                        nc.tensor.matmul(sc[:, 0:P], q[:, 0:P], k[:, 0:P], start=True, stop=True)
                        nc.tensor.matmul(sc[:, P:384], q[:, P:T], k, start=True, stop=True).then_inc(s_mm, 1)
                    v = u - 2
                    if 0 <= v < count:
                        w = base + v
                        pe.wait_ge(s_prob, w + 1)
                        if w >= 2:
                            pe.wait_ge(s_copied, w - 1)
                        for b in range(3):
                            ins = nc.tensor.transpose(bank[6 + w % 2][:, b * P:(b + 1) * P],
                                                      prob[w % 3][:, b * P:(b + 1) * P], ident)
                        ins.then_inc(s_turned, 1)
                    v = u - 3
                    if 0 <= v < count:
                        w = base + v
                        pe.wait_ge(s_copied, w + 1)
                        before_pv(v)
                        pT = probT[w % 2]
                        nc.tensor.matmul(o_of(v), v_of(v, 0), pT[:, 0:T], start=start_of(v), stop=False)
                        nc.tensor.matmul(o_of(v)[:, P:T], v_of(v, 1), pT[:, T:384], start=False,
                                         stop=stop_of(v)).then_inc(s_pv, 1)

            def half(h):
                return slice((h // 4) * HD, (h // 4 + 1) * HD)

            def o1(u):
                b, h = units[u]
                t = h % 4
                return bank[(2 if b == 2 else 0) + t // 2][half(h), (t % 2) * T:(t % 2 + 1) * T]

            def compressed_first(u):
                b, h = units[u]
                if b == 0:
                    if u == 0:
                        pe.wait_ge(cs_done, 4)
                    nc.tensor.matmul(o1(u), vcs[0:NCMP, h // 4, :], pcT[:, h, :], start=True, stop=False)

            pe.wait_ge(cs_dve, 1)
            pe.wait_ge(cs_done, 4)
            attention(NU, 0,
                      lambda u: (qs if units[u][0] == 2 else qn)[half(units[u][1]), units[u][1] % 4, :],
                      lambda u: kT[half(units[u][1]), units[u][0], :],
                      lambda u, kt: vv[:, units[u][0], kt, half(units[u][1])],
                      o1, compressed_first, lambda u: units[u][0] == 2, lambda u: units[u][0] >= 1)

            upbanks = [4, 6, 0, 2]
            for q in range(4):
                n = START["up"] + q
                pe.wait_ge(lo_done, n + 1)
                pe.wait_ge(o_lo, 4)
                for m in range(4):
                    for k in range(4):
                        o = bank[upbanks[q] + m // 2][:, (m % 2) * T:(m % 2 + 1) * T]
                        kk = k + 4 * (q // 2)
                        ins = mm3(o, v4(whi, RING[n])[:, k, m * P:(m + 1) * P], v4(wlo, RING[n])[:, k, m * P:(m + 1) * P],
                                  uhi[:, kk, :], ulo[:, kk, :], k == 0, k == 3)
                ins.then_inc(pe_done, 1)
            for q in range(4):
                n = START["out"] + q
                if q == 0:
                    pe.wait_ge(y_lo, 2)
                dense8(n, RING[n], bank[q])
            norm_sum(1)
            norm_sum(2)

            b = START["mlp"]

            def out_chunk(pos, first, last):
                wh, wl = v2k(whi, pos), v2k(wlo, pos)
                for m in range(KT):
                    for k in range(2):
                        ins = mm3(bank[m // 2][:, (m % 2) * T:(m % 2 + 1) * T], wh[:, k, m * P:(m + 1) * P],
                                  wl[:, k, m * P:(m + 1) * P], hhi[:, k * T:(k + 1) * T], hlo[:, k * T:(k + 1) * T],
                                  first and k == 0 and m % 2 == 0, last and k == 1, skip=True)
                ins.then_inc(pe_done, 1)

            def mlp_in_mm(i, i0):
                loc = b + i_local(i0)
                if not (isinstance(i, int) and i < 2):
                    pe.wait_ge(h_full, i - 1)
                dense8(None, RING[loc], bank[4 + i0 % 2], pre=8 if isinstance(i, int) and i == 0 else None,
                       lo_at=loc + 1 + 2 * (i - i0))

            def mlp_out_mm(i, i0, first=False, last=False):
                loc = b + o_local(i0)
                pe.wait_ge(lo_done, loc + 1 + 2 * (i - i0))
                pe.wait_ge(h_lo, i + 1)
                out_chunk(RING[loc], first, last)

            mlp_in_mm(0, 0)
            mlp_in_mm(1, 1)
            mlp_out_mm(0, 0, first=True)
            mlp_in_mm(2, 2)
            mlp_out_mm(1, 1)
            with pe.Fori(1, MLP_N // 2 - 1) as j:
                mlp_in_mm(2 * j + 1, 3)
                mlp_out_mm(2 * j, 2)
                mlp_in_mm(2 * j + 2, 4)
                mlp_out_mm(2 * j + 1, 3)
            mlp_in_mm(MLP_N - 1, MLP_N - 1)
            mlp_out_mm(MLP_N - 2, MLP_N - 2)
            mlp_out_mm(MLP_N - 1, MLP_N - 1, last=True)
            ada_reduce(1)
            norm_sum(3)
            norm_sum(4)

            def ffn(name, pre):
                b = START[name]
                hb = H_BASE[name]

                def gate_up(i, i0):
                    for q in range(2):
                        loc = b + (q if i0 == 0 else 3 * i0 - 1 + q)
                        if q == 0 and not (isinstance(i, int) and i == 0):
                            pe.wait_ge(h_full, hb + i)
                        dense8(None, q, bank[4 + q], pre=pre if i0 == 0 and q == 0 else None,
                               lo_at=loc + 1 + 3 * (i - i0))

                def down(i, i0, first=False, last=False):
                    loc = b + (3 * i0 + 4 if i0 < FFN_N - 1 else 3 * FFN_N - 1)
                    pe.wait_ge(lo_done, loc + 1 + 3 * (i - i0))
                    pe.wait_ge(h_lo, hb + i + 1)
                    out_chunk(2, first, last)

                gate_up(0, 0)
                gate_up(1, 1)
                down(0, 0, first=True)
                with pe.Fori(2, FFN_N) as i:
                    gate_up(i, 2)
                    down(i - 1, 1)
                down(FFN_N - 1, FFN_N - 1, last=True)

            ffn("ffn0", 16)
            ada_reduce(2)
            norm_sum(5)

            n = START["pool"]
            pe.wait_ge(lo_done, n + 1)
            for g in range(4):
                pe.wait_ge(pool_lo, g + 1)
                for m in range(2):
                    for k in range(2):
                        ins = mm3(bank[g][:, m * T:(m + 1) * T], v8(whi, RING[n])[:, 2 * g + k, m * P:(m + 1) * P],
                                  v8(wlo, RING[n])[:, 2 * g + k, m * P:(m + 1) * P], uhi[:, 2 * g + k, :],
                                  ulo[:, 2 * g + k, :], k == 0, k == 1)
            ins.then_inc(pe_done, 1)
            norm_sum(6)
            ffn("ffn1", 24)
            ada_reduce(3)
            norm_sum(7)

            def rotary(r):
                for b in range(4):
                    pe.wait_ge(r_copy, 8 * r + 2 * b + 2)
                    nc.tensor.matmul(bank[b][:, :], ones, full[:, 2 * b:2 * b + 2, :], start=True,
                                     stop=True).then_inc(r_ss, 1)
                for b in range(4):
                    pe.wait_ge(r_root, 4 * r + b + 1)
                    src = q2 if r else tmp2
                    nc.tensor.matmul(bank[b][:, :], const("swap"), src[:, 2 * b:2 * b + 2, :], start=True,
                                     stop=True).then_inc(r_swap, 1)

            b = START["kv"]
            for n in range(4):
                dense8(b + n, RING[b + n], bank[n], pre=32 if n == 0 else None)
            for n in range(4, 8):
                pe.wait_ge(lo_done, b + n + 1)
                if n >= 6:
                    pe.wait_ge(v2_taken, n - 5)
                wh, wl = v8(whi, RING[b + n]), v8(wlo, RING[b + n])
                for t in range(2):
                    for k in range(KT):
                        ins = mm3(bank[4 + n % 2][:, t * T:(t + 1) * T], uhi[:, k, t * P:(t + 1) * P],
                                  ulo[:, k, t * P:(t + 1) * P], wh[:, k, :], wl[:, k, :], k == 0, k == KT - 1)
                ins.then_inc(pe_done, 1)
            rotary(0)
            pe.wait_ge(v2_taken, 4)
            pe.wait_ge(r_done, 1)
            ffn("ffn2", 40)
            ada_reduce(4)
            norm_sum(8)

            b = START["wq"]
            for n in range(4):
                dense8(b + n, RING[b + n], bank[n], pre=48 if n == 0 else None)
            rotary(1)
            pe.wait_ge(r_done, 2)
            attention(8, NU, lambda u: q2[:, u, :], lambda u: k2[:, u, :],
                      lambda u, kt: v2[:, kt, u * P:(u + 1) * P],
                      lambda u: bank[u // 2][:, (u % 2) * T:(u % 2 + 1) * T],
                      lambda u: None, lambda u: True, lambda u: True)
            b = START["wo"]
            pe.wait_ge(o_lo, 8)
            for n in range(4):
                dense8(b + n, RING[b + n], bank[n])
            norm_sum(9)
            ffn("ffn3", 56)

            pe.wait_ge(x_ready, 36)
            for t in range(2):
                for k in range(KT):
                    ins = nc.tensor.transpose(bank[4 + 2 * t + k // 4][:, (k % 4) * P:(k % 4 + 1) * P],
                                              xT[:, k, t * P:(t + 1) * P], ident)
                    if k % 4 == 3:
                        ins.then_inc(out_turned, 1)

        @block.scalar
        def _(act):
            own = [0]

            def link(ins):
                own[0] += 1
                ins.then_inc(act_own, 1)
                act.wait_ge(act_own, own[0])

            def conv_at(pos, full_at, free_at):
                act.wait_ge(loaded[pos], full_at)
                if free_at is not None:
                    act.wait_ge(pe_done, free_at)
                nc.scalar.activation(whi[:, pos, :], raw[:, pos, :], ACT.Copy).then_inc(hi_done, 1)

            def conv(n):
                if n in QSLOTS:
                    act.wait_ge(loaded[RING[n]], filled(n))
                    if n > 2:
                        act.wait_ge(pe_done, 2)
                    nc.scalar.activation(split_views(whi, n), raw_view(n), ACT.Copy).then_inc(hi_done, 1)
                    return
                conv_at(RING[n], filled(n), before(n) or None)

            def square_x(e, version):
                for q in range(4):
                    act.wait_ge(x_ready, 4 * version - 3 + q)
                    nc.scalar.activation(full[:, 2 * q:2 * q + 2, :], xT[:, 2 * q:2 * q + 2, :],
                                         ACT.Square).then_inc(sq_ready, 1)

            def square_f(done):
                act.wait_ge(pe_done, done)
                for q in range(4):
                    nc.scalar.activation(full[:, 2 * q:2 * q + 2, :], bank[q][:], ACT.Square).then_inc(sq_ready, 1)

            def take_root(e):
                act.wait_ge(ss_done, e + 1)
                nc.scalar.activation(root[:], bank[6][:, 0:T], ACT.Sqrt, bias=eps[:], scale=1.0 / D).then_inc(root_done, 1)

            def split_u(p, free, shift=None):
                if free:
                    act.wait_ge(pe_done, free)
                for k in range(KT):
                    act.wait_ge(u_full, 8 * p + k + 1)
                    if shift is None:
                        nc.scalar.activation(uhi[:, k, :], full[:, k, :], ACT.Copy).then_inc(u_hi, 1)
                    else:
                        nc.scalar.activation(uhi[:, k, :], full[:, k, :], ACT.Identity,
                                             bias=shift[:, k:k + 1]).then_inc(u_hi, 1)

            def cload(dst, src):
                act.dma_start(dst, src).then_inc(consts_in, 16)

            act.dma_start(xin, A["x"][0].rearrange("(t p) d -> p t d", p=P)).then_inc(x_in, 16)
            for args in const_loads():
                cload(*args)
            conv(0)
            act.wait_ge(vec_done, 1)
            nc.scalar.activation(csilu[:], vec[:, VEC["c"]:VEC["c"] + 8], ACT.Silu).then_inc(c_ready, 1)
            square_x(0, 1)
            conv(1)
            take_root(0)
            split_u(0, 0)
            conv(2)

            for n in range(16):
                act.wait_ge(pe_done, {0: 2, 3: 5}.get(n, n + 1))
                o = bank[n % 6]
                if n in (0, 1):
                    ins = nc.scalar.activation(qn[:, 2 * n:2 * n + 2, :], o[:], ACT.Copy, scale=HD ** -0.5)
                elif n in (3, 4):
                    ins = nc.scalar.activation(qs[:, 2 * n - 6:2 * n - 4, :], o[:], ACT.Copy, scale=HD ** -0.5)
                elif n == 2:
                    ins = nc.scalar.activation(kvr, o[:], ACT.Copy)
                elif n in (5, 6, 7):
                    nc.scalar.activation(kT[:, n - 5, :], o[:, 0:T], ACT.Copy)
                    ins = nc.scalar.activation(vv[:, n - 5, :, :], o[:, T:2 * T], ACT.Copy)
                else:
                    ins = nc.scalar.activation(gates[:, 2 * n - 16:2 * n - 14, :], o[:], ACT.Sigmoid)
                ins.then_inc(in_taken, 1)
                conv(n + 3)
            act.wait_ge(gate_mm, 1)
            nc.scalar.activation(gate3[:], bank[6][:, 256:304], ACT.Sigmoid).then_inc(gate_done, 1)
            act.wait_ge(pe_done, 16)
            for a in range(2):
                act.wait_ge(blk_full, a + 1)
                nc.scalar.activation(bparts[a][0], blk[:, a, :], ACT.Copy).then_inc(blk_hi, 1)
            conv(START["cmp"] + 3)
            for a in range(2):
                act.wait_ge(pe_done, START["cmp"] + 2 * a + 2)
                for m in range(2):
                    ins = nc.scalar.activation(h1[:, a, m, 0:30], bank[4 + 2 * a + m][:, 0:30], ACT.Gelu_apprx_tanh)
                ins.then_inc(gelu_done, 1)
            act.wait_ge(ckv_mm, 1)
            nc.scalar.activation(kcT[:, 0:NCMP], bank[4][:, 32:32 + NCMP], ACT.Copy)
            nc.scalar.activation(vcs[0:NCMP, :, :], bank[6][0:NCMP, 64:64 + 2 * HD], ACT.Copy).then_inc(ckv_done, 1)
            for n in range(3):
                conv(START["up"] + n)
            act.wait_ge(cs_dve, 2)
            nc.scalar.activation(cmpE[:, :, :, 0:NCMP], cmpE[:, :, :, 0:NCMP], ACT.Exp).then_inc(cs_exp, 1)
            act.wait_ge(cs_turned, 1)
            for q in range(4):
                nc.scalar.activation(pcT[:, 2 * q:2 * q + 2, :], bank[[2, 3, 6, 7][q]][0:NCMP, :],
                                     ACT.Copy).then_inc(cs_done, 1)

            def attention(count, base, sink_of):
                for u in range(count + 2):
                    if u < count:
                        w = base + u
                        act.wait_ge(s_max, w + 1)
                        sm = small[:, w % 3, :]
                        pr = prob[w % 3]
                        if sink_of(u) is not None:
                            for t in range(2):
                                nc.scalar.activation(sm[:, 4 + t:5 + t], sink_of(u), ACT.Exp, bias=sm[:, t:t + 1])
                        nc.scalar.activation(pr[:, 0:P], pr[:, 0:P], ACT.Exp, bias=sm[:, 0:1], accum_out=sm[:, 2:3])
                        nc.scalar.activation(pr[:, P:384], pr[:, P:384], ACT.Exp, bias=sm[:, 1:2],
                                             accum_out=sm[:, 3:4]).then_inc(s_exp, 1)
                    v = u - 2
                    if 0 <= v < count:
                        w = base + v
                        act.wait_ge(s_turned, w + 1)
                        if w >= 2:
                            act.wait_ge(s_pv, w - 1)
                        nc.scalar.activation(probT[w % 2], bank[6 + w % 2][:, 0:384], ACT.Copy).then_inc(s_copied, 1)

            attention(NU, 0, lambda u: sinks[:, units[u][1]:units[u][1] + 1] if units[u][0] == 2 else None)
            act.wait_ge(s_pv, NU)
            for q in range(4):
                nc.scalar.activation(uhi[:, 2 * q:2 * q + 2, :], bank[q][:], ACT.Copy).then_inc(o_hi, 1)

            for q in range(4):
                conv(START["up"] + 3 + q)
            act.wait_ge(pe_done, START["up"] + 4)
            for q in range(2):
                act.wait_ge(y_full, q + 1)
                nc.scalar.activation(uhi[:, 4 * q:4 * q + 4, :], full[:, 4 * q:4 * q + 4, :], ACT.Copy).then_inc(y_hi, 1)
            conv(START["out"] + 3)
            square_f(START["out"] + 4)
            conv(START["mlp"])
            take_root(1)
            square_x(2, 2)
            conv(START["mlp"] + 1)
            take_root(2)
            split_u(1, START["out"] + 4)

            b = START["mlp"]

            def split_h(i, o_done):
                act.wait_ge(h_full, i + 1)
                if o_done is not None:
                    act.wait_ge(pe_done, o_done)
                nc.scalar.activation(hhi, hfull, ACT.Copy).then_inc(h_hi, 1)

            def sub(i, i0, conv_in=True):
                act.wait_ge(pe_done, b + i_local(i0) + 1 + 2 * (i - i0))
                nc.scalar.activation(act_g, bank[4 + i0 % 2][:], ACT.Relu).then_inc(g_act, 1)
                split_h(i, b + o_local(i0 - 1) + 1 + 2 * (i - i0) if i0 > 0 else None)
                n = b + o_local(i0)
                conv_at(RING[n], filled(n) + 16 * (i - i0), before(n) + 2 * (i - i0))
                if conv_in:
                    n = b + i_local(i0 + 2)
                    conv_at(RING[n], filled(n) + 8 * (i - i0), before(n) + 2 * (i - i0))

            sub(0, 0)
            sub(1, 1)
            sub(2, 2)
            sub(3, 3)
            with act.Fori(2, MLP_N // 2 - 1) as j:
                sub(2 * j, 4)
                sub(2 * j + 1, 5)
            sub(MLP_N - 2, MLP_N - 2, conv_in=False)
            sub(MLP_N - 1, MLP_N - 1, conv_in=False)

            def post(e, done, version, nxt, gap, p, shift):
                square_f(done)
                conv(gap[0])
                take_root(e)
                square_x(e + 1, version)
                conv(gap[1])
                take_root(e + 1)
                split_u(p, done, shift)

            b0 = START["ffn0"]
            post(3, b0, 3, 4, (b0, b0 + 1), 2, mods[:, 0, :])

            def ffn(name):
                b = START[name]
                hb = H_BASE[name]

                def evac(i, i0):
                    loc = b + (1 if i0 == 0 else 3 * i0)
                    act.wait_ge(pe_done, loc + 1 + 3 * (i - i0))
                    nc.scalar.activation(act_g, bank[4][:], ACT.Silu).then_inc(g_act, 1)

                def step(i, i0):
                    n = b + 3 * i0 - 1
                    conv_at(0, filled(n) + 16 * (i - i0), before(n) + 3 * (i - i0))
                    evac(i - 1, i0 - 1)
                    conv_at(1, filled(n + 1) + 16 * (i - i0), before(n + 1) + 3 * (i - i0))
                    split_h(hb + i - 1, before(n + 2) + 3 * (i - i0))
                    conv_at(2, filled(n + 2) + 16 * (i - i0), before(n + 2) + 3 * (i - i0))

                step(1, 1)
                step(2, 2)
                with act.Fori(3, FFN_N) as i:
                    step(i, 3)
                evac(FFN_N - 1, FFN_N - 1)
                split_h(hb + FFN_N - 1, b + 3 * FFN_N - 1)
                conv(b + 3 * FFN_N - 1)

            ffn("ffn0")
            n = START["pool"]
            square_x(5, 4)
            conv(n)
            take_root(5)
            for g in range(4):
                act.wait_ge(pool_full, g + 1)
                nc.scalar.activation(uhi[:, 2 * g:2 * g + 2, :], full[:, 2 * g:2 * g + 2, :], ACT.Copy).then_inc(pool_hi, 1)
            conv(n + 1)
            square_x(6, 5)
            conv(n + 2)
            take_root(6)
            split_u(3, n + 1, mods[:, 6, :])
            ffn("ffn1")
            b = START["kv"]
            square_x(7, 6)
            conv(b)
            take_root(7)
            conv(b + 1)
            conv(b + 2)
            split_u(4, b, mods[:, 18, :])

            def rotary(r, done, scalar, dst):
                for q in range(4):
                    act.wait_ge(pe_done, done - 3 + q)
                    nc.scalar.activation(dst[:, 2 * q:2 * q + 2, :], bank[q][:], ACT.Copy, scale=scalar).then_inc(r_copy, 1)
                    nc.scalar.activation(full[:, 2 * q:2 * q + 2, :], bank[q][:], ACT.Square).then_inc(r_copy, 1)
                    conv_next(r, q)

            def conv_next(r, q):
                n = (START["kv"] if r == 0 else START["wq"]) + 3 + q
                if r == 1 and q == 3:
                    return
                conv(n)

            def rotary_root(r):
                for q in range(4):
                    act.wait_ge(r_ss, 4 * r + q + 1)
                    nc.scalar.activation(full[:, 2 * q:2 * q + 2, :], bank[q][:], ACT.Sqrt, bias=eps[:],
                                         scale=1.0 / P).then_inc(r_root, 1)

            rotary(0, b + 4, vec[:, VEC["k_norm"]:VEC["k_norm"] + 1], tmp2)
            conv(b + 7)
            for n in range(4):
                act.wait_ge(pe_done, b + 5 + n)
                nc.scalar.activation(v2[:, :, 256 * n:256 * n + 256], bank[4 + n % 2][:], ACT.Copy).then_inc(v2_taken, 1)
            rotary_root(0)
            conv(START["ffn2"])
            conv(START["ffn2"] + 1)
            act.wait_ge(r_done, 1)
            split_u(5, b + 8, mods[:, 9, :])
            ffn("ffn2")
            b = START["wq"]
            square_x(8, 7)
            conv(b)
            take_root(8)
            conv(b + 1)
            conv(b + 2)
            split_u(6, b, mods[:, 12, :])
            rotary(1, b + 4, scal[:, QSC, 0:1], q2)
            rotary_root(1)
            conv(b + 6)
            attention(8, NU, lambda u: None)
            act.wait_ge(s_pv, NU + 8)
            for q in range(4):
                nc.scalar.activation(uhi[:, 2 * q:2 * q + 2, :], bank[q][:], ACT.Copy).then_inc(o_hi, 1)
            conv(b + 7)
            b = START["ffn3"]
            square_x(9, 8)
            conv(b)
            take_root(9)
            conv(b + 1)
            split_u(7, b, mods[:, 15, :])
            ffn("ffn3")
            for t in range(2):
                for c in range(2):
                    act.wait_ge(out_turned, 2 * t + c + 1)
                    nc.scalar.activation(xin[:, t, c * 512:(c + 1) * 512], bank[4 + 2 * t + c][:],
                                         ACT.Copy).then_inc(out_copied, 1)

        @block.vector
        def _(dve):
            own = [0]

            def link(ins):
                own[0] += 1
                ins.then_inc(dve_own, 1)
                dve.wait_ge(dve_own, own[0])

            def conv_at(pos, hi_at):
                dve.wait_ge(hi_done, hi_at)
                nc.vector.tensor_tensor(wlo[:, pos, :], raw[:, pos, :], whi[:, pos, :].bitcast(F32),
                                        ALU.subtract).then_inc(lo_done, 1)

            def conv(n):
                if n in QSLOTS:
                    dve.wait_ge(hi_done, n + 1)
                    nc.vector.tensor_tensor(split_views(wlo, n), raw_view(n), split_views(whi, n).bitcast(F32),
                                            ALU.subtract).then_inc(lo_done, 1)
                    return
                conv_at(RING[n], n + 1)

            def ada_add(s, a, k, k0):
                w = len(ADA_SESSIONS[s])
                m = ADA_START[s] + k0 * w + a
                step = 0 if isinstance(k, int) else w
                buf = ADA_BUF[m]
                per = sum(1 for q in range(w) if q % 2 == buf)
                if step == 0:
                    dve.wait_ge(ada_loaded[buf], ada_filled(m))
                else:
                    dve.wait_ge(ada_loaded[buf], ada_filled(m) + 16 * per * (k - k0))
                if isinstance(k, int) and k == 0:
                    if s > 0:
                        dve.wait_ge(ada_sum, s)
                    nc.vector.tensor_scalar(acc[:, a, :], ada[:, buf, :], csilu[:, 0:1], None,
                                            ALU.mult).then_inc(ada_used, 1)
                    return
                dve.wait_ge(ada_used, ada_acc_before(m) + step * (k - k0))
                c = csilu[:, k:k + 1] if isinstance(k, int) else csilu[:, bass.ds(k, 1)]
                nc.vector.scalar_tensor_tensor(out=acc[:, a, :], in0=ada[:, buf, :], scalar=c, in1=acc[:, a, :],
                                               op0=ALU.mult, op1=ALU.add).then_inc(ada_used, 1)

            def take_mods(s):
                dve.wait_ge(ada_sum, s + 1)
                w = ADA_SESSIONS[s]
                for a, pair in enumerate(w):
                    for i, m in enumerate(PAIR_MODS[pair]):
                        c = 16 * a + 8 * i
                        ins = nc.vector.tensor_tensor(mods[:, m, :], bank[7][:, c:c + 8], adab[:, 8 * m:8 * m + 8], ALU.add)
                ins.then_inc(mods_done, 1)
                dve.wait_ge(mods_done, s + 1)

            def gain(i, m, g):
                link(nc.vector.scalar_tensor_tensor(out=scal[:, i, :], in0=mods[:, m, :], scalar=1.0, in1=g,
                                                    op0=ALU.add, op1=ALU.mult))

            def weight(i, m, w):
                link(nc.vector.tensor_scalar(scal[:, i, :], mods[:, m, :], 1.0, w, ALU.add, ALU.mult))

            def norm_g(layer, sub):
                a = VEC["norm_g"] + 8 * (3 * layer + sub)
                return vec[:, a:a + 8]

            def take_rstd(e):
                dve.wait_ge(root_done, e + 1)
                nc.vector.reciprocal(rstd[:], root[:]).then_inc(rstd_done, 1)
                dve.wait_ge(rstd_done, e + 1)

            def make_u(p, a, shift=None):
                for k in range(KT):
                    nc.vector.scalar_tensor_tensor(out=full[:, k, :], in0=xT[:, k, :], scalar=a[:, k:k + 1], in1=rstd[:],
                                                   op0=ALU.mult, op1=ALU.mult).then_inc(u_full, 1)
                for k in range(KT):
                    dve.wait_ge(u_hi, 8 * p + k + 1)
                    if shift is None:
                        nc.vector.tensor_tensor(ulo[:, k, :], full[:, k, :], uhi[:, k, :].bitcast(F32),
                                                ALU.subtract).then_inc(u_lo, 1)
                    else:
                        nc.vector.scalar_tensor_tensor(out=ulo[:, k, :], in0=full[:, k, :], scalar=shift[:, k:k + 1],
                                                       in1=uhi[:, k, :].bitcast(F32), op0=ALU.add,
                                                       op1=ALU.subtract).then_inc(u_lo, 1)

            def add_normed(g, version):
                for k in range(KT):
                    ins = nc.vector.scalar_tensor_tensor(out=full[:, k, :], in0=bank[k // 2][:, (k % 2) * T:(k % 2 + 1) * T],
                                                         scalar=g[:, k:k + 1], in1=rstd[:], op0=ALU.mult, op1=ALU.mult)
                link(ins)
                for q in range(4):
                    s = slice(2 * q, 2 * q + 2)
                    nc.vector.tensor_tensor(xT[:, s, :], xT[:, s, :], full[:, s, :], ALU.add).then_inc(x_ready, 1)
                dve.wait_ge(x_ready, 4 * version)

            def add_scaled(c, version, done):
                dve.wait_ge(pe_done, done)
                for k in range(KT):
                    ins = nc.vector.scalar_tensor_tensor(out=xT[:, k, :], in0=bank[k // 2][:, (k % 2) * T:(k % 2 + 1) * T],
                                                         scalar=c[:, k:k + 1], in1=xT[:, k, :], op0=ALU.mult, op1=ALU.add)
                    if k % 2:
                        ins.then_inc(x_ready, 1)
                dve.wait_ge(x_ready, 4 * version)

            nc.vector.memset(eps[:], EPS)
            dve.wait_ge(vec_t, 1)
            nc.vector.tensor_copy(vec[:, 0:NVEC], bank[6][:, 0:NVEC])
            nc.vector.tensor_copy(adab[:], bank[6][:, 128:288])
            nc.vector.tensor_copy(posx[:].rearrange("p a b -> p (a b)"), bank[6][:, 288:320]).then_inc(vec_done, 1)
            dve.wait_ge(bvec_mm, 1)
            nc.vector.tensor_tensor(bvec, bank[7][0:16, 0:384], dmask, ALU.add).then_inc(bvec_done, 1)
            dve.wait_ge(x_turned, 1)
            for q in range(4):
                nc.vector.tensor_copy(xT[:, 2 * q:2 * q + 2, :], bank[q][:]).then_inc(x_ready, 1)
            dve.wait_ge(x_ready, 4)
            dve.wait_ge(vec_done, 1)
            conv(0)
            take_rstd(0)
            make_u(0, vec[:, vrow("mix_pre")])
            conv(1)
            conv(2)
            dve.wait_ge(c_ready, 1)
            for n in range(16):
                ada_add(0, n % 2, n // 2, n // 2)
                conv(n + 3)

            dve.wait_ge(kvx_in, 64)
            for a in range(2):
                entries = blk[:, a, :].rearrange("p (i g j) -> p i g j", i=16, g=2)
                for g in range(2):
                    tok = kvx[:, a, g, :].rearrange("p (j i r) -> p i j r", i=8, r=2)
                    for s in range(2):
                        ins = nc.vector.tensor_tensor(
                            entries[:, 8 * s:8 * s + 8, g, :], tok[:, :, s:s + NCMP, 0],
                            posx[:, a, 8 * s:8 * s + 8].unsqueeze(2).to_broadcast([P, 8, NCMP]), ALU.add)
                ins.then_inc(blk_full, 1)
            for a in range(2):
                dve.wait_ge(blk_hi, a + 1)
                nc.vector.tensor_tensor(bparts[a][1], blk[:, a, :], bparts[a][0].bitcast(F32), ALU.subtract).then_inc(blk_lo, 1)
            take_mods(0)
            gain(SA["ffn0"], 1, norm_g(0, 0))
            weight(SC["ffn0"], 2, 0.5)
            link(nc.vector.tensor_scalar(scal[:, QSC, 0:1], vec[:, VEC["q_norm"]:VEC["q_norm"] + 1], P ** -0.5, None, ALU.mult))
            conv(START["cmp"] + 3)
            for n in range(3):
                conv(START["up"] + n)

            E = cmpE[:, :, :, 0:NCMP]
            S = [cmpS[:, i, :].rearrange("p (t h) -> p t h", t=2) for i in range(3)]

            def over_blocks(a):
                return a.unsqueeze(3).to_broadcast([P, 2, 8, NCMP])

            dve.wait_ge(cs_mm, 1)
            mask = const("cmpmask").rearrange("p (t n) -> p t n", t=2)
            for t in range(2):
                for g in range(2):
                    sc = bank[4 + g][:, t * 64:(t + 1) * 64].rearrange("p (h n) -> p h n", h=4)[:, :, 0:NCMP]
                    ins = nc.vector.tensor_tensor(E[:, t, 4 * g:4 * g + 4, :], sc,
                                                  mask[:, t:t + 1, 0:NCMP].to_broadcast([P, 4, NCMP]), ALU.add)
            ins.then_inc(cs_dve, 1)
            dve.wait_ge(cs_dve, 1)
            link(nc.vector.tensor_reduce(S[0], E, AX.X, ALU.max))
            link(nc.vector.tensor_scalar(S[0], S[0], FLOOR, None, ALU.max))
            nc.vector.tensor_tensor(E, E, over_blocks(S[0]), ALU.subtract).then_inc(cs_dve, 1)
            dve.wait_ge(cs_exp, 1)
            link(nc.vector.tensor_reduce(S[1], E, AX.X, ALU.add))
            link(nc.vector.tensor_scalar(S[1], S[1], 1e-30, None, ALU.max))
            link(nc.vector.reciprocal(S[2], S[1]))
            dve.wait_ge(gate_done, 1)
            link(nc.vector.tensor_tensor(S[2], S[2], gate3[:].rearrange("p t (h c) -> p t h c", c=3)[:, :, :, 0], ALU.mult))
            nc.vector.tensor_tensor(E, E, over_blocks(S[2]), ALU.mult).then_inc(cs_prob, 1)

            def attention(count, base, bias_of, sink_of, gate_of):
                for u in range(count + 1):
                    if u < count:
                        w = base + u
                        sm = small[:, w % 3, :]
                        pr = prob[w % 3]
                        dve.wait_ge(s_mm, w + 1)
                        if w >= 3:
                            dve.wait_ge(s_turned, w - 2)
                        link(nc.vector.tensor_tensor(pr, bank[4 + w % 2][:, 0:384], bias_of(u), ALU.add))
                        nc.vector.tensor_reduce(sm[:, 6:7], pr[:, 0:P], AX.X, ALU.max)
                        link(nc.vector.tensor_reduce(sm[:, 7:8], pr[:, P:384], AX.X, ALU.max))
                        if sink_of(u) is not None:
                            link(nc.vector.tensor_tensor(sm[:, 6:8], sm[:, 6:8], sink_of(u).to_broadcast([P, 2]), ALU.max))
                        nc.vector.tensor_scalar(sm[:, 0:2], sm[:, 6:8], -1.0, None, ALU.mult).then_inc(s_max, 1)
                    v = u - 1
                    if 0 <= v < count:
                        w = base + v
                        sm = small[:, w % 3, :]
                        pr = prob[w % 3]
                        dve.wait_ge(s_exp, w + 1)
                        if sink_of(v) is not None:
                            link(nc.vector.tensor_tensor(sm[:, 2:4], sm[:, 2:4], sm[:, 4:6], ALU.add))
                        link(nc.vector.reciprocal(sm[:, 8:10], sm[:, 2:4]))
                        if gate_of(v) is not None:
                            link(nc.vector.tensor_tensor(sm[:, 8:10], sm[:, 8:10], gate_of(v), ALU.mult))
                        nc.vector.tensor_scalar(pr[:, 0:P], pr[:, 0:P], sm[:, 8:9], None, ALU.mult)
                        nc.vector.tensor_scalar(pr[:, P:384], pr[:, P:384], sm[:, 9:10], None, ALU.mult).then_inc(s_prob, 1)

            def split_o(done):
                for q in range(4):
                    dve.wait_ge(o_hi, done + q + 1)
                    s = slice(2 * q, 2 * q + 2)
                    nc.vector.tensor_tensor(ulo[:, s, :], bank[q][:].rearrange("p (a b) -> p a b", a=2),
                                            uhi[:, s, :].bitcast(F32), ALU.subtract).then_inc(o_lo, 1)

            dve.wait_ge(bias_in, 32)
            attention(NU, 0,
                      lambda u: bias[:, units[u][1] + (8 if units[u][0] == 2 else 0), :],
                      lambda u: sinks[:, units[u][1]:units[u][1] + 1] if units[u][0] == 2 else None,
                      lambda u: None if units[u][0] == 2 else gate3[:, :, 3 * units[u][1] + 1 + units[u][0]])
            split_o(0)

            for q in range(4):
                n = START["up"] + q
                dve.wait_ge(pe_done, n + 1)
                for m in range(2):
                    t = 4 * q + 2 * m
                    ins = nc.vector.tensor_tensor(gates[:, t:t + 2, :], gates[:, t:t + 2, :],
                                                  bank[[4, 6, 0, 2][q] + m][:].rearrange("p (a b) -> p a b", a=2), ALU.mult)
                ins.then_inc(y_taken, 1)
                conv(n + 3)
            dve.wait_ge(y_taken, 4)
            for q in range(2):
                s = slice(4 * q, 4 * q + 4)
                nc.vector.tensor_tensor(full[:, s, :], gates[:, s, :], gates[:, 8 + 4 * q:12 + 4 * q, :], ALU.add).then_inc(y_full, 1)
            for q in range(2):
                s = slice(4 * q, 4 * q + 4)
                dve.wait_ge(y_hi, q + 1)
                nc.vector.tensor_tensor(ulo[:, s, :], full[:, s, :], uhi[:, s, :].bitcast(F32), ALU.subtract).then_inc(y_lo, 1)
            conv(START["out"] + 3)
            conv(START["mlp"])
            take_rstd(1)
            add_normed(vec[:, vrow("mix_post")], 2)
            conv(START["mlp"] + 1)
            take_rstd(2)
            make_u(1, vec[:, vrow("mlp_pre")])

            b = START["mlp"]

            def split_h(i):
                dve.wait_ge(h_hi, i + 1)
                nc.vector.tensor_tensor(hlo, hfull, hhi.bitcast(F32), ALU.subtract).then_inc(h_lo, 1)

            def sub(i, i0, pieces, j, j0, conv_in=True):
                dve.wait_ge(g_act, i + 1)
                if not isinstance(i, int) or i > 0:
                    dve.wait_ge(h_lo, i)
                nc.vector.tensor_tensor(hfull, act_g, act_g, ALU.mult).then_inc(h_full, 1)
                split_h(i)
                n = b + o_local(i0)
                conv_at(RING[n], n + 1 + 2 * (i - i0))
                ada_add(1, pieces[0], j, j0)
                if conv_in:
                    n = b + i_local(i0 + 2)
                    conv_at(RING[n], n + 1 + 2 * (i - i0))
                for a in pieces[1:]:
                    ada_add(1, a, j, j0)

            def pair(j, j0, conv_in=True):
                sub(2 * j, 2 * j0, [0, 1], j, j0, conv_in)
                sub(2 * j + 1, 2 * j0 + 1, [2], j, j0, conv_in)

            pair(0, 0)
            pair(1, 1)
            with dve.Fori(2, MLP_N // 2 - 1) as j:
                pair(j, 2)
            pair(MLP_N // 2 - 1, MLP_N // 2 - 1, conv_in=False)

            b0 = START["ffn0"]
            conv(b0)
            take_rstd(3)
            add_normed(vec[:, vrow("mlp_post")], 3)
            conv(b0 + 1)
            take_mods(1)
            gain(SA["pool"], 4, norm_g(0, 1))
            link(nc.vector.scalar_tensor_tensor(out=scal[:, SC["pool"], :], in0=mods[:, 5, :], scalar=1.0,
                                                in1=vec[:, vrow("pool_scale")], op0=ALU.add, op1=ALU.mult))
            gain(SA["ffn1"], 7, norm_g(0, 2))
            weight(SC["ffn1"], 8, 0.5)
            weight(SC["ffn3"], 17, 0.5)
            take_rstd(4)
            make_u(2, scal[:, SA["ffn0"], :], mods[:, 0, :])

            def ffn(name):
                b = START[name]
                hb = H_BASE[name]
                s = SESSION[name]

                def times_up(i):
                    dve.wait_ge(g_act, hb + i + 1)
                    dve.wait_ge(h_lo, hb + i)
                    nc.vector.tensor_tensor(hfull, act_g, bank[5][:], ALU.mult).then_inc(h_full, 1)

                def step(i, i0, with_ada):
                    n = b + 3 * i0 - 1
                    conv_at(0, n + 1 + 3 * (i - i0))
                    if with_ada:
                        ada_add(s, 0, i - 1, i0 - 1)
                    times_up(i - 1)
                    conv_at(1, n + 2 + 3 * (i - i0))
                    split_h(hb + i - 1)
                    conv_at(2, n + 3 + 3 * (i - i0))
                    if with_ada and len(ADA_SESSIONS[s]) > 1:
                        ada_add(s, 1, i - 1, i0 - 1)

                step(1, 1, s is not None)
                step(2, 2, s is not None)
                with dve.Fori(3, KT + 1) as i:
                    step(i, 3, s is not None)
                with dve.Fori(KT + 1, FFN_N) as i:
                    step(i, KT + 1, False)
                times_up(FFN_N - 1)
                split_h(hb + FFN_N - 1)
                conv(b + 3 * FFN_N - 1)

            ffn("ffn0")
            n = START["pool"]
            add_scaled(scal[:, SC["ffn0"], :], 4, n)
            conv(n)
            nc.vector.memset(pool_a[:, :, 0:16], 0.0)
            nc.vector.memset(pool_b[:, :, 0:16], 0.0)
            take_rstd(5)
            for k in range(KT):
                ins = nc.vector.scalar_tensor_tensor(out=full[:, k, :], in0=xT[:, k, :], scalar=scal[:, SA["pool"], k:k + 1],
                                                     in1=rstd[:], op0=ALU.mult, op1=ALU.mult)
            link(ins)
            for k in range(KT):
                nc.vector.tensor_scalar(pool_a[:, k, 16:], full[:, k, :], mods[:, 3, k:k + 1], None, ALU.add)
                ins = nc.vector.tensor_scalar(full[:, k, :], full[:, k, :], mods[:, 3, k:k + 1], None, ALU.add)
            link(ins)
            src, dst = pool_a, pool_b
            for g in range(4):
                s = 1 << g
                link(nc.vector.tensor_tensor(dst[:, 2 * g:, 16:], src[:, 2 * g:, 16:], src[:, 2 * g:, 16 - s:272 - s], ALU.add))
                own_tiles = dst[:, 2 * g:2 * g + 2, 16:]
                rc = const("poolrc")[:, g * 16:(g + 1) * 16].unsqueeze(1).to_broadcast([P, 2, 16])
                h = full[:, 2 * g:2 * g + 2, :]
                spare = src[:, 2 * g:2 * g + 2, 16:32]
                link(nc.vector.tensor_tensor(spare, own_tiles[:, :, 0:16], rc, ALU.mult))
                nc.vector.tensor_tensor(h[:, :, 0:16], spare, h[:, :, 0:16], ALU.subtract)
                nc.vector.scalar_tensor_tensor(out=h[:, :, 16:], in0=own_tiles[:, :, 16:], scalar=0.5 / s, in1=h[:, :, 16:],
                                               op0=ALU.mult, op1=ALU.subtract).then_inc(pool_full, 1)
                src, dst = dst, src
            for g in range(4):
                s = slice(2 * g, 2 * g + 2)
                dve.wait_ge(pool_hi, g + 1)
                nc.vector.tensor_tensor(ulo[:, s, :], full[:, s, :], uhi[:, s, :].bitcast(F32), ALU.subtract).then_inc(pool_lo, 1)
            take_mods(2)
            gain(SA["kv"], 19, vec[:, vrow("kv_norm")])
            gain(SA["ffn2"], 10, norm_g(1, 0))
            conv(n + 1)
            add_scaled(scal[:, SC["pool"], :], 5, n + 1)
            conv(n + 2)
            take_rstd(6)
            make_u(3, scal[:, SA["ffn1"], :], mods[:, 6, :])
            ffn("ffn1")
            b = START["kv"]
            add_scaled(scal[:, SC["ffn1"], :], 6, b)
            conv(b)
            take_rstd(7)
            conv(b + 1)
            conv(b + 2)
            make_u(4, scal[:, SA["kv"], :], mods[:, 18, :])

            cos = const("cos").unsqueeze(1).to_broadcast([P, 2, T])
            sin = const("sin").unsqueeze(1).to_broadcast([P, 2, T])

            def rotary(r, src, turned, dst):
                for q in range(4):
                    s = slice(2 * q, 2 * q + 2)
                    dve.wait_ge(r_root, 4 * r + q + 1)
                    link(nc.vector.reciprocal(full[:, s, :], full[:, s, :]))
                    dve.wait_ge(r_swap, 4 * r + q + 1)
                    nc.vector.tensor_tensor(src[:, s, :], src[:, s, :], cos, ALU.mult)
                    link(nc.vector.tensor_tensor(turned[:, s, :], bank[q][:].rearrange("p (a b) -> p a b", a=2), sin, ALU.mult))
                    link(nc.vector.tensor_tensor(dst[:, s, :], src[:, s, :], turned[:, s, :], ALU.add))
                    ins = nc.vector.tensor_tensor(dst[:, s, :], dst[:, s, :], full[:, s, :], ALU.mult)
                ins.then_inc(r_done, 1)
                dve.wait_ge(r_done, r + 1)

            for q in range(5):
                conv(b + 3 + q)
            take_mods(3)
            weight(SC["ffn2"], 11, 0.5)
            gain(SA["moba"], 13, norm_g(1, 1))
            weight(SC["moba"], 14, 1.0)
            rotary(0, tmp2, k2, k2)
            conv(START["ffn2"])
            conv(START["ffn2"] + 1)
            make_u(5, scal[:, SA["ffn2"], :], mods[:, 9, :])
            ffn("ffn2")
            b = START["wq"]
            add_scaled(scal[:, SC["ffn2"], :], 7, b)
            conv(b)
            take_rstd(8)
            conv(b + 1)
            conv(b + 2)
            make_u(6, scal[:, SA["moba"], :], mods[:, 12, :])
            for q in range(3):
                conv(b + 3 + q)
            take_mods(4)
            gain(SA["ffn3"], 16, norm_g(1, 2))
            rotary(1, q2, tmp2, q2)
            conv(b + 6)
            attention(8, NU, lambda u: const("causal"), lambda u: None, lambda u: None)
            split_o(4)
            conv(b + 7)
            b = START["ffn3"]
            add_scaled(scal[:, SC["moba"], :], 8, b)
            conv(b)
            take_rstd(9)
            conv(b + 1)
            make_u(7, scal[:, SA["ffn3"], :], mods[:, 15, :])
            ffn("ffn3")
            add_scaled(scal[:, SC["ffn3"], :], 9, len(RING))


def kernel(**inputs):
    import concourse.bacc as bacc
    from concourse.bass_utils import run_bass_kernel_spmd

    nc = bacc.Bacc("TRN2", target_bir_lowering=False, num_devices=1)
    tables = dict(zip(("table_cst", "table_onehot", "table_mask"), shape_constants()))
    arrays, aps = {}, {}
    for name in NAMES:
        a = np.ascontiguousarray(inputs[name])
        arrays["in_" + name] = a
        aps[name] = nc.dram_tensor("in_" + name, a.shape, mybir.dt.from_np(a.dtype), kind="ExternalInput").ap()
    tabs = []
    for name, a in tables.items():
        arrays[name] = a
        tabs.append(nc.dram_tensor(name, a.shape, F32, kind="ExternalInput").ap())
    bias_rows = nc.dram_tensor("bias_rows", (P, 16, 384), F32, kind="Internal").ap()
    out = nc.dram_tensor("out_0", (1, T, D), F32, kind="ExternalOutput").ap()
    build(nc, aps, *tabs, bias_rows, out)
    r = run_bass_kernel_spmd(nc, [arrays], core_ids=[0])
    return r.results[0]["out_0"]
```

```python
from contextlib import ExitStack
import math

import numpy as np

import concourse.bass as bass
from concourse import mybir

F32 = mybir.dt.float32
F32R = mybir.dt.float32r
ALU = mybir.AluOpType
ACT = mybir.ActivationFunctionType
AX = mybir.AxisListType

P = 128
T = 256
D = 1024
KT = D // P
HD = 64
NH = 8
NCMP = 15
FF = 4096
FF2 = 2816
SLOT = 2048
NEG = -1.0e30
FLOOR = -1.0e29
EPS = 1e-6
NMOD = 20

MLP_N = FF // 256
FFN_N = FF2 // 256


def plan_slots():
    start, ring = {}, []

    def phase(name, positions):
        start[name] = len(ring)
        ring.extend(positions)

    phase("in", [n % 3 for n in range(16)])
    phase("cmp", [1, 2, 0, 1])
    phase("up", [2, 0, 1, 2])
    phase("out", [0, 1, 2, 1])
    order = [0, 2]
    for i in range(MLP_N):
        order.append(1 if i < MLP_N - 1 else 0)
        if i + 2 < MLP_N:
            order.append(0 if i % 2 == 0 else 2)
    phase("mlp", order)
    ffn = [0, 1, 2] * (FFN_N - 1) + [0]
    phase("ffn0", [1, 2] + ffn)
    phase("pool", [1])
    phase("ffn1", [2, 1] + ffn)
    phase("kv", [1, 2, 0, 1, 2, 0, 1, 2])
    phase("ffn2", [1, 2] + ffn)
    phase("wq", [1, 2, 0, 1])
    phase("wo", [2, 0, 1, 0])
    phase("ffn3", [1, 2] + ffn)
    return start, ring


START, RING = plan_slots()


def before(n):
    for m in range(n - 1, -1, -1):
        if RING[m] == RING[n]:
            return m + 1
    return 0


def filled(n):
    return sum(32 if 0 <= m - START["up"] < 4 else 16 for m in range(n + 1) if RING[m] == RING[n])


ADA_SESSIONS = [[0, 1], [2, 3], [4, 5], [6, 7], [8, 9]]
ADA_BUF = []
ADA_ACC = []
ADA_START = []
for _s in ADA_SESSIONS:
    ADA_START.append(len(ADA_BUF))
    for _k in range(KT):
        for _a in range(len(_s)):
            ADA_BUF.append(_a % 2)
            ADA_ACC.append(_a)
PAIR_MODS = [(0, 1), (2, 3), (4, 5), (6, 7), (8, 17), (18, 19), (9, 10), (11, 12), (13, 14), (15, 16)]


def ada_before(m):
    for q in range(m - 1, -1, -1):
        if ADA_BUF[q] == ADA_BUF[m]:
            return q + 1
    return 0


def ada_filled(m):
    return 16 * sum(1 for q in range(m + 1) if ADA_BUF[q] == ADA_BUF[m])


def ada_acc_before(m):
    for q in range(m - 1, -1, -1):
        if ADA_ACC[q] == ADA_ACC[m]:
            return q + 1
    return 0


VEC = {"mix_pre": 0, "mix_post": 8, "mlp_pre": 16, "mlp_post": 24, "norm_g": 32, "pool_scale": 80,
       "kv_norm": 88, "c": 96, "k_norm": 104, "q_norm": 105}
NVEC = 106

CST = {}
_at = 0
for _n, _w in (("ident", 128), ("ones", 128), ("swap", 128), ("causal", 384), ("cos", 256), ("sin", 256),
               ("cmpmask", 32), ("poolrc", 64)):
    CST[_n] = (_at, _at + _w)
    _at += _w
NCST = _at


def shape_constants():
    c = np.zeros((P, NCST), np.float32)

    def put(name, a):
        lo, hi = CST[name]
        c[:, lo:hi] = a.reshape(P, hi - lo)

    q = np.arange(P)[:, None]
    put("ident", np.eye(P, dtype=np.float32))
    put("ones", np.ones((P, P), np.float32))
    put("swap", np.eye(P, dtype=np.float32)[:, (np.arange(P) + 64) % P])
    second = np.where(P + q - np.arange(T)[None] >= 0, 0.0, NEG)
    put("causal", np.concatenate([second[:, P:], second], 1).astype(np.float32))
    inv = (10000.0 ** (-(np.arange(0, P, 2) / float(P)))).astype(np.float32)
    ang = np.arange(T, dtype=np.float32)[:, None] * inv[None, :]
    cos, sin = np.cos(ang).T, np.sin(ang).T
    put("cos", np.concatenate([cos, cos], 0))
    put("sin", np.concatenate([-sin, sin], 0))
    end = np.arange(NCMP) * 16 + 31
    m = np.full((P, 2, 16), NEG, np.float32)
    for t in range(2):
        m[:, t, :NCMP] = np.where(end[None] <= t * P + q, 0.0, NEG)
    put("cmpmask", m)
    rc = np.stack([1.0 / np.minimum(np.arange(16) + 1, w) for w in (2, 4, 8, 16)]).astype(np.float32)
    put("poolrc", np.broadcast_to(rc[None], (P, 4, 16)))
    dist = 255 - np.arange(384)
    d = np.maximum(dist, 0)
    df = np.maximum(d, 1).astype(np.float32)
    large = 16 + (np.log(df / np.float32(16)) / np.float32(math.log(64)) * np.float32(16)).astype(np.int32)
    bucket = np.where(d < 16, d, np.minimum(large, 31))
    onehot = (bucket[None] == np.arange(32)[:, None]).astype(np.float32)
    mask = np.zeros((16, 384), np.float32)
    mask[:8] = np.where(dist < 0, NEG, 0.0)
    mask[8:] = np.where((dist < 0) | (dist >= 128), NEG, 0.0)
    return c, onehot, mask


NAMES = ["x", "norm_mix_pre", "norm_mix_post", "norm_mlp_pre", "norm_mlp_post", "w_in", "cmp_pos_k", "cmp_w1_k",
         "cmp_w2_k", "cmp_pos_v", "cmp_w1_v", "cmp_w2_v", "attn_sinks", "rel_bias", "w_up_nsa", "w_up_swa",
         "w_out", "w_mlp_in", "w_mlp_out", "c_2", "ada_w_2", "ada_b_2", "norm_g_2", "ffn_w_in_2", "ffn_w_out_2",
         "pool_w_2", "pool_scale_2", "kv_norm_2", "kv_ada_w_2", "kv_ada_b_2", "w_kv_2", "k_norm_2", "w_q_2",
         "q_norm_2", "w_o_2"]


def build(nc, A, cst_dram, onehot_dram, dmask_dram, bias_dram, out):
    with ExitStack() as ctx:
        def sb(name, shape, dt=F32):
            return ctx.enter_context(nc.sbuf_tensor(name, shape, dt))

        def sem(name):
            return ctx.enter_context(nc.semaphore(name))

        raw = sb("raw", [P, 3, SLOT])
        whi = sb("whi", [P, 3, SLOT], F32R)
        wlo = sb("wlo", [P, 3, SLOT], F32R)
        ada = sb("ada", [P, 2, SLOT])
        acc = sb("acc", [P, 3, SLOT])
        xT = sb("xT", [P, KT, T])
        full = sb("full", [P, KT, T])
        uhi = sb("uhi", [P, KT, T], F32R)
        ulo = sb("ulo", [P, KT, T], F32R)
        cst = sb("cst", [P, NCST])
        wide = sb("wide", [P, 4352])
        arena = sb("arena", [P, 5632])
        mix = sb("mix", [P, 2048])
        hsplit = sb("hsplit", [P, 2, 512], F32R)
        vec = sb("vec", [P, 112])
        adab = sb("adab", [P, NMOD * KT])
        mods = sb("mods", [P, NMOD, KT])
        scal = sb("scal", [P, 16, KT])
        csilu = sb("csilu", [P, KT])
        root = sb("root", [P, T])
        eps = sb("eps", [P, 1])
        sinks = sb("sinks", [P, 8])
        small = sb("small", [P, 3, 16])
        gate3 = sb("gate3", [P, 2, 24])
        wg = sb("wg", [P, KT, 24])
        posx = sb("posx", [P, 2, 16])
        h1 = sb("h1", [P, 2, 2, 32])
        kcT = sb("kcT", [P, 16])
        cmpS = sb("cmpS", [P, 3, 16])

        bank = [ctx.enter_context(nc.psum_tensor(f"bank{i}", [P, 512], F32)) for i in range(8)]

        def const(name):
            return cst[:, CST[name][0]:CST[name][1]]

        ident, ones = const("ident"), const("ones")
        SA = {"ffn0": 0, "pool": 1, "ffn1": 2, "kv": 3, "ffn2": 4, "moba": 5, "ffn3": 6}
        SC = {"ffn0": 7, "pool": 8, "ffn1": 9, "ffn2": 10, "moba": 11, "ffn3": 12}
        QSC = 13

        def cols(buf, a, *dims):
            n = int(np.prod(dims))
            v = buf[:, a:a + n]
            if len(dims) == 2:
                return v.rearrange("p (a b) -> p a b", a=dims[0])
            if len(dims) == 3:
                return v.rearrange("p (a b c) -> p a b c", a=dims[0], b=dims[1])
            return v

        gates = cols(wide, 0, 16, T)
        qn = cols(arena, 0, 4, T)
        qs = cols(arena, 1024, 4, T)
        kT = cols(arena, 2048, 3, T)
        vv = cols(arena, 2816, 3, 2, P)
        kvr = cols(arena, 3584, 2, T)
        kvx = cols(arena, 4096, 2, 2, T)
        vcs = arena[0:16, 5120:5248].rearrange("p (g d) -> p g d", g=2)
        w2 = cols(arena, 5248, 2, 2, HD)
        cmpE = cols(wide, 4096, 2, 8, 16)
        blk = cols(mix, 0, 2, 480)
        uhi_flat = uhi[:].rearrange("p a b -> p (a b)")
        ulo_flat = ulo[:].rearrange("p a b -> p (a b)")
        bparts = [(uhi_flat[:, 1024 * a:1024 * a + 480], ulo_flat[:, 1024 * a:1024 * a + 480]) for a in range(2)]
        hrow = cols(mix, 1024, 2, T)[0:30]
        vrows = cols(mix, 0, 4, P)
        onehot = mix[0:32, 512:896]
        dmask = mix[0:16, 896:1280]
        relb = mix[0:32, 1280:1296]
        bvec = mix[0:16, 1600:1984]
        bias = acc[:].rearrange("p a b -> p (a b)").rearrange("p (h c) -> p h c", h=16)
        prob = [mix[:, 384 * i:384 * i + 384] for i in range(3)]
        probT = [mix[:, 1152 + 384 * i:1536 + 384 * i] for i in range(2)]
        pcT = full[0:NCMP, :, :]
        act_g = mix[:, 0:512]
        hfull = mix[:, 512:1024]
        hhi, hlo = hsplit[:, 0, :], hsplit[:, 1, :]
        pool_a = cols(wide, 0, KT, 272)
        pool_b = cols(arena, 0, KT, 272)
        k2 = cols(wide, 0, KT, T)
        v2 = cols(wide, 2048, 2, D)
        q2 = cols(arena, 0, KT, T)
        tmp2 = cols(arena, 2048, KT, T)
        hroot = cols(mix, 0, KT, T)
        xin = full[:].rearrange("p a b -> p (a b)").rearrange("p (t d) -> p t d", t=2)

        loaded = [sem(f"loaded{i}") for i in range(3)]
        ada_loaded = [sem(f"ada_loaded{i}") for i in range(2)]
        consts_in = sem("consts_in")
        x_in = sem("x_in")
        cst_in = sem("cst_in")
        late_in = sem("late_in")
        late_t = sem("late_t")
        f_ready = sem("f_ready")
        hi_done = sem("hi_done")
        lo_done = sem("lo_done")
        pe_done = sem("pe_done")
        ada_used = sem("ada_used")
        ada_sum = sem("ada_sum")
        mods_done = sem("mods_done")
        vec_t = sem("vec_t")
        vec_done = sem("vec_done")
        late_done = sem("late_done")
        c_ready = sem("c_ready")
        x_turned = sem("x_turned")
        x_ready = sem("x_ready")
        sq_ready = sem("sq_ready")
        ss_done = sem("ss_done")
        root_done = sem("root_done")
        f_normed = sem("f_normed")
        u_full = sem("u_full")
        u_hi = sem("u_hi")
        u_lo = sem("u_lo")
        in_taken = sem("in_taken")
        kvx_in = sem("kvx_in")
        gate_mm = sem("gate_mm")
        gate_done = sem("gate_done")
        blk_full = sem("blk_full")
        blk_hi = sem("blk_hi")
        blk_lo = sem("blk_lo")
        gelu_done = sem("gelu_done")
        h1_turned = sem("h1_turned")
        h1_done = sem("h1_done")
        ckv_mm = sem("ckv_mm")
        ckv_done = sem("ckv_done")
        bvec_mm = sem("bvec_mm")
        bvec_done = sem("bvec_done")
        bvec_out = sem("bvec_out")
        bias_in = sem("bias_in")
        cs_mm = sem("cs_mm")
        cs_dve = sem("cs_dve")
        cs_exp = sem("cs_exp")
        cs_prob = sem("cs_prob")
        cs_turned = sem("cs_turned")
        cs_done = sem("cs_done")
        s_mm = sem("s_mm")
        s_max = sem("s_max")
        s_exp = sem("s_exp")
        s_prob = sem("s_prob")
        s_turned = sem("s_turned")
        s_copied = sem("s_copied")
        s_pv = sem("s_pv")
        o_hi = sem("o_hi")
        o_lo = sem("o_lo")
        y_taken = sem("y_taken")
        y_full = sem("y_full")
        y_hi = sem("y_hi")
        y_lo = sem("y_lo")
        g_act = sem("g_act")
        h_full = sem("h_full")
        h_hi = sem("h_hi")
        h_lo = sem("h_lo")
        pool_full = sem("pool_full")
        pool_hi = sem("pool_hi")
        pool_lo = sem("pool_lo")
        v2_taken = sem("v2_taken")
        r_copy = sem("r_copy")
        r_ss = sem("r_ss")
        r_root = sem("r_root")
        r_swap = sem("r_swap")
        r_done = sem("r_done")
        out_turned = sem("out_turned")
        out_copied = sem("out_copied")
        out_dma = sem("out_dma")
        dve_own = sem("dve_own")
        act_own = sem("act_own")

        block = ctx.enter_context(nc.Block())

        def v8(buf, p):
            return buf[:, p, :].rearrange("p (k c) -> p k c", k=8)

        def pair_view(buf, p):
            return buf[:, p:p + 2, :].rearrange("p a b -> p (a b)").rearrange("p (k g d) -> p k g d", g=2, d=HD)

        QSLOTS = {0: (0, 0), 1: (0, 1), 3: (0, 0), 4: (0, 1)}

        def split_views(buf, n):
            if n in QSLOTS:
                return pair_view(buf, QSLOTS[n][0])[:, :, QSLOTS[n][1], :]
            return buf[:, RING[n], :]

        def raw_view(n):
            return raw[:, RING[n], :].rearrange("p (k d) -> p k d", d=HD) if n in QSLOTS else raw[:, RING[n], :]

        def v4(buf, p):
            return buf[:, p, :].rearrange("p (k c) -> p k c", k=4)

        def v2k(buf, p):
            return buf[:, p, :].rearrange("p (k c) -> p k c", k=2)

        def vrow(name):
            return slice(VEC[name], VEC[name] + 8)

        def const_loads():
            for name, key in (("mix_pre", "norm_mix_pre"), ("mix_post", "norm_mix_post"), ("mlp_pre", "norm_mlp_pre"),
                              ("mlp_post", "norm_mlp_post"), ("pool_scale", "pool_scale_2"), ("c", "c_2")):
                yield vrows[vrow(name), 0, :], A[key][0].rearrange("(r c) -> r c", c=P)
            yield vrows[32:80, 0, :], A["norm_g_2"].rearrange("l s (r c) -> (l s r) c", c=P)
            yield vrows[vrow("kv_norm"), 0, :], A["kv_norm_2"].rearrange("(r c) -> r c", c=P)
            yield vrows[104:105, 0, :], A["k_norm_2"].rearrange("(r c) -> r c", c=P)
            yield vrows[105:106, 0, :], A["q_norm_2"]

        def late_loads():
            ada_rows = A["ada_b_2"].rearrange("l (r c) -> (l r) c", c=P)
            yield vrows[0:80, 1, :], ada_rows[0:80]
            yield vrows[0:64, 2, :], ada_rows[80:144]
            yield vrows[64:80, 2, :], A["kv_ada_b_2"].rearrange("(r c) -> r c", c=P)
            yield vrows[0:16, 3, :], A["cmp_pos_k"][0].rearrange("(r i) d -> r (i d)", i=2)
            yield vrows[16:32, 3, :], A["cmp_pos_v"][0].rearrange("(r i) d -> r (i d)", i=2)
            yield relb, A["rel_bias"]
            yield onehot, onehot_dram
            yield dmask, dmask_dram
            yield wg[:], A["w_in"][0].rearrange("(k p) c -> p k c", p=P)[:, :, 1280:1304]
            yield w2[:, 0], A["cmp_w2_k"][0].rearrange("(m p) d -> p m d", p=P)
            yield w2[:, 1], A["cmp_w2_v"][0].rearrange("(m p) d -> p m d", p=P)
            yield sinks[:], A["attn_sinks"].partition_broadcast(P).rearrange("p a h -> p (a h)")

        N_CONSTS, N_LATE = len(list(const_loads())), len(list(late_loads()))

        ffn_phase = [("ffn0", 0, 0), ("ffn1", 0, 1), ("ffn2", 1, 0), ("ffn3", 1, 1)]
        units = [(b, t + 4 * g) for t in range(4) for g in range(2) for b in (0, 1)]
        units += [(2, t + 4 * g) for t in range(4) for g in range(2)]
        NU = len(units)
        H_BASE = {"mlp": 0, "ffn0": MLP_N, "ffn1": MLP_N + FFN_N, "ffn2": MLP_N + 2 * FFN_N, "ffn3": MLP_N + 3 * FFN_N}
        SESSION = {"in": 0, "mlp": 1, "ffn0": 2, "ffn1": 3, "ffn2": 4, "ffn3": None}

        def o_local(i):
            return 2 * i + 2 if not isinstance(i, int) or i < MLP_N - 1 else 2 * MLP_N - 1

        def i_local(i):
            return 2 * i - 1 if not isinstance(i, int) or i > 0 else 0

        CHUNKED = ["mlp", "ffn0", "pool", "ffn1", "ffn2", "ffn3"]

        def end_of(name):
            return START[name] + {"mlp": 2 * MLP_N, "pool": 1, "out": 4, "wo": 4}.get(name, 3 * FFN_N)

        def wait_bank(eng, name, q):
            if name in CHUNKED and q < 3:
                eng.wait_ge(f_ready, 3 * CHUNKED.index(name) + q + 1)
            else:
                eng.wait_ge(pe_done, end_of(name) if name in CHUNKED else START[name] + q + 1)

        @block.sync
        def _(sp):
            def load(n, pos, free, dst_view, src):
                if free is not None:
                    sp.wait_ge(lo_done, free)
                sp.dma_start(dst_view, src).then_inc(loaded[pos], 16)

            def slot(n, view, src):
                load(n, RING[n], before(n) or None, view(raw, RING[n]), src)

            def ada_src(pair, k):
                rows = bass.ds(k * P, P) if not isinstance(k, int) else slice(k * P, k * P + P)
                if pair == 4:
                    return A["ada_w_2"][:, rows, 8 * D:9 * D].rearrange("l p c -> p l c")
                if pair == 5:
                    return A["kv_ada_w_2"][rows, :].rearrange("p (a c) -> p a c", a=2)
                layer, at = (0, pair) if pair < 4 else (1, pair - 6)
                return A["ada_w_2"][layer, rows, 2 * at * D:2 * (at + 1) * D].rearrange("p (a c) -> p a c", a=2)

            def ada_load(s, a, k, k0):
                w = len(ADA_SESSIONS[s])
                m = ADA_START[s] + k0 * w + a
                free = ada_before(m)
                step = 0 if isinstance(k, int) else w
                if free:
                    sp.wait_ge(ada_used, free + step * (k - k0))
                sp.dma_start(ada[:, ADA_BUF[m], :].rearrange("p (a c) -> p a c", a=2),
                             ada_src(ADA_SESSIONS[s][a], k)).then_inc(ada_loaded[ADA_BUF[m]], 16)

            w_in = A["w_in"][0].rearrange("(k p) c -> p k c", p=P)
            q1, q2_ = 1304, 2072
            starts = [0, 256, 512, q1, q1 + 256, 768, 1024, q1 + 512] + [q2_ + 256 * j for j in range(8)]
            sp.dma_start(xin, A["x"][0].rearrange("(t p) d -> p t d", p=P)).then_inc(x_in, 16)
            sp.dma_start(cst[:], cst_dram).then_inc(cst_in, 16)
            for n in range(3):
                slot(n, v8, w_in[:, :, starts[n]:starts[n] + 256])
            for n in range(2):
                ada_load(0, n % 2, n // 2, n // 2)
            for n in range(3, 18):
                if n < 16:
                    slot(n, v8, w_in[:, :, starts[n]:starts[n] + 256])
                if n < 17:
                    ada_load(0, (n - 1) % 2, (n - 1) // 2, (n - 1) // 2)
            for n, name in enumerate(["cmp_w1_k", "cmp_w1_k", "cmp_w1_v", "cmp_w1_v"]):
                src = A[name][0].rearrange("(s k p) c -> s p k c", p=P, k=8)[n % 2]
                slot(START["cmp"] + n, v8, src)
            for n in range(4):
                w = A["w_up_nsa" if n < 2 else "w_up_swa"][0].rearrange("(g t d) c -> g d t c", g=2, d=HD)
                s = START["up"] + n
                c0 = 512 * (n % 2)
                sp.wait_ge(lo_done, before(s))
                sp.dma_start(v4(raw, RING[s])[0:HD], w[0][:, :, c0:c0 + 512]).then_inc(loaded[RING[s]], 16)
                sp.dma_start(v4(raw, RING[s])[HD:P], w[1][:, :, c0:c0 + 512]).then_inc(loaded[RING[s]], 16)
            w_out = A["w_out"][0].rearrange("(k p) c -> p k c", p=P)
            for n in range(4):
                slot(START["out"] + n, v8, w_out[:, :, 256 * n:256 * n + 256])

            mi = A["w_mlp_in"][0]
            mo = A["w_mlp_out"][0]
            b = START["mlp"]

            def mlp_load_in(i, i0):
                n = b + i_local(i0)
                c = bass.ds(i * 256, 256) if not isinstance(i, int) else slice(i * 256, i * 256 + 256)
                load(n, RING[n], before(n) + 2 * (i - i0), v8(raw, RING[n]), mi[:, c].rearrange("(k p) c -> p k c", p=P))

            def mlp_load_out(i, i0):
                n = b + o_local(i0)
                r = bass.ds(i * 256, 256) if not isinstance(i, int) else slice(i * 256, i * 256 + 256)
                load(n, RING[n], before(n) + 2 * (i - i0), v2k(raw, RING[n]), mo[r, :].rearrange("(k p) c -> p k c", p=P))

            def mlp_pair(j, j0, last=False):
                i, i0 = 2 * j, 2 * j0
                mlp_load_out(i, i0)
                ada_load(1, 0, j, j0)
                if not last:
                    mlp_load_in(i + 2, i0 + 2)
                mlp_load_out(i + 1, i0 + 1)
                ada_load(1, 1, j, j0)
                if not last:
                    mlp_load_in(i + 3, i0 + 3)

            mlp_load_in(0, 0)
            mlp_load_in(1, 1)
            mlp_pair(0, 0)
            mlp_pair(1, 1)
            with sp.Fori(2, MLP_N // 2 - 1) as j:
                mlp_pair(j, 2)
            mlp_pair(MLP_N // 2 - 1, MLP_N // 2 - 1, last=True)

            def ffn(name, layer, sub):
                b = START[name]
                wi, wo = A["ffn_w_in_2"][layer, sub], A["ffn_w_out_2"][layer, sub]
                s = SESSION[name]

                def body(i, i0, with_ada):
                    n = b + 3 * i0 - 1
                    for q in range(2):
                        if not isinstance(i, int):
                            c = bass.ds(i * 256 + q * FF2, 256)
                        else:
                            c = slice(i * 256 + q * FF2, i * 256 + q * FF2 + 256)
                        load(n + q, q, before(n + q) + 3 * (i - i0), v8(raw, q), wi[:, c].rearrange("(k p) c -> p k c", p=P))
                        if q == 0 and with_ada:
                            ada_load(s, 0, i - 1, i0 - 1)
                    r = bass.ds((i - 1) * 256, 256) if not isinstance(i, int) else slice((i - 1) * 256, i * 256)
                    load(n + 2, 2, before(n + 2) + 3 * (i - i0), v2k(raw, 2), wo[r, :].rearrange("(k p) c -> p k c", p=P))
                    if with_ada and len(ADA_SESSIONS[s]) > 1:
                        ada_load(s, 1, i - 1, i0 - 1)

                for q in range(2):
                    slot(b + q, v8, wi[:, q * FF2:q * FF2 + 256].rearrange("(k p) c -> p k c", p=P))
                body(1, 1, s is not None)
                body(2, 2, s is not None)
                with sp.Fori(3, KT + 1) as i:
                    body(i, 3, s is not None)
                with sp.Fori(KT + 1, FFN_N) as i:
                    body(i, KT + 1, False)
                slot(b + 3 * FFN_N - 1, v2k, wo[FF2 - 256:FF2, :].rearrange("(k p) c -> p k c", p=P))

            ffn(*ffn_phase[0])
            slot(START["pool"], v8, A["pool_w_2"][0].rearrange("g (k p) c -> p (g k) c", p=P))
            ffn(*ffn_phase[1])
            w_kv = A["w_kv_2"].rearrange("(k p) c -> p k c", p=P)
            for n in range(8):
                slot(START["kv"] + n, v8, w_kv[:, :, 256 * n:256 * n + 256])
            ffn(*ffn_phase[2])
            for name, key in (("wq", "w_q_2"), ("wo", "w_o_2")):
                w = A[key][0].rearrange("(k p) c -> p k c", p=P)
                for n in range(4):
                    slot(START[name] + n, v8, w[:, :, 256 * n:256 * n + 256])
            ffn(*ffn_phase[3])
            for t in range(2):
                sp.wait_ge(out_copied, 2 * (t + 1))
                sp.dma_start(out[0, t * P:(t + 1) * P, :], xin[:, t, :]).then_inc(out_dma, 16)
            sp.wait_ge(out_dma, 32)

        @block.gpsimd
        def _(pool):
            for dst, src in late_loads():
                pool.dma_start(dst, src).then_inc(late_in, 16)
            pool.wait_ge(bvec_done, 1)
            pool.dma_start(bias_dram.rearrange("q h c -> h q c"),
                           bvec.unsqueeze(1).to_broadcast([16, P, 384])).then_inc(bvec_out, 16)
            pool.wait_ge(in_taken, 3)
            for g in range(2):
                src = kvr[g * HD:(g + 1) * HD]
                pool.dma_start(kvx[0:HD, :, g, :], src).then_inc(kvx_in, 16)
                pool.dma_start(kvx[HD:P, :, g, 0:T - 1], src[:, :, 1:T]).then_inc(kvx_in, 16)
            pool.wait_ge(bvec_out, 16)
            pool.wait_ge(ada_sum, 1)
            second = bass.AP(bias_dram.tensor, 127, [[16 * 384 - 1, P], [384, 16], [1, T]])
            first = bass.AP(bias_dram.tensor, 127 + P, [[16 * 384 - 1, P], [384, 16], [1, P]])
            pool.dma_start(bias[:, :, 0:P], first).then_inc(bias_in, 16)
            pool.dma_start(bias[:, :, P:384], second).then_inc(bias_in, 16)

        @block.tensor
        def _(pe):
            def mm3(o, wh, wl, xh, xl, start, stop, skip=False):
                nc.tensor.matmul(o, wh, xh, start=start, stop=False, skip_group_check=skip)
                nc.tensor.matmul(o, wh, xl, start=False, stop=False, skip_group_check=skip)
                return nc.tensor.matmul(o, wl, xh, start=False, stop=stop, skip_group_check=skip)

            def dense8(n, pos, o, pre=None, lo_at=None):
                pe.wait_ge(lo_done, lo_at if lo_at is not None else n + 1)
                wh, wl = v8(whi, pos), v8(wlo, pos)
                for m in range(2):
                    for k in range(KT):
                        if pre is not None and m == 0:
                            pe.wait_ge(u_lo, pre + k + 1)
                        ins = mm3(o[:, m * T:(m + 1) * T], wh[:, k, m * P:(m + 1) * P], wl[:, k, m * P:(m + 1) * P],
                                  uhi[:, k, :], ulo[:, k, :], k == 0, k == KT - 1)
                ins.then_inc(pe_done, 1)

            def norm_sum(e):
                for k in range(KT):
                    if k % 2 == 0:
                        pe.wait_ge(sq_ready, 4 * e + k // 2 + 1)
                    ins = nc.tensor.matmul(bank[6][:, 0:T], ones, full[:, k, :], start=k == 0, stop=k == KT - 1)
                ins.then_inc(ss_done, 1)

            def ada_reduce(s):
                w = len(ADA_SESSIONS[s])
                pe.wait_ge(ada_used, ADA_START[s] + KT * w)
                for a in range(w):
                    for j in range(16):
                        ins = nc.tensor.matmul(bank[7][:, 16 * a + j:16 * a + j + 1], acc[:, a, j * P:(j + 1) * P],
                                               ones[:, 0:1], start=True, stop=True)
                ins.then_inc(ada_sum, 1)

            pe.wait_ge(cst_in, 16)
            pe.wait_ge(x_in, 16)
            for k in range(KT):
                for t in range(2):
                    ins = nc.tensor.transpose(bank[k // 2][:, (k % 2) * T + t * P:(k % 2) * T + (t + 1) * P],
                                              xin[:, t, k * P:(k + 1) * P], ident)
                if k % 2:
                    ins.then_inc(x_turned, 1)
            pe.wait_ge(consts_in, 16 * N_CONSTS)
            nc.tensor.transpose(bank[7][:, 384:384 + NVEC], vrows[0:NVEC, 0, :], ident[0:NVEC, 0:NVEC]).then_inc(vec_t, 1)
            norm_sum(0)
            pe.wait_ge(late_in, 16 * N_LATE)
            pe.wait_ge(root_done, 1)
            nc.tensor.transpose(bank[6][:, 128:208], vrows[0:80, 1, :], ident[0:80, 0:80])
            nc.tensor.transpose(bank[6][:, 208:288], vrows[0:80, 2, :], ident[0:80, 0:80])
            nc.tensor.transpose(bank[6][:, 288:320], vrows[0:32, 3, :], ident[0:32, 0:32]).then_inc(late_t, 1)
            pe.wait_ge(vec_done, 1)
            nc.tensor.matmul(bank[7][0:16, 0:384], relb, onehot, start=True, stop=True).then_inc(bvec_mm, 1)

            pool6 = [0, 1, 2, 3, 4, 5]

            def q_pair(n):
                pe.wait_ge(lo_done, n + 2)
                p = RING[n]
                for t in range(4):
                    o = bank[pool6[(n + t // 2) % 6]][:, (t % 2) * T:(t % 2 + 1) * T]
                    for k in range(KT):
                        if n == 0 and t == 0:
                            pe.wait_ge(u_lo, k + 1)
                        wh, wl = pair_view(whi, p)[:, 4 * k + t, :, :], pair_view(wlo, p)[:, 4 * k + t, :, :]
                        wh, wl = wh.rearrange("p g d -> p (g d)"), wl.rearrange("p g d -> p (g d)")
                        ins = mm3(o, wh, wl, uhi[:, k, :], ulo[:, k, :], k == 0, k == KT - 1)
                ins.then_inc(pe_done, 2)

            def k_and_v(n):
                pe.wait_ge(lo_done, n + 1)
                wh, wl = v8(whi, RING[n]), v8(wlo, RING[n])
                o = bank[pool6[n % 6]]
                for k in range(KT):
                    mm3(o[:, 0:T], wh[:, k, 0:P], wl[:, k, 0:P], uhi[:, k, :], ulo[:, k, :], k == 0, k == KT - 1)
                for t in range(2):
                    for k in range(KT):
                        ins = mm3(o[:, T + t * P:T + (t + 1) * P], uhi[:, k, t * P:(t + 1) * P],
                                  ulo[:, k, t * P:(t + 1) * P], wh[:, k, P:2 * P], wl[:, k, P:2 * P], k == 0, k == KT - 1)
                ins.then_inc(pe_done, 1)

            n = 0
            while n < 16:
                if n >= 5:
                    pe.wait_ge(in_taken, n - 4)
                if n in (0, 3):
                    q_pair(n)
                    n += 2
                    continue
                if n in (5, 6, 7):
                    k_and_v(n)
                else:
                    dense8(n, RING[n], bank[pool6[n % 6]])
                n += 1
            for t in range(2):
                for k in range(KT):
                    ins = nc.tensor.matmul(bank[6][:, 256 + 24 * t:280 + 24 * t], full[:, k, t * P:(t + 1) * P], wg[:, k, :],
                                           start=k == 0, stop=k == KT - 1)
            ins.then_inc(gate_mm, 1)
            pe.wait_ge(bvec_done, 1)
            ada_reduce(0)

            pe.wait_ge(in_taken, 16)
            for a in range(2):
                pe.wait_ge(blk_lo, a + 1)
                for ii in range(16):
                    n = START["cmp"] + 2 * a + ii // 8
                    if ii % 8 == 0:
                        pe.wait_ge(lo_done, n + 1)
                    c = slice(1024 * a + 30 * ii, 1024 * a + 30 * ii + P)
                    ins = mm3(bank[4 + a][:, 0:T], uhi_flat[:, c], ulo_flat[:, c], v8(whi, RING[n])[:, ii % 8, :],
                              v8(wlo, RING[n])[:, ii % 8, :], ii == 0, ii == 15)
                    if ii % 8 == 7:
                        ins.then_inc(pe_done, 1)
            pe.wait_ge(gate_done, 1)
            for a in range(2):
                pe.wait_ge(gelu_done, a + 1)
                for m in range(2):
                    ins = nc.tensor.transpose(bank[6][:, 32 * (2 * a + m):32 * (2 * a + m) + 30],
                                              hrow[:, a, m * P:(m + 1) * P], ident[0:30, 0:30])
            ins.then_inc(h1_turned, 1)
            pe.wait_ge(h1_done, 1)
            for g in range(2):
                for m in range(2):
                    nc.tensor.matmul(bank[4][g * HD:(g + 1) * HD, 256:256 + NCMP], w2[:, 0, m, :],
                                     h1[:, 0, m, g * NCMP:(g + 1) * NCMP], start=m == 0, stop=m == 1)
            for g in range(2):
                for m in range(2):
                    ins = nc.tensor.matmul(bank[5][0:NCMP, 256 + g * HD:256 + (g + 1) * HD],
                                           h1[:, 1, m, g * NCMP:(g + 1) * NCMP], w2[:, 1, m, :], start=m == 0, stop=m == 1)
            ins.then_inc(ckv_mm, 1)

            pe.wait_ge(ckv_done, 1)
            for h in range(NH):
                g, t = h // 4, h % 4
                for qt in range(2):
                    c = qt * 64 + t * 16
                    ins = nc.tensor.matmul(bank[4 + g][:, c:c + NCMP],
                                           qn[g * HD:(g + 1) * HD, t, qt * P:(qt + 1) * P], kcT[g * HD:(g + 1) * HD, 0:NCMP],
                                           start=True, stop=True)
            ins.then_inc(cs_mm, 1)
            pe.wait_ge(cs_prob, 1)
            for h in range(NH):
                for qt in range(2):
                    b = [2, 3, 6, 7][h // 2]
                    if h == 6 and qt == 0:
                        pe.wait_ge(mods_done, 1)
                    c = (h % 2) * T + qt * P
                    ins = nc.tensor.transpose(bank[b][0:NCMP, c:c + P], cmpE[:, qt, h, 0:NCMP], ident)
            ins.then_inc(cs_turned, 1)

            def attention(count, base, q_of, k_of, v_of, o_of, before_pv, start_of, stop_of):
                for u in range(count + 3):
                    if u < count:
                        w = base + u
                        if w >= 2:
                            pe.wait_ge(s_max, w - 1)
                        sc = bank[4 + w % 2]
                        q, k = q_of(u), k_of(u)
                        nc.tensor.matmul(sc[:, 0:P], q[:, 0:P], k[:, 0:P], start=True, stop=True)
                        nc.tensor.matmul(sc[:, P:384], q[:, P:T], k, start=True, stop=True).then_inc(s_mm, 1)
                    v = u - 2
                    if 0 <= v < count:
                        w = base + v
                        pe.wait_ge(s_prob, w + 1)
                        if w >= 2:
                            pe.wait_ge(s_copied, w - 1)
                        for b in range(3):
                            ins = nc.tensor.transpose(bank[6 + w % 2][:, b * P:(b + 1) * P],
                                                      prob[w % 3][:, b * P:(b + 1) * P], ident)
                        ins.then_inc(s_turned, 1)
                    v = u - 3
                    if 0 <= v < count:
                        w = base + v
                        pe.wait_ge(s_copied, w + 1)
                        before_pv(v)
                        pT = probT[w % 2]
                        nc.tensor.matmul(o_of(v), v_of(v, 0), pT[:, 0:T], start=start_of(v), stop=False)
                        nc.tensor.matmul(o_of(v)[:, P:T], v_of(v, 1), pT[:, T:384], start=False,
                                         stop=stop_of(v)).then_inc(s_pv, 1)

            def half(h):
                return slice((h // 4) * HD, (h // 4 + 1) * HD)

            def o1(u):
                b, h = units[u]
                t = h % 4
                return bank[(2 if b == 2 else 0) + t // 2][half(h), (t % 2) * T:(t % 2 + 1) * T]

            def compressed_first(u):
                b, h = units[u]
                if b == 0:
                    if u == 0:
                        pe.wait_ge(cs_done, 4)
                    nc.tensor.matmul(o1(u), vcs[0:NCMP, h // 4, :], pcT[:, h, :], start=True, stop=False)

            pe.wait_ge(cs_dve, 1)
            pe.wait_ge(cs_done, 4)
            attention(NU, 0,
                      lambda u: (qs if units[u][0] == 2 else qn)[half(units[u][1]), units[u][1] % 4, :],
                      lambda u: kT[half(units[u][1]), units[u][0], :],
                      lambda u, kt: vv[:, units[u][0], kt, half(units[u][1])],
                      o1, compressed_first, lambda u: units[u][0] == 2, lambda u: units[u][0] >= 1)

            upbanks = [4, 6, 0, 2]
            for q in range(4):
                n = START["up"] + q
                pe.wait_ge(lo_done, n + 1)
                pe.wait_ge(o_lo, 4)
                for m in range(4):
                    for k in range(4):
                        o = bank[upbanks[q] + m // 2][:, (m % 2) * T:(m % 2 + 1) * T]
                        kk = k + 4 * (q // 2)
                        ins = mm3(o, v4(whi, RING[n])[:, k, m * P:(m + 1) * P], v4(wlo, RING[n])[:, k, m * P:(m + 1) * P],
                                  uhi[:, kk, :], ulo[:, kk, :], k == 0, k == 3)
                ins.then_inc(pe_done, 1)
            for q in range(4):
                n = START["out"] + q
                if q == 0:
                    pe.wait_ge(y_lo, 2)
                dense8(n, RING[n], bank[q])
            norm_sum(1)
            norm_sum(2)

            b = START["mlp"]

            def out_chunk(pos, first, last):
                hh = uhi_flat[:, 0:512] if last else hhi
                hl = ulo_flat[:, 0:512] if last else hlo
                wh, wl = v2k(whi, pos), v2k(wlo, pos)
                for m in range(KT):
                    for k in range(2):
                        ins = mm3(bank[m // 2][:, (m % 2) * T:(m % 2 + 1) * T], wh[:, k, m * P:(m + 1) * P],
                                  wl[:, k, m * P:(m + 1) * P], hh[:, k * T:(k + 1) * T], hl[:, k * T:(k + 1) * T],
                                  first and k == 0 and m % 2 == 0, last and k == 1, skip=True)
                    if last and m in (1, 3, 5):
                        ins.then_inc(f_ready, 1)
                ins.then_inc(pe_done, 1)

            def mlp_in_mm(i, i0):
                loc = b + i_local(i0)
                if not (isinstance(i, int) and i < 2):
                    pe.wait_ge(h_full, i - 1)
                dense8(None, RING[loc], bank[4 + i0 % 2], pre=8 if isinstance(i, int) and i == 0 else None,
                       lo_at=loc + 1 + 2 * (i - i0))

            def mlp_out_mm(i, i0, first=False, last=False):
                loc = b + o_local(i0)
                pe.wait_ge(lo_done, loc + 1 + 2 * (i - i0))
                pe.wait_ge(h_lo, i + 1)
                out_chunk(RING[loc], first, last)

            mlp_in_mm(0, 0)
            mlp_in_mm(1, 1)
            mlp_out_mm(0, 0, first=True)
            mlp_in_mm(2, 2)
            mlp_out_mm(1, 1)
            with pe.Fori(1, MLP_N // 2 - 1) as j:
                mlp_in_mm(2 * j + 1, 3)
                mlp_out_mm(2 * j, 2)
                mlp_in_mm(2 * j + 2, 4)
                mlp_out_mm(2 * j + 1, 3)
            mlp_in_mm(MLP_N - 1, MLP_N - 1)
            mlp_out_mm(MLP_N - 2, MLP_N - 2)
            mlp_out_mm(MLP_N - 1, MLP_N - 1, last=True)
            norm_sum(3)
            norm_sum(4)
            ada_reduce(1)

            def ffn(name, pre):
                b = START[name]
                hb = H_BASE[name]

                def gate_up(i, i0):
                    for q in range(2):
                        loc = b + (q if i0 == 0 else 3 * i0 - 1 + q)
                        if q == 0 and not (isinstance(i, int) and i == 0):
                            pe.wait_ge(h_full, hb + i)
                        dense8(None, RING[loc], bank[4 + q], pre=pre if i0 == 0 and q == 0 else None,
                               lo_at=loc + 1 + 3 * (i - i0))

                def down(i, i0, first=False, last=False):
                    loc = b + (3 * i0 + 4 if i0 < FFN_N - 1 else 3 * FFN_N - 1)
                    pe.wait_ge(lo_done, loc + 1 + 3 * (i - i0))
                    pe.wait_ge(h_lo, hb + i + 1)
                    out_chunk(RING[loc], first, last)

                gate_up(0, 0)
                gate_up(1, 1)
                down(0, 0, first=True)
                with pe.Fori(2, FFN_N) as i:
                    gate_up(i, 2)
                    down(i - 1, 1)
                if name == "ffn2":
                    pe.wait_ge(mods_done, 4)
                    ada_reduce(4)
                down(FFN_N - 1, FFN_N - 1, last=True)

            ffn("ffn0", 16)
            norm_sum(5)
            pe.wait_ge(mods_done, 2)
            ada_reduce(2)

            n = START["pool"]
            pe.wait_ge(lo_done, n + 1)
            for g in range(4):
                pe.wait_ge(pool_lo, g + 1)
                for m in range(2):
                    for k in range(2):
                        ins = mm3(bank[g][:, m * T:(m + 1) * T], v8(whi, RING[n])[:, 2 * g + k, m * P:(m + 1) * P],
                                  v8(wlo, RING[n])[:, 2 * g + k, m * P:(m + 1) * P], uhi[:, 2 * g + k, :],
                                  ulo[:, 2 * g + k, :], k == 0, k == 1)
                ins.then_inc(f_ready if g < 3 else pe_done, 1)
            norm_sum(6)
            ffn("ffn1", 24)
            norm_sum(7)
            pe.wait_ge(mods_done, 3)
            ada_reduce(3)

            def head_sums(r):
                for b in range(4):
                    pe.wait_ge(r_copy, 8 * r + 2 * b + 2)
                    nc.tensor.matmul(bank[b][:, :], ones, hroot[:, 2 * b:2 * b + 2, :], start=True,
                                     stop=True).then_inc(r_ss, 1)

            def swap_halves(r):
                for b in range(4):
                    pe.wait_ge(r_root, 4 * r + b + 1)
                    src = q2 if r else tmp2
                    nc.tensor.matmul(bank[b][:, :], const("swap"), src[:, 2 * b:2 * b + 2, :], start=True,
                                     stop=True).then_inc(r_swap, 1)

            b = START["kv"]
            for n in range(4):
                dense8(b + n, RING[b + n], bank[n], pre=32 if n == 0 else None)
            for n in range(4, 8):
                if n == 5:
                    head_sums(0)
                if n == 6:
                    swap_halves(0)
                pe.wait_ge(lo_done, b + n + 1)
                if n >= 6:
                    pe.wait_ge(v2_taken, n - 5)
                wh, wl = v8(whi, RING[b + n]), v8(wlo, RING[b + n])
                for t in range(2):
                    for k in range(KT):
                        ins = mm3(bank[4 + n % 2][:, t * T:(t + 1) * T], uhi[:, k, t * P:(t + 1) * P],
                                  ulo[:, k, t * P:(t + 1) * P], wh[:, k, :], wl[:, k, :], k == 0, k == KT - 1)
                ins.then_inc(pe_done, 1)
            pe.wait_ge(v2_taken, 4)
            pe.wait_ge(r_done, 4)
            ffn("ffn2", 40)
            norm_sum(8)

            b = START["wq"]
            for n in range(4):
                dense8(b + n, RING[b + n], bank[n], pre=48 if n == 0 else None)
            head_sums(1)
            swap_halves(1)

            def rotated(u):
                pe.wait_ge(r_done, 4 + u // 2 + 1)
                return q2[:, u, :]

            attention(8, NU, rotated, lambda u: k2[:, u, :],
                      lambda u, kt: v2[:, kt, u * P:(u + 1) * P],
                      lambda u: bank[u // 2][:, (u % 2) * T:(u % 2 + 1) * T],
                      lambda u: None, lambda u: True, lambda u: True)
            b = START["wo"]
            pe.wait_ge(o_lo, 8)
            for n in range(4):
                dense8(b + n, RING[b + n], bank[n])
            norm_sum(9)
            ffn("ffn3", 56)

            pe.wait_ge(x_ready, 36)
            for t in range(2):
                for k in range(KT):
                    ins = nc.tensor.transpose(bank[4 + 2 * t + k // 4][:, (k % 4) * P:(k % 4 + 1) * P],
                                              xT[:, k, t * P:(t + 1) * P], ident)
                    if k % 4 == 3:
                        ins.then_inc(out_turned, 1)

        @block.scalar
        def _(act):
            own = [0]

            def link(ins):
                own[0] += 1
                ins.then_inc(act_own, 1)
                act.wait_ge(act_own, own[0])

            def conv_at(pos, full_at, free_at):
                act.wait_ge(loaded[pos], full_at)
                if free_at is not None:
                    act.wait_ge(pe_done, free_at)
                nc.scalar.activation(whi[:, pos, :], raw[:, pos, :], ACT.Copy).then_inc(hi_done, 1)

            def conv(n):
                if n == len(RING):
                    return
                if n in QSLOTS:
                    act.wait_ge(loaded[RING[n]], filled(n))
                    if n > 2:
                        act.wait_ge(pe_done, 2)
                    nc.scalar.activation(split_views(whi, n), raw_view(n), ACT.Copy).then_inc(hi_done, 1)
                    return
                conv_at(RING[n], filled(n), before(n) or None)

            def square_x(e, version):
                for q in range(4):
                    act.wait_ge(x_ready, 4 * version - 3 + q)
                    nc.scalar.activation(full[:, 2 * q:2 * q + 2, :], xT[:, 2 * q:2 * q + 2, :],
                                         ACT.Square).then_inc(sq_ready, 1)

            def square_f(name):
                for q in range(4):
                    wait_bank(act, name, q)
                    nc.scalar.activation(full[:, 2 * q:2 * q + 2, :], bank[q][:], ACT.Square).then_inc(sq_ready, 1)

            def take_root(e):
                act.wait_ge(ss_done, e + 1)
                nc.scalar.activation(root[:], bank[6][:, 0:T], ACT.Sqrt, bias=eps[:], scale=1.0 / D).then_inc(root_done, 1)

            def split_u(p, free, shift=None):
                if free:
                    act.wait_ge(pe_done, free)
                for k in range(KT):
                    act.wait_ge(u_full, 8 * p + k + 1)
                    if shift is None:
                        nc.scalar.activation(uhi[:, k, :], full[:, k, :], ACT.Copy).then_inc(u_hi, 1)
                    else:
                        nc.scalar.activation(uhi[:, k, :], full[:, k, :], ACT.Identity,
                                             bias=shift[:, k:k + 1]).then_inc(u_hi, 1)

            def cload(dst, src):
                act.dma_start(dst, src).then_inc(consts_in, 16)

            for args in const_loads():
                cload(*args)
            act.wait_ge(x_ready, 4)
            square_x(0, 1)
            conv(0)
            take_root(0)
            split_u(0, 0)
            conv(1)
            conv(2)
            act.wait_ge(vec_done, 1)
            nc.scalar.activation(csilu[:], vec[:, VEC["c"]:VEC["c"] + 8], ACT.Silu).then_inc(c_ready, 1)

            for n in range(16):
                act.wait_ge(pe_done, {0: 2, 3: 5}.get(n, n + 1))
                o = bank[n % 6]
                if n in (0, 1):
                    ins = nc.scalar.activation(qn[:, 2 * n:2 * n + 2, :], o[:], ACT.Copy, scale=HD ** -0.5)
                elif n in (3, 4):
                    ins = nc.scalar.activation(qs[:, 2 * n - 6:2 * n - 4, :], o[:], ACT.Copy, scale=HD ** -0.5)
                elif n == 2:
                    ins = nc.scalar.activation(kvr, o[:], ACT.Copy)
                elif n in (5, 6, 7):
                    nc.scalar.activation(kT[:, n - 5, :], o[:, 0:T], ACT.Copy)
                    ins = nc.scalar.activation(vv[:, n - 5, :, :], o[:, T:2 * T], ACT.Copy)
                else:
                    ins = nc.scalar.activation(gates[:, 2 * n - 16:2 * n - 14, :], o[:], ACT.Sigmoid)
                ins.then_inc(in_taken, 1)
                conv(n + 3)
            act.wait_ge(gate_mm, 1)
            nc.scalar.activation(gate3[:], bank[6][:, 256:304], ACT.Sigmoid).then_inc(gate_done, 1)
            act.wait_ge(pe_done, 16)
            for a in range(2):
                act.wait_ge(blk_full, a + 1)
                nc.scalar.activation(bparts[a][0], blk[:, a, :], ACT.Copy).then_inc(blk_hi, 1)
            conv(START["cmp"] + 3)
            for a in range(2):
                act.wait_ge(pe_done, START["cmp"] + 2 * a + 2)
                nc.scalar.activation(hrow[:, a, :], bank[4 + a][0:30, 0:T], ACT.Gelu_apprx_tanh).then_inc(gelu_done, 1)
            act.wait_ge(h1_turned, 1)
            nc.scalar.activation(h1[:].rearrange("p a m c -> p (a m) c")[:, :, 0:30],
                                 bank[6][:, 0:P].rearrange("p (a c) -> p a c", a=4)[:, :, 0:30], ACT.Copy).then_inc(h1_done, 1)
            act.wait_ge(ckv_mm, 1)
            nc.scalar.activation(kcT[:, 0:NCMP], bank[4][:, 256:256 + NCMP], ACT.Copy)
            nc.scalar.activation(vcs[0:NCMP, :, :], bank[5][0:NCMP, 256:256 + 2 * HD], ACT.Copy).then_inc(ckv_done, 1)
            for n in range(3):
                conv(START["up"] + n)
            act.wait_ge(cs_dve, 2)
            nc.scalar.activation(cmpE[:, :, :, 0:NCMP], cmpE[:, :, :, 0:NCMP], ACT.Exp).then_inc(cs_exp, 1)
            act.wait_ge(cs_turned, 1)
            for q in range(4):
                nc.scalar.activation(pcT[:, 2 * q:2 * q + 2, :], bank[[2, 3, 6, 7][q]][0:NCMP, :],
                                     ACT.Copy).then_inc(cs_done, 1)

            def attention(count, base, sink_of):
                for u in range(count + 2):
                    if u < count:
                        w = base + u
                        act.wait_ge(s_max, w + 1)
                        sm = small[:, w % 3, :]
                        pr = prob[w % 3]
                        if sink_of(u) is not None:
                            for t in range(2):
                                nc.scalar.activation(sm[:, 4 + t:5 + t], sink_of(u), ACT.Exp, bias=sm[:, t:t + 1])
                        nc.scalar.activation(pr[:, 0:P], pr[:, 0:P], ACT.Exp, bias=sm[:, 0:1], accum_out=sm[:, 2:3])
                        nc.scalar.activation(pr[:, P:384], pr[:, P:384], ACT.Exp, bias=sm[:, 1:2],
                                             accum_out=sm[:, 3:4]).then_inc(s_exp, 1)
                    v = u - 2
                    if 0 <= v < count:
                        w = base + v
                        act.wait_ge(s_turned, w + 1)
                        if w >= 2:
                            act.wait_ge(s_pv, w - 1)
                        nc.scalar.activation(probT[w % 2], bank[6 + w % 2][:, 0:384], ACT.Copy).then_inc(s_copied, 1)

            attention(NU, 0, lambda u: sinks[:, units[u][1]:units[u][1] + 1] if units[u][0] == 2 else None)
            act.wait_ge(s_pv, NU)
            for q in range(4):
                nc.scalar.activation(uhi[:, 2 * q:2 * q + 2, :], bank[q][:], ACT.Copy).then_inc(o_hi, 1)

            for q in range(4):
                conv(START["up"] + 3 + q)
            act.wait_ge(pe_done, START["up"] + 4)
            for q in range(2):
                act.wait_ge(y_full, q + 1)
                nc.scalar.activation(uhi[:, 4 * q:4 * q + 4, :], full[:, 4 * q:4 * q + 4, :], ACT.Copy).then_inc(y_hi, 1)
            conv(START["out"] + 3)
            square_f("out")
            conv(START["mlp"])
            take_root(1)
            square_x(2, 2)
            conv(START["mlp"] + 1)
            take_root(2)
            split_u(1, START["out"] + 4)

            b = START["mlp"]

            def split_h(i, o_done, last=False):
                act.wait_ge(h_full, i + 1)
                if o_done is not None:
                    act.wait_ge(pe_done, o_done)
                nc.scalar.activation(uhi_flat[:, 0:512] if last else hhi, hfull, ACT.Copy).then_inc(h_hi, 1)

            def sub(i, i0, conv_in=True):
                act.wait_ge(pe_done, b + i_local(i0) + 1 + 2 * (i - i0))
                nc.scalar.activation(act_g, bank[4 + i0 % 2][:], ACT.Relu).then_inc(g_act, 1)
                if isinstance(i, int) and i == MLP_N - 1:
                    split_h(i, None, last=True)
                else:
                    split_h(i, b + o_local(i0 - 1) + 1 + 2 * (i - i0) if i0 > 0 else None)
                n = b + o_local(i0)
                conv_at(RING[n], filled(n) + 16 * (i - i0), before(n) + 2 * (i - i0))
                if conv_in:
                    n = b + i_local(i0 + 2)
                    conv_at(RING[n], filled(n) + 8 * (i - i0), before(n) + 2 * (i - i0))

            sub(0, 0)
            sub(1, 1)
            sub(2, 2)
            sub(3, 3)
            with act.Fori(2, MLP_N // 2 - 1) as j:
                sub(2 * j, 4)
                sub(2 * j + 1, 5)
            sub(MLP_N - 2, MLP_N - 2, conv_in=False)
            sub(MLP_N - 1, MLP_N - 1, conv_in=False)

            b0 = START["ffn0"]
            conv(b0)
            square_f("mlp")
            conv(b0 + 1)
            take_root(3)
            square_x(4, 3)
            take_root(4)
            split_u(2, b0, mods[:, 0, :])

            def ffn(name):
                b = START[name]
                hb = H_BASE[name]

                def evac(i, i0):
                    loc = b + (1 if i0 == 0 else 3 * i0)
                    act.wait_ge(pe_done, loc + 1 + 3 * (i - i0))
                    nc.scalar.activation(act_g, bank[4][:], ACT.Silu).then_inc(g_act, 1)

                def step(i, i0):
                    n = b + 3 * i0 - 1
                    conv_at(0, filled(n) + 16 * (i - i0), before(n) + 3 * (i - i0))
                    evac(i - 1, i0 - 1)
                    conv_at(1, filled(n + 1) + 16 * (i - i0), before(n + 1) + 3 * (i - i0))
                    split_h(hb + i - 1, before(n + 2) + 3 * (i - i0))
                    conv_at(2, filled(n + 2) + 16 * (i - i0), before(n + 2) + 3 * (i - i0))

                step(1, 1)
                step(2, 2)
                with act.Fori(3, FFN_N) as i:
                    step(i, 3)
                conv(b + 3 * FFN_N - 1)
                evac(FFN_N - 1, FFN_N - 1)
                split_h(hb + FFN_N - 1, None, last=True)
                conv(b + 3 * FFN_N)

            ffn("ffn0")
            n = START["pool"]
            conv(n + 1)
            square_x(5, 4)
            take_root(5)
            for g in range(4):
                act.wait_ge(pool_full, g + 1)
                nc.scalar.activation(uhi[:, 2 * g:2 * g + 2, :], full[:, 2 * g:2 * g + 2, :], ACT.Copy).then_inc(pool_hi, 1)
            square_x(6, 5)
            conv(n + 2)
            take_root(6)
            split_u(3, n + 1, mods[:, 6, :])
            ffn("ffn1")
            b = START["kv"]
            conv(b + 1)
            square_x(7, 6)
            take_root(7)
            split_u(4, b, mods[:, 18, :])
            conv(b + 2)

            def rotary(r, done, scalar, dst):
                for q in range(4):
                    act.wait_ge(pe_done, done - 3 + q)
                    nc.scalar.activation(dst[:, 2 * q:2 * q + 2, :], bank[q][:], ACT.Copy, scale=scalar).then_inc(r_copy, 1)
                    nc.scalar.activation(hroot[:, 2 * q:2 * q + 2, :], bank[q][:], ACT.Square).then_inc(r_copy, 1)
                    conv_next(r, q)

            def conv_next(r, q):
                n = (START["kv"] if r == 0 else START["wq"]) + 3 + q
                if r == 1 and q == 3:
                    return
                conv(n)

            def rotary_root(r):
                for q in range(4):
                    act.wait_ge(r_ss, 4 * r + q + 1)
                    nc.scalar.activation(hroot[:, 2 * q:2 * q + 2, :], bank[q][:], ACT.Sqrt, bias=eps[:],
                                         scale=1.0 / P).then_inc(r_root, 1)

            def take_v(n):
                act.wait_ge(pe_done, b + 5 + n)
                nc.scalar.activation(v2[:, :, 256 * n:256 * n + 256], bank[4 + n % 2][:], ACT.Copy).then_inc(v2_taken, 1)

            rotary(0, b + 4, vec[:, VEC["k_norm"]:VEC["k_norm"] + 1], tmp2)
            take_v(0)
            conv(b + 7)
            rotary_root(0)
            for n in range(1, 4):
                take_v(n)
            split_u(5, b + 8, mods[:, 9, :])
            conv(START["ffn2"])
            conv(START["ffn2"] + 1)
            act.wait_ge(r_done, 4)
            ffn("ffn2")
            b = START["wq"]
            conv(b + 1)
            square_x(8, 7)
            take_root(8)
            split_u(6, b, mods[:, 12, :])
            conv(b + 2)
            rotary(1, b + 4, scal[:, QSC, 0:1], q2)
            rotary_root(1)
            conv(b + 6)
            attention(8, NU, lambda u: None)
            act.wait_ge(s_pv, NU + 8)
            for q in range(4):
                nc.scalar.activation(uhi[:, 2 * q:2 * q + 2, :], bank[q][:], ACT.Copy).then_inc(o_hi, 1)
            conv(b + 7)
            b = START["ffn3"]
            square_x(9, 8)
            conv(b)
            conv(b + 1)
            take_root(9)
            split_u(7, b, mods[:, 15, :])
            ffn("ffn3")
            for t in range(2):
                for c in range(2):
                    act.wait_ge(out_turned, 2 * t + c + 1)
                    nc.scalar.activation(xin[:, t, c * 512:(c + 1) * 512], bank[4 + 2 * t + c][:],
                                         ACT.Copy).then_inc(out_copied, 1)

        @block.vector
        def _(dve):
            own = [0]

            def link(ins):
                own[0] += 1
                ins.then_inc(dve_own, 1)
                dve.wait_ge(dve_own, own[0])

            def conv_at(pos, hi_at):
                dve.wait_ge(hi_done, hi_at)
                nc.vector.tensor_tensor(wlo[:, pos, :], raw[:, pos, :], whi[:, pos, :].bitcast(F32),
                                        ALU.subtract).then_inc(lo_done, 1)

            def conv(n):
                if n == len(RING):
                    return
                if n in QSLOTS:
                    dve.wait_ge(hi_done, n + 1)
                    nc.vector.tensor_tensor(split_views(wlo, n), raw_view(n), split_views(whi, n).bitcast(F32),
                                            ALU.subtract).then_inc(lo_done, 1)
                    return
                conv_at(RING[n], n + 1)

            def ada_add(s, a, k, k0):
                w = len(ADA_SESSIONS[s])
                m = ADA_START[s] + k0 * w + a
                step = 0 if isinstance(k, int) else w
                buf = ADA_BUF[m]
                per = sum(1 for q in range(w) if q % 2 == buf)
                if step == 0:
                    dve.wait_ge(ada_loaded[buf], ada_filled(m))
                else:
                    dve.wait_ge(ada_loaded[buf], ada_filled(m) + 16 * per * (k - k0))
                if isinstance(k, int) and k == 0:
                    if s > 0:
                        dve.wait_ge(ada_sum, s)
                    nc.vector.tensor_scalar(acc[:, a, :], ada[:, buf, :], csilu[:, 0:1], None,
                                            ALU.mult).then_inc(ada_used, 1)
                    return
                dve.wait_ge(ada_used, ada_acc_before(m) + step * (k - k0))
                c = csilu[:, k:k + 1] if isinstance(k, int) else csilu[:, bass.ds(k, 1)]
                nc.vector.scalar_tensor_tensor(out=acc[:, a, :], in0=ada[:, buf, :], scalar=c, in1=acc[:, a, :],
                                               op0=ALU.mult, op1=ALU.add).then_inc(ada_used, 1)

            def take_mods(s):
                dve.wait_ge(ada_sum, s + 1)
                w = ADA_SESSIONS[s]
                for a, pair in enumerate(w):
                    for i, m in enumerate(PAIR_MODS[pair]):
                        c = 16 * a + 8 * i
                        ins = nc.vector.tensor_tensor(mods[:, m, :], bank[7][:, c:c + 8], adab[:, 8 * m:8 * m + 8], ALU.add)
                ins.then_inc(mods_done, 1)
                dve.wait_ge(mods_done, s + 1)

            def gain(i, m, g):
                link(nc.vector.scalar_tensor_tensor(out=scal[:, i, :], in0=mods[:, m, :], scalar=1.0, in1=g,
                                                    op0=ALU.add, op1=ALU.mult))

            def weight(i, m, w):
                link(nc.vector.tensor_scalar(scal[:, i, :], mods[:, m, :], 1.0, w, ALU.add, ALU.mult))

            def norm_g(layer, sub):
                a = VEC["norm_g"] + 8 * (3 * layer + sub)
                return vec[:, a:a + 8]

            def make_u(e, p, a, shift=None, turned=False):
                dve.wait_ge(root_done, e + 1)
                if not turned:
                    link(nc.vector.reciprocal(root[:], root[:]))
                if p > 0:
                    dve.wait_ge(u_lo, 8 * p)
                for kk in range(KT + 2):
                    if kk < KT:
                        nc.vector.scalar_tensor_tensor(out=full[:, kk, :], in0=xT[:, kk, :], scalar=a[:, kk:kk + 1],
                                                       in1=root[:], op0=ALU.mult, op1=ALU.mult).then_inc(u_full, 1)
                    k = kk - 2
                    if k < 0:
                        continue
                    dve.wait_ge(u_hi, 8 * p + k + 1)
                    if shift is None:
                        nc.vector.tensor_tensor(ulo[:, k, :], full[:, k, :], uhi[:, k, :].bitcast(F32),
                                                ALU.subtract).then_inc(u_lo, 1)
                    else:
                        nc.vector.scalar_tensor_tensor(out=ulo[:, k, :], in0=full[:, k, :], scalar=shift[:, k:k + 1],
                                                       in1=uhi[:, k, :].bitcast(F32), op0=ALU.add,
                                                       op1=ALU.subtract).then_inc(u_lo, 1)

            def add_normed(e, g, version):
                dve.wait_ge(root_done, e + 1)
                link(nc.vector.reciprocal(root[:], root[:]))
                for q in range(5):
                    if q < 4:
                        for k in (2 * q, 2 * q + 1):
                            ins = nc.vector.scalar_tensor_tensor(
                                out=full[:, k, :], in0=bank[k // 2][:, (k % 2) * T:(k % 2 + 1) * T],
                                scalar=g[:, k:k + 1], in1=root[:], op0=ALU.mult, op1=ALU.mult)
                        ins.then_inc(f_normed, 1)
                    if q > 0:
                        dve.wait_ge(f_normed, 4 * (version - 2) + q)
                        s = slice(2 * q - 2, 2 * q)
                        nc.vector.tensor_tensor(xT[:, s, :], xT[:, s, :], full[:, s, :], ALU.add).then_inc(x_ready, 1)
                dve.wait_ge(x_ready, 4 * version)

            def add_scaled(c, version, name):
                for k in range(KT):
                    if k % 2 == 0:
                        wait_bank(dve, name, k // 2)
                    ins = nc.vector.scalar_tensor_tensor(out=xT[:, k, :], in0=bank[k // 2][:, (k % 2) * T:(k % 2 + 1) * T],
                                                         scalar=c[:, k:k + 1], in1=xT[:, k, :], op0=ALU.mult, op1=ALU.add)
                    if k % 2:
                        ins.then_inc(x_ready, 1)
                dve.wait_ge(x_ready, 4 * version)

            nc.vector.memset(eps[:], EPS)
            for q in range(4):
                dve.wait_ge(x_turned, q + 1)
                nc.vector.tensor_copy(xT[:, 2 * q:2 * q + 2, :], bank[q][:]).then_inc(x_ready, 1)
            dve.wait_ge(vec_t, 1)
            nc.vector.tensor_copy(vec[:, 0:NVEC], bank[7][:, 384:384 + NVEC]).then_inc(vec_done, 1)
            conv(0)
            dve.wait_ge(x_ready, 4)
            dve.wait_ge(vec_done, 1)
            make_u(0, 0, vec[:, vrow("mix_pre")])
            conv(1)
            conv(2)
            dve.wait_ge(late_t, 1)
            nc.vector.tensor_copy(adab[:], bank[6][:, 128:288])
            nc.vector.tensor_copy(posx[:].rearrange("p a b -> p (a b)"), bank[6][:, 288:320]).then_inc(late_done, 1)
            dve.wait_ge(bvec_mm, 1)
            nc.vector.tensor_tensor(bvec, bank[7][0:16, 0:384], dmask, ALU.add).then_inc(bvec_done, 1)
            dve.wait_ge(c_ready, 1)
            for n in range(16):
                ada_add(0, n % 2, n // 2, n // 2)
                conv(n + 3)

            dve.wait_ge(kvx_in, 64)
            for a in range(2):
                entries = blk[:, a, :].rearrange("p (i g j) -> p i g j", i=16, g=2)
                for g in range(2):
                    tok = kvx[:, a, g, :].rearrange("p (j i r) -> p i j r", i=8, r=2)
                    for s in range(2):
                        ins = nc.vector.tensor_tensor(
                            entries[:, 8 * s:8 * s + 8, g, :], tok[:, :, s:s + NCMP, 0],
                            posx[:, a, 8 * s:8 * s + 8].unsqueeze(2).to_broadcast([P, 8, NCMP]), ALU.add)
                ins.then_inc(blk_full, 1)
            for a in range(2):
                dve.wait_ge(blk_hi, a + 1)
                nc.vector.tensor_tensor(bparts[a][1], blk[:, a, :], bparts[a][0].bitcast(F32), ALU.subtract).then_inc(blk_lo, 1)
            take_mods(0)
            gain(SA["ffn0"], 1, norm_g(0, 0))
            weight(SC["ffn0"], 2, 0.5)
            link(nc.vector.tensor_scalar(scal[:, QSC, 0:1], vec[:, VEC["q_norm"]:VEC["q_norm"] + 1], P ** -0.5, None, ALU.mult))
            conv(START["cmp"] + 3)
            for n in range(3):
                conv(START["up"] + n)

            E = cmpE[:, :, :, 0:NCMP]
            S = [cmpS[:, i, :].rearrange("p (t h) -> p t h", t=2) for i in range(3)]

            def over_blocks(a):
                return a.unsqueeze(3).to_broadcast([P, 2, 8, NCMP])

            dve.wait_ge(cs_mm, 1)
            mask = const("cmpmask").rearrange("p (t n) -> p t n", t=2)
            for t in range(2):
                for g in range(2):
                    sc = bank[4 + g][:, t * 64:(t + 1) * 64].rearrange("p (h n) -> p h n", h=4)[:, :, 0:NCMP]
                    ins = nc.vector.tensor_tensor(E[:, t, 4 * g:4 * g + 4, :], sc,
                                                  mask[:, t:t + 1, 0:NCMP].to_broadcast([P, 4, NCMP]), ALU.add)
            ins.then_inc(cs_dve, 1)
            dve.wait_ge(cs_dve, 1)
            link(nc.vector.tensor_reduce(S[0], E, AX.X, ALU.max))
            link(nc.vector.tensor_scalar(S[0], S[0], FLOOR, None, ALU.max))
            nc.vector.tensor_tensor(E, E, over_blocks(S[0]), ALU.subtract).then_inc(cs_dve, 1)
            dve.wait_ge(cs_exp, 1)
            link(nc.vector.tensor_reduce(S[1], E, AX.X, ALU.add))
            link(nc.vector.tensor_scalar(S[1], S[1], 1e-30, None, ALU.max))
            link(nc.vector.reciprocal(S[2], S[1]))
            dve.wait_ge(gate_done, 1)
            link(nc.vector.tensor_tensor(S[2], S[2], gate3[:].rearrange("p t (h c) -> p t h c", c=3)[:, :, :, 0], ALU.mult))
            nc.vector.tensor_tensor(E, E, over_blocks(S[2]), ALU.mult).then_inc(cs_prob, 1)

            def attention(count, base, bias_of, sink_of, gate_of):
                for u in range(count + 1):
                    if u < count:
                        w = base + u
                        sm = small[:, w % 3, :]
                        pr = prob[w % 3]
                        dve.wait_ge(s_mm, w + 1)
                        if w >= 3:
                            dve.wait_ge(s_turned, w - 2)
                        link(nc.vector.tensor_tensor(pr, bank[4 + w % 2][:, 0:384], bias_of(u), ALU.add))
                        nc.vector.tensor_reduce(sm[:, 6:7], pr[:, 0:P], AX.X, ALU.max)
                        link(nc.vector.tensor_reduce(sm[:, 7:8], pr[:, P:384], AX.X, ALU.max))
                        if sink_of(u) is not None:
                            link(nc.vector.tensor_tensor(sm[:, 6:8], sm[:, 6:8], sink_of(u).to_broadcast([P, 2]), ALU.max))
                        nc.vector.tensor_scalar(sm[:, 0:2], sm[:, 6:8], -1.0, None, ALU.mult).then_inc(s_max, 1)
                    v = u - 1
                    if 0 <= v < count:
                        w = base + v
                        sm = small[:, w % 3, :]
                        pr = prob[w % 3]
                        dve.wait_ge(s_exp, w + 1)
                        if sink_of(v) is not None:
                            link(nc.vector.tensor_tensor(sm[:, 2:4], sm[:, 2:4], sm[:, 4:6], ALU.add))
                        link(nc.vector.reciprocal(sm[:, 8:10], sm[:, 2:4]))
                        if gate_of(v) is not None:
                            link(nc.vector.tensor_tensor(sm[:, 8:10], sm[:, 8:10], gate_of(v), ALU.mult))
                        nc.vector.tensor_scalar(pr[:, 0:P], pr[:, 0:P], sm[:, 8:9], None, ALU.mult)
                        nc.vector.tensor_scalar(pr[:, P:384], pr[:, P:384], sm[:, 9:10], None, ALU.mult).then_inc(s_prob, 1)

            def split_o(done):
                for q in range(4):
                    dve.wait_ge(o_hi, done + q + 1)
                    s = slice(2 * q, 2 * q + 2)
                    nc.vector.tensor_tensor(ulo[:, s, :], bank[q][:].rearrange("p (a b) -> p a b", a=2),
                                            uhi[:, s, :].bitcast(F32), ALU.subtract).then_inc(o_lo, 1)

            dve.wait_ge(bias_in, 32)
            attention(NU, 0,
                      lambda u: bias[:, units[u][1] + (8 if units[u][0] == 2 else 0), :],
                      lambda u: sinks[:, units[u][1]:units[u][1] + 1] if units[u][0] == 2 else None,
                      lambda u: None if units[u][0] == 2 else gate3[:, :, 3 * units[u][1] + 1 + units[u][0]])
            split_o(0)

            for q in range(4):
                n = START["up"] + q
                dve.wait_ge(pe_done, n + 1)
                for m in range(2):
                    t = 4 * q + 2 * m
                    ins = nc.vector.tensor_tensor(gates[:, t:t + 2, :], gates[:, t:t + 2, :],
                                                  bank[[4, 6, 0, 2][q] + m][:].rearrange("p (a b) -> p a b", a=2), ALU.mult)
                ins.then_inc(y_taken, 1)
                conv(n + 3)
            dve.wait_ge(y_taken, 4)
            for q in range(2):
                s = slice(4 * q, 4 * q + 4)
                nc.vector.tensor_tensor(full[:, s, :], gates[:, s, :], gates[:, 8 + 4 * q:12 + 4 * q, :], ALU.add).then_inc(y_full, 1)
            for q in range(2):
                s = slice(4 * q, 4 * q + 4)
                dve.wait_ge(y_hi, q + 1)
                nc.vector.tensor_tensor(ulo[:, s, :], full[:, s, :], uhi[:, s, :].bitcast(F32), ALU.subtract).then_inc(y_lo, 1)
            conv(START["out"] + 3)
            conv(START["mlp"])
            add_normed(1, vec[:, vrow("mix_post")], 2)
            conv(START["mlp"] + 1)
            make_u(2, 1, vec[:, vrow("mlp_pre")])

            b = START["mlp"]

            def split_h(i, last=False):
                dve.wait_ge(h_hi, i + 1)
                hi, lo = (uhi_flat[:, 0:512], ulo_flat[:, 0:512]) if last else (hhi, hlo)
                nc.vector.tensor_tensor(lo, hfull, hi.bitcast(F32), ALU.subtract).then_inc(h_lo, 1)

            def sub(i, i0, piece, j, j0, conv_in=True):
                dve.wait_ge(g_act, i + 1)
                if not isinstance(i, int) or i > 0:
                    dve.wait_ge(h_lo, i)
                nc.vector.tensor_tensor(hfull, act_g, act_g, ALU.mult).then_inc(h_full, 1)
                split_h(i, last=isinstance(i, int) and i == MLP_N - 1)
                n = b + o_local(i0)
                conv_at(RING[n], n + 1 + 2 * (i - i0))
                ada_add(1, piece, j, j0)
                if conv_in:
                    n = b + i_local(i0 + 2)
                    conv_at(RING[n], n + 1 + 2 * (i - i0))

            def pair(j, j0, conv_in=True):
                sub(2 * j, 2 * j0, 0, j, j0, conv_in)
                sub(2 * j + 1, 2 * j0 + 1, 1, j, j0, conv_in)

            pair(0, 0)
            pair(1, 1)
            with dve.Fori(2, MLP_N // 2 - 1) as j:
                pair(j, 2)
            pair(MLP_N // 2 - 1, MLP_N // 2 - 1, conv_in=False)

            b0 = START["ffn0"]
            conv(b0)
            conv(b0 + 1)
            add_normed(3, vec[:, vrow("mlp_post")], 3)
            make_u(4, 2, scal[:, SA["ffn0"], :], mods[:, 0, :])
            take_mods(1)
            gain(SA["pool"], 4, norm_g(0, 1))
            link(nc.vector.scalar_tensor_tensor(out=scal[:, SC["pool"], :], in0=mods[:, 5, :], scalar=1.0,
                                                in1=vec[:, vrow("pool_scale")], op0=ALU.add, op1=ALU.mult))
            gain(SA["ffn1"], 7, norm_g(0, 2))

            def ffn(name):
                b = START[name]
                hb = H_BASE[name]
                s = SESSION[name]

                def times_up(i):
                    dve.wait_ge(g_act, hb + i + 1)
                    dve.wait_ge(h_lo, hb + i)
                    nc.vector.tensor_tensor(hfull, act_g, bank[5][:], ALU.mult).then_inc(h_full, 1)

                def step(i, i0, with_ada):
                    n = b + 3 * i0 - 1
                    conv_at(0, n + 1 + 3 * (i - i0))
                    if with_ada:
                        ada_add(s, 0, i - 1, i0 - 1)
                    times_up(i - 1)
                    conv_at(1, n + 2 + 3 * (i - i0))
                    split_h(hb + i - 1)
                    conv_at(2, n + 3 + 3 * (i - i0))
                    if with_ada and len(ADA_SESSIONS[s]) > 1:
                        ada_add(s, 1, i - 1, i0 - 1)

                step(1, 1, s is not None)
                step(2, 2, s is not None)
                with dve.Fori(3, KT + 1) as i:
                    step(i, 3, s is not None)
                with dve.Fori(KT + 1, FFN_N) as i:
                    step(i, KT + 1, False)
                conv(b + 3 * FFN_N - 1)
                times_up(FFN_N - 1)
                split_h(hb + FFN_N - 1, last=True)
                conv(b + 3 * FFN_N)

            ffn("ffn0")
            n = START["pool"]
            conv(n + 1)
            add_scaled(scal[:, SC["ffn0"], :], 4, "ffn0")
            nc.vector.memset(pool_a[:, :, 0:16], 0.0)
            nc.vector.memset(pool_b[:, :, 0:16], 0.0)
            dve.wait_ge(root_done, 6)
            link(nc.vector.reciprocal(root[:], root[:]))
            for k in range(KT):
                ins = nc.vector.scalar_tensor_tensor(out=full[:, k, :], in0=xT[:, k, :], scalar=scal[:, SA["pool"], k:k + 1],
                                                     in1=root[:], op0=ALU.mult, op1=ALU.mult)
            link(ins)
            for k in range(KT):
                nc.vector.tensor_scalar(pool_a[:, k, 16:], full[:, k, :], mods[:, 3, k:k + 1], None, ALU.add)
                ins = nc.vector.tensor_scalar(full[:, k, :], full[:, k, :], mods[:, 3, k:k + 1], None, ALU.add)
            link(ins)
            src, dst = pool_a, pool_b
            for g in range(4):
                s = 1 << g
                link(nc.vector.tensor_tensor(dst[:, 2 * g:, 16:], src[:, 2 * g:, 16:], src[:, 2 * g:, 16 - s:272 - s], ALU.add))
                own_tiles = dst[:, 2 * g:2 * g + 2, 16:]
                rc = const("poolrc")[:, g * 16:(g + 1) * 16].unsqueeze(1).to_broadcast([P, 2, 16])
                h = full[:, 2 * g:2 * g + 2, :]
                spare = src[:, 2 * g:2 * g + 2, 16:32]
                link(nc.vector.tensor_tensor(spare, own_tiles[:, :, 0:16], rc, ALU.mult))
                nc.vector.tensor_tensor(h[:, :, 0:16], spare, h[:, :, 0:16], ALU.subtract)
                nc.vector.scalar_tensor_tensor(out=h[:, :, 16:], in0=own_tiles[:, :, 16:], scalar=0.5 / s, in1=h[:, :, 16:],
                                               op0=ALU.mult, op1=ALU.subtract).then_inc(pool_full, 1)
                src, dst = dst, src
            for g in range(4):
                s = slice(2 * g, 2 * g + 2)
                dve.wait_ge(pool_hi, g + 1)
                nc.vector.tensor_tensor(ulo[:, s, :], full[:, s, :], uhi[:, s, :].bitcast(F32), ALU.subtract).then_inc(pool_lo, 1)
            add_scaled(scal[:, SC["pool"], :], 5, "pool")
            conv(n + 2)
            make_u(6, 3, scal[:, SA["ffn1"], :], mods[:, 6, :])
            take_mods(2)
            weight(SC["ffn1"], 8, 0.5)
            weight(SC["ffn3"], 17, 0.5)
            gain(SA["kv"], 19, vec[:, vrow("kv_norm")])
            ffn("ffn1")
            b = START["kv"]
            conv(b + 1)
            add_scaled(scal[:, SC["ffn1"], :], 6, "ffn1")
            make_u(7, 4, scal[:, SA["kv"], :], mods[:, 18, :])
            conv(b + 2)

            cos = const("cos").unsqueeze(1).to_broadcast([P, 2, T])
            sin = const("sin").unsqueeze(1).to_broadcast([P, 2, T])

            def rotary(r, src, turned, dst):
                for q in range(4):
                    s = slice(2 * q, 2 * q + 2)
                    dve.wait_ge(r_root, 4 * r + q + 1)
                    dve.wait_ge(r_swap, 4 * r + q + 1)
                    nc.vector.reciprocal(hroot[:, s, :], hroot[:, s, :])
                    nc.vector.tensor_tensor(src[:, s, :], src[:, s, :], cos, ALU.mult)
                    link(nc.vector.tensor_tensor(turned[:, s, :], bank[q][:].rearrange("p (a b) -> p a b", a=2), sin, ALU.mult))
                    link(nc.vector.tensor_tensor(dst[:, s, :], src[:, s, :], turned[:, s, :], ALU.add))
                    nc.vector.tensor_tensor(dst[:, s, :], dst[:, s, :], hroot[:, s, :], ALU.mult).then_inc(r_done, 1)
                dve.wait_ge(r_done, 4 * r + 4)

            for q in range(5):
                conv(b + 3 + q)
            take_mods(3)
            gain(SA["ffn2"], 10, norm_g(1, 0))
            weight(SC["ffn2"], 11, 0.5)
            rotary(0, tmp2, k2, k2)
            make_u(7, 5, scal[:, SA["ffn2"], :], mods[:, 9, :], turned=True)
            conv(START["ffn2"])
            conv(START["ffn2"] + 1)
            ffn("ffn2")
            b = START["wq"]
            conv(b + 1)
            take_mods(4)
            gain(SA["moba"], 13, norm_g(1, 1))
            add_scaled(scal[:, SC["ffn2"], :], 7, "ffn2")
            make_u(8, 6, scal[:, SA["moba"], :], mods[:, 12, :])
            conv(b + 2)
            for q in range(3):
                conv(b + 3 + q)
            weight(SC["moba"], 14, 1.0)
            gain(SA["ffn3"], 16, norm_g(1, 2))
            rotary(1, q2, tmp2, q2)
            conv(b + 6)
            attention(8, NU, lambda u: const("causal"), lambda u: None, lambda u: None)
            split_o(4)
            conv(b + 7)
            b = START["ffn3"]
            add_scaled(scal[:, SC["moba"], :], 8, "wo")
            conv(b)
            conv(b + 1)
            make_u(9, 7, scal[:, SA["ffn3"], :], mods[:, 15, :])
            ffn("ffn3")
            add_scaled(scal[:, SC["ffn3"], :], 9, "ffn3")


def kernel(**inputs):
    import concourse.bacc as bacc
    from concourse.bass_utils import run_bass_kernel_spmd

    nc = bacc.Bacc("TRN2", target_bir_lowering=False, num_devices=1)
    tables = dict(zip(("table_cst", "table_onehot", "table_mask"), shape_constants()))
    arrays, aps = {}, {}
    for name in NAMES:
        a = np.ascontiguousarray(inputs[name])
        arrays["in_" + name] = a
        aps[name] = nc.dram_tensor("in_" + name, a.shape, mybir.dt.from_np(a.dtype), kind="ExternalInput").ap()
    tabs = []
    for name, a in tables.items():
        arrays[name] = a
        tabs.append(nc.dram_tensor(name, a.shape, F32, kind="ExternalInput").ap())
    bias_rows = nc.dram_tensor("bias_rows", (P, 16, 384), F32, kind="Internal").ap()
    out = nc.dram_tensor("out_0", (1, T, D), F32, kind="ExternalOutput").ap()
    build(nc, aps, *tabs, bias_rows, out)
    r = run_bass_kernel_spmd(nc, [arrays], core_ids=[0])
    return r.results[0]["out_0"]
```

```python
from contextlib import ExitStack
import math

import numpy as np

import concourse.bass as bass
from concourse import mybir

F32 = mybir.dt.float32
F32R = mybir.dt.float32r
ALU = mybir.AluOpType
ACT = mybir.ActivationFunctionType
AX = mybir.AxisListType

P = 128
T = 256
D = 1024
KT = D // P
HD = 64
NH = 8
NCMP = 15
FF = 4096
FF2 = 2816
SLOT = 2048
NEG = -1.0e30
FLOOR = -1.0e29
EPS = 1e-6
NMOD = 20

MLP_N = FF // 256
FFN_N = FF2 // 256


def plan_slots():
    start, ring = {}, []

    def phase(name, positions):
        start[name] = len(ring)
        ring.extend(positions)

    phase("in", [n % 3 for n in range(8)])
    phase("cmp", [2, 0, 1, 2])
    phase("gate", [n % 3 for n in range(8)])
    phase("up", [2, 0, 1, 2])
    phase("out", [0, 1, 2, 1])
    order = [0, 2]
    for i in range(MLP_N):
        order.append(1 if i < MLP_N - 1 else 0)
        if i + 2 < MLP_N:
            order.append(0 if i % 2 == 0 else 2)
    phase("mlp", order)
    ffn = [0, 1, 2] * (FFN_N - 1) + [0]
    phase("ffn0", [1, 2] + ffn)
    phase("pool", [1])
    phase("ffn1", [2, 1] + ffn)
    phase("kv", [1, 2, 0, 1, 2, 0, 1, 2])
    phase("ffn2", [1, 2] + ffn)
    phase("wq", [1, 2, 0, 1])
    phase("wo", [2, 0, 1, 0])
    phase("ffn3", [1, 2] + ffn)
    return start, ring


START, RING = plan_slots()


def before(n):
    for m in range(n - 1, -1, -1):
        if RING[m] == RING[n]:
            return m + 1
    return 0


def filled(n):
    return sum(32 if 0 <= m - START["up"] < 4 else 16 for m in range(n + 1) if RING[m] == RING[n])


ADA_SESSIONS = [[0, 1], [2, 3], [4, 5], [6, 7], [8, 9]]
ADA_BUF = []
ADA_ACC = []
ADA_START = []
for _s in ADA_SESSIONS:
    ADA_START.append(len(ADA_BUF))
    for _k in range(KT):
        for _a in range(len(_s)):
            ADA_BUF.append(_a % 2)
            ADA_ACC.append(_a)
PAIR_MODS = [(0, 1), (2, 3), (4, 5), (6, 7), (8, 17), (18, 19), (9, 10), (11, 12), (13, 14), (15, 16)]


def ada_before(m):
    for q in range(m - 1, -1, -1):
        if ADA_BUF[q] == ADA_BUF[m]:
            return q + 1
    return 0


def ada_filled(m):
    return 16 * sum(1 for q in range(m + 1) if ADA_BUF[q] == ADA_BUF[m])


def ada_acc_before(m):
    for q in range(m - 1, -1, -1):
        if ADA_ACC[q] == ADA_ACC[m]:
            return q + 1
    return 0


VEC = {"mix_pre": 0, "mix_post": 8, "mlp_pre": 16, "mlp_post": 24, "norm_g": 32, "pool_scale": 80,
       "kv_norm": 88, "c": 96, "k_norm": 104, "q_norm": 105}
NVEC = 106

CST = {}
_at = 0
for _n, _w in (("ident", 128), ("ones", 128), ("swap", 128), ("causal", 256), ("cmpmask", 32), ("poolrc", 64),
               ("cos", 256), ("sin", 256)):
    CST[_n] = (_at, _at + _w)
    _at += _w
NCST = _at


def shape_constants():
    c = np.zeros((P, NCST), np.float32)

    def put(name, a):
        lo, hi = CST[name]
        c[:, lo:hi] = a.reshape(P, hi - lo)

    q = np.arange(P)[:, None]
    put("ident", np.eye(P, dtype=np.float32))
    put("ones", np.ones((P, P), np.float32))
    put("swap", np.eye(P, dtype=np.float32)[:, (np.arange(P) + 64) % P])
    second = np.where(P + q - np.arange(T)[None] >= 0, 0.0, NEG)
    put("causal", second.astype(np.float32))
    inv = (10000.0 ** (-(np.arange(0, P, 2) / float(P)))).astype(np.float32)
    ang = np.arange(T, dtype=np.float32)[:, None] * inv[None, :]
    cos, sin = np.cos(ang).T, np.sin(ang).T
    put("cos", np.concatenate([cos, cos], 0))
    put("sin", np.concatenate([-sin, sin], 0))
    end = np.arange(NCMP) * 16 + 31
    m = np.full((P, 2, 16), NEG, np.float32)
    for t in range(2):
        m[:, t, :NCMP] = np.where(end[None] <= t * P + q, 0.0, NEG)
    put("cmpmask", m)
    rc = np.stack([1.0 / np.minimum(np.arange(16) + 1, w) for w in (2, 4, 8, 16)]).astype(np.float32)
    put("poolrc", np.broadcast_to(rc[None], (P, 4, 16)))
    dist = 255 - np.arange(384)
    d = np.maximum(dist, 0)
    df = np.maximum(d, 1).astype(np.float32)
    large = 16 + (np.log(df / np.float32(16)) / np.float32(math.log(64)) * np.float32(16)).astype(np.int32)
    bucket = np.where(d < 16, d, np.minimum(large, 31))
    onehot = (bucket[None] == np.arange(32)[:, None]).astype(np.float32)
    mask = np.zeros((16, 384), np.float32)
    mask[:8] = np.where(dist < 0, NEG, 0.0)
    mask[8:] = np.where((dist < 0) | (dist >= 128), NEG, 0.0)
    return c, onehot, mask


NAMES = ["x", "norm_mix_pre", "norm_mix_post", "norm_mlp_pre", "norm_mlp_post", "w_in", "cmp_pos_k", "cmp_w1_k",
         "cmp_w2_k", "cmp_pos_v", "cmp_w1_v", "cmp_w2_v", "attn_sinks", "rel_bias", "w_up_nsa", "w_up_swa",
         "w_out", "w_mlp_in", "w_mlp_out", "c_2", "ada_w_2", "ada_b_2", "norm_g_2", "ffn_w_in_2", "ffn_w_out_2",
         "pool_w_2", "pool_scale_2", "kv_norm_2", "kv_ada_w_2", "kv_ada_b_2", "w_kv_2", "k_norm_2", "w_q_2",
         "q_norm_2", "w_o_2"]


def build(nc, A, cst_dram, onehot_dram, dmask_dram, bias_dram, out):
    with ExitStack() as ctx:
        def sb(name, shape, dt=F32):
            return ctx.enter_context(nc.sbuf_tensor(name, shape, dt))

        def sem(name):
            return ctx.enter_context(nc.semaphore(name))

        raw = sb("raw", [P, 3, SLOT])
        whi = sb("whi", [P, 3, SLOT], F32R)
        wlo = sb("wlo", [P, 3, SLOT], F32R)
        ada = sb("ada", [P, 2, SLOT])
        acc = sb("acc", [P, 3, SLOT])
        xT = sb("xT", [P, KT, T])
        full = sb("full", [P, KT, T])
        uhi = sb("uhi", [P, KT, T], F32R)
        ulo = sb("ulo", [P, KT, T], F32R)
        cst = sb("cst", [P, NCST])
        wide = sb("wide", [P, 4352])
        arena = sb("arena", [P, 5632])
        mix = sb("mix", [P, 2048])
        hsplit = sb("hsplit", [P, 1060], F32R)
        vec = sb("vec", [P, 112])
        adab = sb("adab", [P, NMOD * KT])
        mods = sb("mods", [P, NMOD, KT])
        scal = sb("scal", [P, 16, KT])
        csilu = sb("csilu", [P, KT])
        root = sb("root", [P, T])
        eps = sb("eps", [P, 1])
        sinks = sb("sinks", [P, 8])
        small = sb("small", [P, 3, 16])
        gate3 = sb("gate3", [P, 2, 24])
        wg = sb("wg", [P, KT, 24])
        posx = sb("posx", [P, 2, 16])
        h1 = sb("h1", [P, 2, 2, 32])
        kcT = sb("kcT", [P, 16])
        cmpS = sb("cmpS", [P, 3, 16])

        bank = [ctx.enter_context(nc.psum_tensor(f"bank{i}", [P, 512], F32)) for i in range(8)]

        def const(name):
            return cst[:, CST[name][0]:CST[name][1]]

        ident, ones = const("ident"), const("ones")
        SA = {"ffn0": 0, "pool": 1, "ffn1": 2, "kv": 3, "ffn2": 4, "moba": 5, "ffn3": 6}
        SC = {"ffn0": 7, "pool": 8, "ffn1": 9, "ffn2": 10, "moba": 11, "ffn3": 12}
        QSC = 13
        NEG_SHIFT = 14

        def cols(buf, a, *dims):
            n = int(np.prod(dims))
            v = buf[:, a:a + n]
            if len(dims) == 2:
                return v.rearrange("p (a b) -> p a b", a=dims[0])
            if len(dims) == 3:
                return v.rearrange("p (a b c) -> p a b c", a=dims[0], b=dims[1])
            return v

        gates = cols(wide, 0, 16, T)
        qn = cols(arena, 0, 4, T)
        qs = cols(arena, 1024, 4, T)
        o_swa = qs
        kT = cols(arena, 2048, 3, T)
        vv = cols(arena, 2816, 3, 2, P)
        kvr = cols(arena, 3584, 2, T)
        kvx = cols(arena, 4096, 2, 2, T)
        vcs = arena[0:16, 5120:5248].rearrange("p (g d) -> p g d", g=2)
        w2 = cols(arena, 5248, 2, 2, HD)
        cmpE = cols(wide, 4096, 2, 8, 16)
        blk = cols(mix, 0, 2, 480)
        uhi_flat = uhi[:].rearrange("p a b -> p (a b)")
        ulo_flat = ulo[:].rearrange("p a b -> p (a b)")
        bpart_hi, bpart_lo = hsplit[:, 0:480], hsplit[:, 480:960]
        hrow = cols(mix, 1024, 2, T)[0:30]
        vrows = cols(mix, 0, 4, P)
        onehot = mix[0:32, 512:896]
        dmask = mix[0:16, 896:1280]
        relb = mix[0:32, 1280:1296]
        bvec = mix[0:16, 1600:1984]
        bias_nsa = cols(acc[:, 2, :], 0, NH, T)
        bias_swa = [cols(arena, 3584, 6, T), cols(cst, CST["cos"][0], 2, T)]
        prob = [mix[:, 384 * i:384 * i + 384] for i in range(3)]
        probT = [mix[:, 1152 + 384 * i:1536 + 384 * i] for i in range(2)]
        pcT = full[0:NCMP, :, :]
        act_g = mix[:, 0:512]
        hfull = mix[:, 512:1024]
        hhi, hlo = hsplit[:, 0:512], hsplit[:, 512:1024]
        pool_a = cols(wide, 0, KT, 272)
        pool_b = cols(arena, 0, KT, 272)
        k2 = cols(wide, 0, KT, T)
        v2 = cols(wide, 2048, 2, D)
        q2 = cols(arena, 0, KT, T)
        tmp2 = cols(arena, 2048, KT, T)
        hroot = cols(mix, 0, KT, T)
        xin = full[:].rearrange("p a b -> p (a b)").rearrange("p (t d) -> p t d", t=2)

        loaded = [sem(f"loaded{i}") for i in range(3)]
        ada_loaded = [sem(f"ada_loaded{i}") for i in range(2)]
        consts_in = sem("consts_in")
        x_in = sem("x_in")
        cst_in = sem("cst_in")
        late_in = sem("late_in")
        late_t = sem("late_t")
        f_ready = sem("f_ready")
        hi_done = sem("hi_done")
        lo_done = sem("lo_done")
        pe_done = sem("pe_done")
        ada_used = sem("ada_used")
        ada_sum = sem("ada_sum")
        mods_done = sem("mods_done")
        vec_t = sem("vec_t")
        vec_done = sem("vec_done")
        late_done = sem("late_done")
        c_ready = sem("c_ready")
        x_turned = sem("x_turned")
        x_ready = sem("x_ready")
        sq_ready = sem("sq_ready")
        ss_done = sem("ss_done")
        root_done = sem("root_done")
        f_normed = sem("f_normed")
        u_full = sem("u_full")
        u_hi = sem("u_hi")
        u_lo = sem("u_lo")
        in_taken = sem("in_taken")
        kvx_in = sem("kvx_in")
        gate_mm = sem("gate_mm")
        gate_done = sem("gate_done")
        blk_full = sem("blk_full")
        blk_hi = sem("blk_hi")
        blk_lo = sem("blk_lo")
        gelu_done = sem("gelu_done")
        h1_turned = sem("h1_turned")
        h1_done = sem("h1_done")
        ckv_mm = sem("ckv_mm")
        ckv_done = sem("ckv_done")
        bvec_mm = sem("bvec_mm")
        bvec_done = sem("bvec_done")
        bvec_out = sem("bvec_out")
        bias_in = sem("bias_in")
        parts_clear = sem("parts_clear")
        rotary_in = sem("rotary_in")
        mix_pre_in = sem("mix_pre_in")
        mix_pre_t = sem("mix_pre_t")
        mix_pre_done = sem("mix_pre_done")
        cs_mm = sem("cs_mm")
        cs_dve = sem("cs_dve")
        cs_exp = sem("cs_exp")
        cs_prob = sem("cs_prob")
        cs_turned = sem("cs_turned")
        cs_done = sem("cs_done")
        s_mm = sem("s_mm")
        s_max = sem("s_max")
        s_exp = sem("s_exp")
        s_prob = sem("s_prob")
        s_turned = sem("s_turned")
        s_copied = sem("s_copied")
        s_pv = sem("s_pv")
        o_taken = sem("o_taken")
        gates_ready = sem("gates_ready")
        o_hi = sem("o_hi")
        o_lo = sem("o_lo")
        y_taken = sem("y_taken")
        y_full = sem("y_full")
        y_hi = sem("y_hi")
        y_lo = sem("y_lo")
        g_act = sem("g_act")
        h_full = sem("h_full")
        h_hi = sem("h_hi")
        h_lo = sem("h_lo")
        pool_normed = sem("pool_normed")
        pool_shifted = sem("pool_shifted")
        pool_full = sem("pool_full")
        pool_hi = sem("pool_hi")
        pool_lo = sem("pool_lo")
        v2_taken = sem("v2_taken")
        r_copy = sem("r_copy")
        r_ss = sem("r_ss")
        r_root = sem("r_root")
        r_swap = sem("r_swap")
        r_done = sem("r_done")
        out_turned = sem("out_turned")
        out_copied = sem("out_copied")
        out_dma = sem("out_dma")
        dve_own = sem("dve_own")
        act_own = sem("act_own")

        block = ctx.enter_context(nc.Block())

        def v8(buf, p):
            return buf[:, p, :].rearrange("p (k c) -> p k c", k=8)

        def pair_view(buf, p):
            return buf[:, p:p + 2, :].rearrange("p a b -> p (a b)").rearrange("p (k g d) -> p k g d", g=2, d=HD)

        QSLOTS = {0: (0, 0), 1: (0, 1), 3: (0, 0), 4: (0, 1)}

        def split_views(buf, n):
            if n in QSLOTS:
                return pair_view(buf, QSLOTS[n][0])[:, :, QSLOTS[n][1], :]
            return buf[:, RING[n], :]

        def raw_view(n):
            return raw[:, RING[n], :].rearrange("p (k d) -> p k d", d=HD) if n in QSLOTS else raw[:, RING[n], :]

        def v4(buf, p):
            return buf[:, p, :].rearrange("p (k c) -> p k c", k=4)

        def v2k(buf, p):
            return buf[:, p, :].rearrange("p (k c) -> p k c", k=2)

        def vrow(name):
            return slice(VEC[name], VEC[name] + 8)

        def const_loads():
            for name, key in (("mix_pre", "norm_mix_pre"), ("mix_post", "norm_mix_post"), ("mlp_pre", "norm_mlp_pre"),
                              ("mlp_post", "norm_mlp_post"), ("pool_scale", "pool_scale_2"), ("c", "c_2")):
                yield vrows[vrow(name), 0, :], A[key][0].rearrange("(r c) -> r c", c=P)
            yield vrows[32:80, 0, :], A["norm_g_2"].rearrange("l s (r c) -> (l s r) c", c=P)
            yield vrows[vrow("kv_norm"), 0, :], A["kv_norm_2"].rearrange("(r c) -> r c", c=P)
            yield vrows[104:105, 0, :], A["k_norm_2"].rearrange("(r c) -> r c", c=P)
            yield vrows[105:106, 0, :], A["q_norm_2"]

        def late_loads():
            ada_rows = A["ada_b_2"].rearrange("l (r c) -> (l r) c", c=P)
            yield vrows[0:80, 1, :], ada_rows[0:80]
            yield vrows[0:64, 2, :], ada_rows[80:144]
            yield vrows[64:80, 2, :], A["kv_ada_b_2"].rearrange("(r c) -> r c", c=P)
            yield vrows[0:16, 3, :], A["cmp_pos_k"][0].rearrange("(r i) d -> r (i d)", i=2)
            yield vrows[16:32, 3, :], A["cmp_pos_v"][0].rearrange("(r i) d -> r (i d)", i=2)
            yield relb, A["rel_bias"]
            yield onehot, onehot_dram
            yield dmask, dmask_dram
            yield wg[:], A["w_in"][0].rearrange("(k p) c -> p k c", p=P)[:, :, 1280:1304]
            yield w2[:, 0], A["cmp_w2_k"][0].rearrange("(m p) d -> p m d", p=P)
            yield w2[:, 1], A["cmp_w2_v"][0].rearrange("(m p) d -> p m d", p=P)
            yield sinks[:], A["attn_sinks"].partition_broadcast(P).rearrange("p a h -> p (a h)")

        N_CONSTS, N_LATE = len(list(const_loads())), len(list(late_loads()))

        ffn_phase = [("ffn0", 0, 0), ("ffn1", 0, 1), ("ffn2", 1, 0), ("ffn3", 1, 1)]
        units = [(2, t + 4 * g) for t in range(4) for g in range(2)]
        units += [(b, t + 4 * g) for t in range(4) for g in range(2) for b in (0, 1)]
        NU = len(units)
        GATE_STEPS = {5: (2, 4, 6, 8), 6: (10, 12, 14, 16), 7: (18, 20, 22, 24)}
        GATE_TAKEN = {j: at[-1] + 1 for j, at in GATE_STEPS.items()}
        GATE_BANK = {4: 0, 5: 1, 6: 1, 7: 2}
        SLIDING_TAKEN = 12
        H_BASE = {"mlp": 0, "ffn0": MLP_N, "ffn1": MLP_N + FFN_N, "ffn2": MLP_N + 2 * FFN_N, "ffn3": MLP_N + 3 * FFN_N}
        SESSION = {"in": 0, "mlp": 1, "ffn0": 2, "ffn1": 3, "ffn2": 4, "ffn3": None}

        def o_local(i):
            return 2 * i + 2 if not isinstance(i, int) or i < MLP_N - 1 else 2 * MLP_N - 1

        def i_local(i):
            return 2 * i - 1 if not isinstance(i, int) or i > 0 else 0

        CHUNKED = ["mlp", "ffn0", "pool", "ffn1", "ffn2", "ffn3"]

        def end_of(name):
            return START[name] + {"mlp": 2 * MLP_N, "pool": 1, "out": 4, "wo": 4}.get(name, 3 * FFN_N)

        def wait_bank(eng, name, q):
            if name in CHUNKED and q < 3:
                eng.wait_ge(f_ready, 3 * CHUNKED.index(name) + q + 1)
            else:
                eng.wait_ge(pe_done, end_of(name) if name in CHUNKED else START[name] + q + 1)

        @block.sync
        def _(sp):
            def load(n, pos, free, dst_view, src):
                if free is not None:
                    sp.wait_ge(lo_done, free)
                sp.dma_start(dst_view, src).then_inc(loaded[pos], 16)

            def slot(n, view, src):
                load(n, RING[n], before(n) or None, view(raw, RING[n]), src)

            def ada_src(pair, k):
                rows = bass.ds(k * P, P) if not isinstance(k, int) else slice(k * P, k * P + P)
                if pair == 4:
                    return A["ada_w_2"][:, rows, 8 * D:9 * D].rearrange("l p c -> p l c")
                if pair == 5:
                    return A["kv_ada_w_2"][rows, :].rearrange("p (a c) -> p a c", a=2)
                layer, at = (0, pair) if pair < 4 else (1, pair - 6)
                return A["ada_w_2"][layer, rows, 2 * at * D:2 * (at + 1) * D].rearrange("p (a c) -> p a c", a=2)

            def ada_load(s, a, k, k0):
                w = len(ADA_SESSIONS[s])
                m = ADA_START[s] + k0 * w + a
                free = ada_before(m)
                step = 0 if isinstance(k, int) else w
                if free:
                    sp.wait_ge(ada_used, free + step * (k - k0))
                sp.dma_start(ada[:, ADA_BUF[m], :].rearrange("p (a c) -> p a c", a=2),
                             ada_src(ADA_SESSIONS[s][a], k)).then_inc(ada_loaded[ADA_BUF[m]], 16)

            w_in = A["w_in"][0].rearrange("(k p) c -> p k c", p=P)
            q1, q2_ = 1304, 2072
            starts = [0, 256, 512, q1, q1 + 256, 768, 1024, q1 + 512] + [q2_ + 256 * j for j in range(8)]
            sp.dma_start(xin, A["x"][0].rearrange("(t p) d -> p t d", p=P)).then_inc(x_in, 16)
            sp.dma_start(cst[:, 0:CST["cos"][0]], cst_dram[:, 0:CST["cos"][0]]).then_inc(cst_in, 16)
            w1 = [A[name][0].rearrange("(s k p) c -> s p k c", p=P, k=8) for name in ("cmp_w1_k", "cmp_w1_v")]
            srcs = [w_in[:, :, c:c + 256] for c in starts]
            srcs[8:8] = [w1[a][i] for a in range(2) for i in range(2)]
            for n in range(START["up"]):
                slot(n, v8, srcs[n])
                if n >= 4:
                    m = n - 4
                    ada_load(0, m % 2, m // 2, m // 2)
            for n in range(4):
                w = A["w_up_nsa" if n < 2 else "w_up_swa"][0].rearrange("(g t d) c -> g d t c", g=2, d=HD)
                s = START["up"] + n
                c0 = 512 * (n % 2)
                sp.wait_ge(lo_done, before(s))
                sp.dma_start(v4(raw, RING[s])[0:HD], w[0][:, :, c0:c0 + 512]).then_inc(loaded[RING[s]], 16)
                sp.dma_start(v4(raw, RING[s])[HD:P], w[1][:, :, c0:c0 + 512]).then_inc(loaded[RING[s]], 16)
            w_out = A["w_out"][0].rearrange("(k p) c -> p k c", p=P)
            for n in range(4):
                slot(START["out"] + n, v8, w_out[:, :, 256 * n:256 * n + 256])

            mi = A["w_mlp_in"][0]
            mo = A["w_mlp_out"][0]
            b = START["mlp"]

            def mlp_load_in(i, i0):
                n = b + i_local(i0)
                c = bass.ds(i * 256, 256) if not isinstance(i, int) else slice(i * 256, i * 256 + 256)
                load(n, RING[n], before(n) + 2 * (i - i0), v8(raw, RING[n]), mi[:, c].rearrange("(k p) c -> p k c", p=P))

            def mlp_load_out(i, i0):
                n = b + o_local(i0)
                r = bass.ds(i * 256, 256) if not isinstance(i, int) else slice(i * 256, i * 256 + 256)
                load(n, RING[n], before(n) + 2 * (i - i0), v2k(raw, RING[n]), mo[r, :].rearrange("(k p) c -> p k c", p=P))

            def mlp_pair(j, j0, last=False):
                i, i0 = 2 * j, 2 * j0
                mlp_load_out(i, i0)
                ada_load(1, 0, j, j0)
                if not last:
                    mlp_load_in(i + 2, i0 + 2)
                mlp_load_out(i + 1, i0 + 1)
                ada_load(1, 1, j, j0)
                if not last:
                    mlp_load_in(i + 3, i0 + 3)

            mlp_load_in(0, 0)
            mlp_load_in(1, 1)
            mlp_pair(0, 0)
            mlp_pair(1, 1)
            with sp.Fori(2, MLP_N // 2 - 1) as j:
                mlp_pair(j, 2)
            mlp_pair(MLP_N // 2 - 1, MLP_N // 2 - 1, last=True)

            def ffn(name, layer, sub):
                b = START[name]
                wi, wo = A["ffn_w_in_2"][layer, sub], A["ffn_w_out_2"][layer, sub]
                s = SESSION[name]

                def body(i, i0, with_ada):
                    n = b + 3 * i0 - 1
                    for q in range(2):
                        if not isinstance(i, int):
                            c = bass.ds(i * 256 + q * FF2, 256)
                        else:
                            c = slice(i * 256 + q * FF2, i * 256 + q * FF2 + 256)
                        load(n + q, q, before(n + q) + 3 * (i - i0), v8(raw, q), wi[:, c].rearrange("(k p) c -> p k c", p=P))
                        if q == 0 and with_ada:
                            ada_load(s, 0, i - 1, i0 - 1)
                    r = bass.ds((i - 1) * 256, 256) if not isinstance(i, int) else slice((i - 1) * 256, i * 256)
                    load(n + 2, 2, before(n + 2) + 3 * (i - i0), v2k(raw, 2), wo[r, :].rearrange("(k p) c -> p k c", p=P))
                    if with_ada and len(ADA_SESSIONS[s]) > 1:
                        ada_load(s, 1, i - 1, i0 - 1)

                for q in range(2):
                    slot(b + q, v8, wi[:, q * FF2:q * FF2 + 256].rearrange("(k p) c -> p k c", p=P))
                body(1, 1, s is not None)
                body(2, 2, s is not None)
                with sp.Fori(3, KT + 1) as i:
                    body(i, 3, s is not None)
                with sp.Fori(KT + 1, FFN_N) as i:
                    body(i, KT + 1, False)
                slot(b + 3 * FFN_N - 1, v2k, wo[FF2 - 256:FF2, :].rearrange("(k p) c -> p k c", p=P))

            ffn(*ffn_phase[0])
            slot(START["pool"], v8, A["pool_w_2"][0].rearrange("g (k p) c -> p (g k) c", p=P))
            ffn(*ffn_phase[1])
            w_kv = A["w_kv_2"].rearrange("(k p) c -> p k c", p=P)
            for n in range(8):
                slot(START["kv"] + n, v8, w_kv[:, :, 256 * n:256 * n + 256])
            ffn(*ffn_phase[2])
            for name, key in (("wq", "w_q_2"), ("wo", "w_o_2")):
                w = A[key][0].rearrange("(k p) c -> p k c", p=P)
                for n in range(4):
                    slot(START[name] + n, v8, w[:, :, 256 * n:256 * n + 256])
            ffn(*ffn_phase[3])
            for t in range(2):
                sp.wait_ge(out_copied, 2 * (t + 1))
                sp.dma_start(out[0, t * P:(t + 1) * P, :], xin[:, t, :]).then_inc(out_dma, 16)
            sp.wait_ge(out_dma, 32)

        @block.gpsimd
        def _(pool):
            for dst, src in late_loads():
                pool.dma_start(dst, src).then_inc(late_in, 16)
            nc.gpsimd.memset(hsplit[:, 960:1060].bitcast(F32), 0.0).then_inc(parts_clear, 1)
            pool.wait_ge(bvec_done, 1)
            pool.dma_start(bias_dram.rearrange("q h c -> h q c"),
                           bvec.unsqueeze(1).to_broadcast([16, P, 384])).then_inc(bvec_out, 16)
            pool.wait_ge(in_taken, 3)
            for g in range(2):
                src = kvr[g * HD:(g + 1) * HD]
                pool.dma_start(kvx[0:HD, :, g, :], src).then_inc(kvx_in, 16)
                pool.dma_start(kvx[HD:P, :, g, 0:T - 1], src[:, :, 1:T]).then_inc(kvx_in, 16)
            pool.wait_ge(bvec_out, 16)

            def toeplitz(h, count):
                return bass.AP(bias_dram.tensor, 127 + 384 * h, [[16 * 384 - 1, P], [384, count], [1, T]])

            pool.dma_start(bias_nsa, toeplitz(0, NH)).then_inc(bias_in, 16)
            pool.dma_start(bias_swa[1], toeplitz(NH + 6, 2)).then_inc(bias_in, 16)
            pool.wait_ge(blk_full, 2)
            pool.wait_ge(kvx_in, 64)
            pool.dma_start(bias_swa[0], toeplitz(NH, 6)).then_inc(bias_in, 16)
            pool.wait_ge(o_lo, 4)
            pool.wait_ge(bias_in, 48)
            pool.dma_start(cst[:, CST["cos"][0]:], cst_dram[:, CST["cos"][0]:]).then_inc(rotary_in, 16)

        @block.tensor
        def _(pe):
            def mm3(o, wh, wl, xh, xl, start, stop, skip=False):
                nc.tensor.matmul(o, wh, xh, start=start, stop=False, skip_group_check=skip)
                nc.tensor.matmul(o, wh, xl, start=False, stop=False, skip_group_check=skip)
                return nc.tensor.matmul(o, wl, xh, start=False, stop=stop, skip_group_check=skip)

            def dense8(n, pos, o, pre=None, lo_at=None):
                pe.wait_ge(lo_done, lo_at if lo_at is not None else n + 1)
                wh, wl = v8(whi, pos), v8(wlo, pos)
                for m in range(2):
                    for k in range(KT):
                        if pre is not None and m == 0:
                            pe.wait_ge(u_lo, pre + k + 1)
                        ins = mm3(o[:, m * T:(m + 1) * T], wh[:, k, m * P:(m + 1) * P], wl[:, k, m * P:(m + 1) * P],
                                  uhi[:, k, :], ulo[:, k, :], k == 0, k == KT - 1)
                ins.then_inc(pe_done, 1)

            def norm_part(e, q):
                pe.wait_ge(sq_ready, 4 * e + q + 1)
                for k in (2 * q, 2 * q + 1):
                    ins = nc.tensor.matmul(bank[6][:, 0:T], ones, full[:, k, :], start=k == 0, stop=k == KT - 1,
                                           skip_group_check=True)
                if q == 3:
                    ins.then_inc(ss_done, 1)

            def norm_sum(e, done=0):
                for q in range(done, 4):
                    norm_part(e, q)

            def ada_reduce(s):
                w = len(ADA_SESSIONS[s])
                pe.wait_ge(ada_used, ADA_START[s] + KT * w)
                for a in range(w):
                    for j in range(16):
                        ins = nc.tensor.matmul(bank[7][:, 16 * a + j:16 * a + j + 1], acc[:, a, j * P:(j + 1) * P],
                                               ones[:, 0:1], start=True, stop=True)
                ins.then_inc(ada_sum, 1)

            pe.wait_ge(cst_in, 16)
            pe.wait_ge(x_in, 16)
            for k in range(KT):
                for t in range(2):
                    ins = nc.tensor.transpose(bank[k // 2][:, (k % 2) * T + t * P:(k % 2) * T + (t + 1) * P],
                                              xin[:, t, k * P:(k + 1) * P], ident)
                if k % 2:
                    ins.then_inc(x_turned, 1)
            pe.wait_ge(mix_pre_in, 16)
            nc.tensor.transpose(bank[7][:, 384:392], vrows[0:8, 0, :], ident[0:8, 0:8]).then_inc(mix_pre_t, 1)
            norm_sum(0)
            pe.wait_ge(consts_in, 16 * (N_CONSTS - 1))
            pe.wait_ge(mix_pre_done, 1)
            nc.tensor.transpose(bank[7][:, 384:384 + NVEC], vrows[0:NVEC, 0, :], ident[0:NVEC, 0:NVEC]).then_inc(vec_t, 1)
            pe.wait_ge(late_in, 16 * N_LATE)
            pe.wait_ge(root_done, 1)
            nc.tensor.transpose(bank[6][:, 128:208], vrows[0:80, 1, :], ident[0:80, 0:80])
            nc.tensor.transpose(bank[6][:, 208:288], vrows[0:80, 2, :], ident[0:80, 0:80])
            nc.tensor.transpose(bank[6][:, 288:320], vrows[0:32, 3, :], ident[0:32, 0:32]).then_inc(late_t, 1)
            pe.wait_ge(vec_done, 1)
            nc.tensor.matmul(bank[7][0:16, 0:384], relb, onehot, start=True, stop=True).then_inc(bvec_mm, 1)

            pool6 = [0, 1, 2, 3, 4, 5]

            def q_pair(n):
                pe.wait_ge(lo_done, n + 2)
                p = RING[n]
                for t in range(4):
                    o = bank[pool6[(n + t // 2) % 6]][:, (t % 2) * T:(t % 2 + 1) * T]
                    for k in range(KT):
                        if n == 0 and t == 0:
                            pe.wait_ge(u_lo, k + 1)
                        wh, wl = pair_view(whi, p)[:, 4 * k + t, :, :], pair_view(wlo, p)[:, 4 * k + t, :, :]
                        wh, wl = wh.rearrange("p g d -> p (g d)"), wl.rearrange("p g d -> p (g d)")
                        ins = mm3(o, wh, wl, uhi[:, k, :], ulo[:, k, :], k == 0, k == KT - 1)
                ins.then_inc(pe_done, 2)

            def k_and_v(n):
                pe.wait_ge(lo_done, n + 1)
                wh, wl = v8(whi, RING[n]), v8(wlo, RING[n])
                o = bank[pool6[n % 6]]
                for k in range(KT):
                    mm3(o[:, 0:T], wh[:, k, 0:P], wl[:, k, 0:P], uhi[:, k, :], ulo[:, k, :], k == 0, k == KT - 1)
                for t in range(2):
                    for k in range(KT):
                        ins = mm3(o[:, T + t * P:T + (t + 1) * P], uhi[:, k, t * P:(t + 1) * P],
                                  ulo[:, k, t * P:(t + 1) * P], wh[:, k, P:2 * P], wl[:, k, P:2 * P], k == 0, k == KT - 1)
                ins.then_inc(pe_done, 1)

            n = 0
            while n < 8:
                if n >= 5:
                    pe.wait_ge(in_taken, n - 4)
                if n in (0, 3):
                    q_pair(n)
                    n += 2
                    continue
                if n in (5, 6, 7):
                    k_and_v(n)
                else:
                    dense8(n, RING[n], bank[pool6[n % 6]])
                n += 1
            pe.wait_ge(late_done, 1)
            for t in range(2):
                for k in range(KT):
                    ins = nc.tensor.matmul(bank[6][:, 256 + 24 * t:280 + 24 * t], full[:, k, t * P:(t + 1) * P], wg[:, k, :],
                                           start=k == 0, stop=k == KT - 1)
            ins.then_inc(gate_mm, 1)

            def output_gates(j):
                n = START["gate"] + j
                pe.wait_ge(in_taken, 7 + j)
                dense8(n, RING[n], bank[j % 2])

            pe.wait_ge(in_taken, 6)
            pe.wait_ge(parts_clear, 1)
            for a in range(2):
                pe.wait_ge(blk_lo, a + 1)
                for ii in range(16):
                    n = START["cmp"] + 2 * a + ii // 8
                    if ii % 8 == 0:
                        pe.wait_ge(lo_done, n + 1)
                    c = 30 * ii
                    ins = mm3(bank[4 + a][:, 0:T], hsplit[:, c:c + P], hsplit[:, 480 + c:480 + c + P],
                              v8(whi, RING[n])[:, ii % 8, :],
                              v8(wlo, RING[n])[:, ii % 8, :], ii == 0, ii == 15)
                    if ii % 8 == 7:
                        ins.then_inc(pe_done, 1)
            output_gates(0)
            pe.wait_ge(gate_done, 1)
            for a in range(2):
                pe.wait_ge(gelu_done, a + 1)
                for m in range(2):
                    ins = nc.tensor.transpose(bank[6][:, 32 * (2 * a + m):32 * (2 * a + m) + 30],
                                              hrow[:, a, m * P:(m + 1) * P], ident[0:30, 0:30])
            ins.then_inc(h1_turned, 1)
            pe.wait_ge(h1_done, 1)
            for g in range(2):
                for m in range(2):
                    nc.tensor.matmul(bank[4][g * HD:(g + 1) * HD, 256:256 + NCMP], w2[:, 0, m, :],
                                     h1[:, 0, m, g * NCMP:(g + 1) * NCMP], start=m == 0, stop=m == 1)
            for g in range(2):
                for m in range(2):
                    ins = nc.tensor.matmul(bank[5][0:NCMP, 256 + g * HD:256 + (g + 1) * HD],
                                           h1[:, 1, m, g * NCMP:(g + 1) * NCMP], w2[:, 1, m, :], start=m == 0, stop=m == 1)
            ins.then_inc(ckv_mm, 1)

            pe.wait_ge(ckv_done, 1)
            for h in range(NH):
                g, t = h // 4, h % 4
                for qt in range(2):
                    c = qt * 64 + t * 16
                    ins = nc.tensor.matmul(bank[4 + g][:, c:c + NCMP],
                                           qn[g * HD:(g + 1) * HD, t, qt * P:(qt + 1) * P], kcT[g * HD:(g + 1) * HD, 0:NCMP],
                                           start=True, stop=True)
            ins.then_inc(cs_mm, 1)
            output_gates(1)
            output_gates(2)
            output_gates(3)
            pe.wait_ge(cs_prob, 1)
            for h in range(NH):
                for qt in range(2):
                    b = [2, 3, 6, 7][h // 2]
                    c = (h % 2) * T + qt * P
                    ins = nc.tensor.transpose(bank[b][0:NCMP, c:c + P], cmpE[:, qt, h, 0:NCMP], ident)
            ins.then_inc(cs_turned, 1)
            output_gates(4)

            def gates_quarter(u):
                for j, at in GATE_STEPS.items():
                    if u not in at:
                        continue
                    n = START["gate"] + j
                    if u == at[0]:
                        pe.wait_ge(lo_done, n + 1)
                        if j < 7:
                            pe.wait_ge(in_taken, {5: 12, 6: 14}[j])
                        else:
                            pe.wait_ge(o_taken, 1)
                    m, half_k = at.index(u) // 2, at.index(u) % 2
                    wh, wl = v8(whi, RING[n]), v8(wlo, RING[n])
                    for k in range(4 * half_k, 4 * half_k + 4):
                        ins = mm3(bank[GATE_BANK[j]][:, m * T:(m + 1) * T], wh[:, k, m * P:(m + 1) * P],
                                  wl[:, k, m * P:(m + 1) * P], uhi[:, k, :], ulo[:, k, :], k == 0, k == KT - 1)
                    if u == at[-1]:
                        ins.then_inc(pe_done, 1)
                if u == 1:
                    pe.wait_ge(cs_done, 4)

            def attention(count, base, q_of, k_of, v_of, o_of, before_pv, start_of, stop_of, between=None):
                for u in range(count + 3):
                    if u < count:
                        w = base + u
                        if w >= 2:
                            pe.wait_ge(s_max, w - 1)
                        sc = bank[4 + w % 2]
                        q, k = q_of(u), k_of(u)
                        nc.tensor.matmul(sc[:, 0:P], q[:, 0:P], k[:, 0:P], start=True, stop=True)
                        nc.tensor.matmul(sc[:, P:384], q[:, P:T], k, start=True, stop=True).then_inc(s_mm, 1)
                    v = u - 2
                    if 0 <= v < count:
                        w = base + v
                        pe.wait_ge(s_prob, w + 1)
                        if w >= 2:
                            pe.wait_ge(s_copied, w - 1)
                        for b in range(3):
                            ins = nc.tensor.transpose(bank[6 + w % 2][:, b * P:(b + 1) * P],
                                                      prob[w % 3][:, b * P:(b + 1) * P], ident)
                        ins.then_inc(s_turned, 1)
                    v = u - 3
                    if 0 <= v < count:
                        w = base + v
                        pe.wait_ge(s_copied, w + 1)
                        before_pv(v)
                        pT = probT[w % 2]
                        nc.tensor.matmul(o_of(v), v_of(v, 0), pT[:, 0:T], start=start_of(v), stop=False)
                        nc.tensor.matmul(o_of(v)[:, P:T], v_of(v, 1), pT[:, T:384], start=False,
                                         stop=stop_of(v)).then_inc(s_pv, 1)
                    if between is not None:
                        between(u)

            def half(h):
                return slice((h // 4) * HD, (h // 4 + 1) * HD)

            def o1(u):
                b, h = units[u]
                t = h % 4
                return bank[(2 if b == 2 else 0) + t // 2][half(h), (t % 2) * T:(t % 2 + 1) * T]

            def compressed_first(u):
                b, h = units[u]
                if b == 0:
                    if u in (NH, 2 * NH):
                        pe.wait_ge(in_taken, 13 if u == NH else 15)
                    nc.tensor.matmul(o1(u), vcs[0:NCMP, h // 4, :], pcT[:, h, :], start=True, stop=False)

            pe.wait_ge(cs_dve, 1)
            attention(NU, 0,
                      lambda u: (qs if units[u][0] == 2 else qn)[half(units[u][1]), units[u][1] % 4, :],
                      lambda u: kT[half(units[u][1]), units[u][0], :],
                      lambda u, kt: vv[:, units[u][0], kt, half(units[u][1])],
                      o1, compressed_first, lambda u: units[u][0] == 2, lambda u: units[u][0] >= 1, gates_quarter)

            upbanks = [4, 6, 0, 2]
            for q in range(4):
                n = START["up"] + q
                pe.wait_ge(lo_done, n + 1)
                pe.wait_ge(o_lo, 4)
                for m in range(4):
                    for k in range(4):
                        o = bank[upbanks[q] + m // 2][:, (m % 2) * T:(m % 2 + 1) * T]
                        kk = k + 4 * (q // 2)
                        ins = mm3(o, v4(whi, RING[n])[:, k, m * P:(m + 1) * P], v4(wlo, RING[n])[:, k, m * P:(m + 1) * P],
                                  uhi[:, kk, :], ulo[:, kk, :], k == 0, k == 3)
                ins.then_inc(pe_done, 1)
            pe.wait_ge(y_taken, 2)
            ada_reduce(0)
            for q in range(4):
                n = START["out"] + q
                if q == 0:
                    pe.wait_ge(y_lo, 2)
                dense8(n, RING[n], bank[q])
                if q > 1:
                    norm_part(1, q - 2)
            norm_sum(1, 2)
            norm_sum(2)

            b = START["mlp"]

            def out_chunk(pos, first, last, e=None):
                hh = uhi_flat[:, 0:512] if last else hhi
                hl = ulo_flat[:, 0:512] if last else hlo
                wh, wl = v2k(whi, pos), v2k(wlo, pos)
                for m in range(KT):
                    for k in range(2):
                        ins = mm3(bank[m // 2][:, (m % 2) * T:(m % 2 + 1) * T], wh[:, k, m * P:(m + 1) * P],
                                  wl[:, k, m * P:(m + 1) * P], hh[:, k * T:(k + 1) * T], hl[:, k * T:(k + 1) * T],
                                  first and k == 0 and m % 2 == 0, last and k == 1, skip=True)
                    if last and m in (1, 3, 5):
                        ins.then_inc(f_ready, 1)
                    if last and e is not None and m == 5:
                        norm_part(e, 0)
                ins.then_inc(pe_done, 1)

            def mlp_in_mm(i, i0):
                loc = b + i_local(i0)
                if not (isinstance(i, int) and i < 2):
                    pe.wait_ge(h_full, i - 1)
                dense8(None, RING[loc], bank[4 + i0 % 2], pre=8 if isinstance(i, int) and i == 0 else None,
                       lo_at=loc + 1 + 2 * (i - i0))

            def mlp_out_mm(i, i0, first=False, last=False):
                loc = b + o_local(i0)
                pe.wait_ge(lo_done, loc + 1 + 2 * (i - i0))
                pe.wait_ge(h_lo, i + 1)
                out_chunk(RING[loc], first, last, 3)

            mlp_in_mm(0, 0)
            mlp_in_mm(1, 1)
            mlp_out_mm(0, 0, first=True)
            mlp_in_mm(2, 2)
            mlp_out_mm(1, 1)
            with pe.Fori(1, MLP_N // 2 - 1) as j:
                mlp_in_mm(2 * j + 1, 3)
                mlp_out_mm(2 * j, 2)
                mlp_in_mm(2 * j + 2, 4)
                mlp_out_mm(2 * j + 1, 3)
            mlp_in_mm(MLP_N - 1, MLP_N - 1)
            mlp_out_mm(MLP_N - 2, MLP_N - 2)
            mlp_out_mm(MLP_N - 1, MLP_N - 1, last=True)
            norm_sum(3, 1)
            norm_sum(4)
            ada_reduce(1)

            FFN_NORM = {"ffn0": 5, "ffn1": 7, "ffn2": 8, "ffn3": None}

            def ffn(name, pre):
                b = START[name]
                hb = H_BASE[name]

                def gate_up(i, i0):
                    for q in range(2):
                        loc = b + (q if i0 == 0 else 3 * i0 - 1 + q)
                        if q == 0 and not (isinstance(i, int) and i == 0):
                            pe.wait_ge(h_full, hb + i)
                        dense8(None, RING[loc], bank[4 + q], pre=pre if i0 == 0 and q == 0 else None,
                               lo_at=loc + 1 + 3 * (i - i0))

                def down(i, i0, first=False, last=False):
                    loc = b + (3 * i0 + 4 if i0 < FFN_N - 1 else 3 * FFN_N - 1)
                    pe.wait_ge(lo_done, loc + 1 + 3 * (i - i0))
                    pe.wait_ge(h_lo, hb + i + 1)
                    out_chunk(RING[loc], first, last, FFN_NORM[name])

                gate_up(0, 0)
                gate_up(1, 1)
                down(0, 0, first=True)
                with pe.Fori(2, FFN_N) as i:
                    gate_up(i, 2)
                    down(i - 1, 1)
                if name == "ffn2":
                    pe.wait_ge(mods_done, 4)
                    ada_reduce(4)
                down(FFN_N - 1, FFN_N - 1, last=True)

            ffn("ffn0", 16)
            norm_sum(5, 1)
            pe.wait_ge(mods_done, 2)
            ada_reduce(2)

            n = START["pool"]
            pe.wait_ge(lo_done, n + 1)
            for g in range(4):
                pe.wait_ge(pool_lo, 2 * g + 2)
                for m in range(2):
                    for k in range(2):
                        ins = mm3(bank[g][:, m * T:(m + 1) * T], v8(whi, RING[n])[:, 2 * g + k, m * P:(m + 1) * P],
                                  v8(wlo, RING[n])[:, 2 * g + k, m * P:(m + 1) * P], uhi[:, 2 * g + k, :],
                                  ulo[:, 2 * g + k, :], k == 0, k == 1)
                ins.then_inc(f_ready if g < 3 else pe_done, 1)
                if g == 2:
                    norm_part(6, 0)
            norm_sum(6, 1)
            ffn("ffn1", 24)
            norm_sum(7, 1)
            pe.wait_ge(mods_done, 3)
            ada_reduce(3)

            def head_sums(r):
                for b in range(4):
                    pe.wait_ge(r_copy, 8 * r + 2 * b + 2)
                    nc.tensor.matmul(bank[b][:, :], ones, hroot[:, 2 * b:2 * b + 2, :], start=True,
                                     stop=True).then_inc(r_ss, 1)

            def swap_halves(r):
                for b in range(4):
                    pe.wait_ge(r_root, 4 * r + b + 1)
                    src = q2 if r else tmp2
                    nc.tensor.matmul(bank[b][:, :], const("swap"), src[:, 2 * b:2 * b + 2, :], start=True,
                                     stop=True).then_inc(r_swap, 1)

            b = START["kv"]
            for n in range(4):
                dense8(b + n, RING[b + n], bank[n], pre=32 if n == 0 else None)
            for n in range(4, 8):
                if n == 5:
                    head_sums(0)
                if n == 6:
                    swap_halves(0)
                pe.wait_ge(lo_done, b + n + 1)
                if n >= 6:
                    pe.wait_ge(v2_taken, n - 5)
                wh, wl = v8(whi, RING[b + n]), v8(wlo, RING[b + n])
                for t in range(2):
                    for k in range(KT):
                        ins = mm3(bank[4 + n % 2][:, t * T:(t + 1) * T], uhi[:, k, t * P:(t + 1) * P],
                                  ulo[:, k, t * P:(t + 1) * P], wh[:, k, :], wl[:, k, :], k == 0, k == KT - 1)
                ins.then_inc(pe_done, 1)
            pe.wait_ge(v2_taken, 4)
            pe.wait_ge(r_done, 4)
            ffn("ffn2", 40)
            norm_sum(8, 1)

            b = START["wq"]
            for n in range(4):
                dense8(b + n, RING[b + n], bank[n], pre=48 if n == 0 else None)
            head_sums(1)
            swap_halves(1)

            def rotated(u):
                pe.wait_ge(r_done, 4 + u // 2 + 1)
                return q2[:, u, :]

            attention(8, NU, rotated, lambda u: k2[:, u, :],
                      lambda u, kt: v2[:, kt, u * P:(u + 1) * P],
                      lambda u: bank[u // 2][:, (u % 2) * T:(u % 2 + 1) * T],
                      lambda u: None, lambda u: True, lambda u: True)
            b = START["wo"]
            pe.wait_ge(o_lo, 8)
            for n in range(4):
                dense8(b + n, RING[b + n], bank[n])
                if n > 1:
                    norm_part(9, n - 2)
            norm_sum(9, 2)
            ffn("ffn3", 56)

            pe.wait_ge(x_ready, 36)
            for t in range(2):
                for k in range(KT):
                    ins = nc.tensor.transpose(bank[4 + 2 * t + k // 4][:, (k % 4) * P:(k % 4 + 1) * P],
                                              xT[:, k, t * P:(t + 1) * P], ident)
                    if k % 4 == 3:
                        ins.then_inc(out_turned, 1)

        @block.scalar
        def _(act):
            own = [0]

            def link(ins):
                own[0] += 1
                ins.then_inc(act_own, 1)
                act.wait_ge(act_own, own[0])

            def conv_at(pos, full_at, free_at):
                act.wait_ge(loaded[pos], full_at)
                if free_at is not None:
                    act.wait_ge(pe_done, free_at)
                nc.scalar.activation(whi[:, pos, :], raw[:, pos, :], ACT.Copy).then_inc(hi_done, 1)

            def conv(n):
                if n == len(RING):
                    return
                if n in QSLOTS:
                    act.wait_ge(loaded[RING[n]], filled(n))
                    if n > 2:
                        act.wait_ge(pe_done, 2)
                    nc.scalar.activation(split_views(whi, n), raw_view(n), ACT.Copy).then_inc(hi_done, 1)
                    return
                conv_at(RING[n], filled(n), before(n) or None)

            def square_x(e, version):
                for q in range(4):
                    act.wait_ge(x_ready, 4 * version - 3 + q)
                    nc.scalar.activation(full[:, 2 * q:2 * q + 2, :], xT[:, 2 * q:2 * q + 2, :],
                                         ACT.Square).then_inc(sq_ready, 1)

            def square_f(name):
                for q in range(4):
                    wait_bank(act, name, q)
                    nc.scalar.activation(full[:, 2 * q:2 * q + 2, :], bank[q][:], ACT.Square).then_inc(sq_ready, 1)

            def take_root(e):
                act.wait_ge(ss_done, e + 1)
                link(nc.scalar.activation(root[:], bank[6][:, 0:T], ACT.Ln, bias=eps[:], scale=1.0 / D))
                nc.scalar.activation(root[:], root[:], ACT.Exp, scale=-0.5).then_inc(root_done, 1)

            LN_EXP, SILU, GELU = "natural_log_exp_and_others", "silu_and_others", "gelu_apprx_tanh_and_others"

            def split_u(p, free, shift=None):
                if free:
                    act.wait_ge(pe_done, free)
                for k in range(KT):
                    act.wait_ge(u_full, 8 * p + k + 1)
                    if shift is None:
                        nc.scalar.activation(uhi[:, k, :], full[:, k, :], ACT.Copy).then_inc(u_hi, 1)
                    else:
                        nc.scalar.activation(uhi[:, k, :], full[:, k, :], ACT.Identity,
                                             bias=shift[:, k:k + 1]).then_inc(u_hi, 1)

            for n, (dst, src) in enumerate(const_loads()):
                act.dma_start(dst, src).then_inc(consts_in if n else mix_pre_in, 16)
            nc.scalar.preload_act_table_set(LN_EXP)
            act.wait_ge(x_ready, 4)
            square_x(0, 1)
            conv(0)
            take_root(0)
            conv(1)
            split_u(0, 0)
            conv(2)
            act.wait_ge(vec_done, 1)
            nc.scalar.activation(csilu[:], vec[:, VEC["c"]:VEC["c"] + 8], ACT.Silu).then_inc(c_ready, 1)

            def entries_hi(a):
                act.wait_ge(blk_full, a + 1)
                nc.scalar.activation(bpart_hi, blk[:, a, :], ACT.Copy).then_inc(blk_hi, 1)

            for n in range(8):
                act.wait_ge(pe_done, {0: 2, 3: 5}.get(n, n + 1))
                o = bank[n % 6]
                if n in (0, 1):
                    ins = nc.scalar.activation(qn[:, 2 * n:2 * n + 2, :], o[:], ACT.Copy, scale=HD ** -0.5)
                elif n in (3, 4):
                    ins = nc.scalar.activation(qs[:, 2 * n - 6:2 * n - 4, :], o[:], ACT.Copy, scale=HD ** -0.5)
                elif n == 2:
                    ins = nc.scalar.activation(kvr, o[:], ACT.Copy)
                else:
                    nc.scalar.activation(kT[:, n - 5, :], o[:, 0:T], ACT.Copy)
                    ins = nc.scalar.activation(vv[:, n - 5, :, :], o[:, T:2 * T], ACT.Copy)
                ins.then_inc(in_taken, 1)
                conv(n + 3)
                if n == 6:
                    entries_hi(0)
            act.wait_ge(gate_mm, 1)
            nc.scalar.activation(gate3[:], bank[6][:, 256:304], ACT.Sigmoid).then_inc(gate_done, 1)
            conv(START["cmp"] + 3)

            def take_gates(j):
                act.wait_ge(pe_done, START["gate"] + j + 1)
                nc.scalar.activation(gates[:, 2 * j:2 * j + 2, :], bank[j % 2][:], ACT.Sigmoid).then_inc(in_taken, 1)

            nc.scalar.preload_act_table_set(GELU)
            for a in range(2):
                act.wait_ge(pe_done, START["cmp"] + 2 * a + 2)
                if a == 0:
                    entries_hi(1)
                nc.scalar.activation(hrow[:, a, :], bank[4 + a][0:30, 0:T], ACT.Gelu_apprx_tanh).then_inc(gelu_done, 1)
                conv(START["gate"] + a)
            conv(START["gate"] + 2)
            take_gates(0)
            act.wait_ge(h1_turned, 1)
            nc.scalar.activation(h1[:].rearrange("p a m c -> p (a m) c")[:, :, 0:30],
                                 bank[6][:, 0:P].rearrange("p (a c) -> p a c", a=4)[:, :, 0:30], ACT.Copy).then_inc(h1_done, 1)
            act.wait_ge(ckv_mm, 1)
            nc.scalar.activation(kcT[:, 0:NCMP], bank[4][:, 256:256 + NCMP], ACT.Copy)
            nc.scalar.activation(vcs[0:NCMP, :, :], bank[5][0:NCMP, 256:256 + 2 * HD], ACT.Copy).then_inc(ckv_done, 1)
            conv(START["gate"] + 3)
            act.wait_ge(cs_dve, 2)
            nc.scalar.activation(cmpE[:, :, :, 0:NCMP], cmpE[:, :, :, 0:NCMP], ACT.Exp).then_inc(cs_exp, 1)
            for j in range(1, 4):
                take_gates(j)
                conv(START["gate"] + 3 + j)
            act.wait_ge(cs_turned, 1)
            for q in range(4):
                nc.scalar.activation(pcT[:, 2 * q:2 * q + 2, :], bank[[2, 3, 6, 7][q]][0:NCMP, :],
                                     ACT.Copy).then_inc(cs_done, 1)

            def take_raw_gates(j):
                act.wait_ge(pe_done, START["gate"] + j + 1)
                nc.scalar.activation(gates[:, 2 * j:2 * j + 2, :], bank[GATE_BANK[j]][:], ACT.Copy).then_inc(in_taken, 1)
                if j in (5, 6):
                    conv(START["gate"] + 3 + j)

            take_raw_gates(4)

            def take_between(u):
                if u == 2:
                    conv(START["gate"] + 7)
                for j, at in GATE_TAKEN.items():
                    if u == at:
                        take_raw_gates(j)
                if u == SLIDING_TAKEN:
                    act.wait_ge(s_pv, NH)
                    for q in range(2):
                        nc.scalar.activation(o_swa[:, 2 * q:2 * q + 2, :], bank[2 + q][:], ACT.Copy).then_inc(o_taken, 1)

            def attention(count, base, sink_of, between=None):
                for u in range(count + 2):
                    if u < count:
                        w = base + u
                        act.wait_ge(s_max, w + 1)
                        sm = small[:, w % 3, :]
                        pr = prob[w % 3]
                        if sink_of(u) is not None:
                            for t in range(2):
                                nc.scalar.activation(sm[:, 4 + t:5 + t], sink_of(u), ACT.Exp, bias=sm[:, t:t + 1])
                        nc.scalar.activation(pr[:, 0:P], pr[:, 0:P], ACT.Exp, bias=sm[:, 0:1], accum_out=sm[:, 2:3])
                        nc.scalar.activation(pr[:, P:384], pr[:, P:384], ACT.Exp, bias=sm[:, 1:2],
                                             accum_out=sm[:, 3:4]).then_inc(s_exp, 1)
                    v = u - 2
                    if 0 <= v < count:
                        w = base + v
                        act.wait_ge(s_turned, w + 1)
                        if w >= 2:
                            act.wait_ge(s_pv, w - 1)
                        nc.scalar.activation(probT[w % 2], bank[6 + w % 2][:, 0:384], ACT.Copy).then_inc(s_copied, 1)
                    if between is not None:
                        between(u)

            attention(NU, 0, lambda u: sinks[:, units[u][1]:units[u][1] + 1] if units[u][0] == 2 else None, take_between)
            act.wait_ge(in_taken, 16)
            act.wait_ge(o_taken, 2)
            for q in (2, 3):
                nc.scalar.activation(uhi[:, 2 * q:2 * q + 2, :], o_swa[:, 2 * q - 4:2 * q - 2, :], ACT.Copy).then_inc(o_hi, 1)
            act.wait_ge(s_pv, NU)
            for q in (0, 1):
                nc.scalar.activation(uhi[:, 2 * q:2 * q + 2, :], bank[q][:], ACT.Copy).then_inc(o_hi, 1)
            conv(START["up"] + 2)
            nc.scalar.activation(gates[:, 8:16, :], gates[:, 8:16, :], ACT.Sigmoid).then_inc(gates_ready, 1)

            for q in range(4):
                conv(START["up"] + 3 + q)
            act.wait_ge(pe_done, START["up"] + 4)
            for q in range(2):
                act.wait_ge(y_full, q + 1)
                nc.scalar.activation(uhi[:, 4 * q:4 * q + 4, :], full[:, 4 * q:4 * q + 4, :], ACT.Copy).then_inc(y_hi, 1)
            conv(START["out"] + 3)
            nc.scalar.preload_act_table_set(LN_EXP)
            square_f("out")
            conv(START["mlp"])
            take_root(1)
            square_x(2, 2)
            conv(START["mlp"] + 1)
            take_root(2)
            split_u(1, START["out"] + 4)

            b = START["mlp"]

            def split_h(i, o_done, last=False):
                act.wait_ge(h_full, i + 1)
                if o_done is not None:
                    act.wait_ge(pe_done, o_done)
                nc.scalar.activation(uhi_flat[:, 0:512] if last else hhi, hfull, ACT.Copy).then_inc(h_hi, 1)

            def sub(i, i0, conv_in=True):
                act.wait_ge(pe_done, b + i_local(i0) + 1 + 2 * (i - i0))
                nc.scalar.activation(act_g, bank[4 + i0 % 2][:], ACT.Relu).then_inc(g_act, 1)
                if isinstance(i, int) and i == MLP_N - 1:
                    split_h(i, None, last=True)
                else:
                    split_h(i, b + o_local(i0 - 1) + 1 + 2 * (i - i0) if i0 > 0 else None)
                n = b + o_local(i0)
                conv_at(RING[n], filled(n) + 16 * (i - i0), before(n) + 2 * (i - i0))
                if conv_in:
                    n = b + i_local(i0 + 2)
                    conv_at(RING[n], filled(n) + 8 * (i - i0), before(n) + 2 * (i - i0))

            sub(0, 0)
            sub(1, 1)
            sub(2, 2)
            sub(3, 3)
            with act.Fori(2, MLP_N // 2 - 1) as j:
                sub(2 * j, 4)
                sub(2 * j + 1, 5)
            sub(MLP_N - 2, MLP_N - 2, conv_in=False)
            sub(MLP_N - 1, MLP_N - 1, conv_in=False)

            b0 = START["ffn0"]
            conv(b0)
            nc.scalar.preload_act_table_set(LN_EXP)
            square_f("mlp")
            take_root(3)
            conv(b0 + 1)
            square_x(4, 3)
            take_root(4)
            split_u(2, b0, mods[:, 0, :])

            def ffn(name):
                b = START[name]
                hb = H_BASE[name]

                def evac(i, i0):
                    loc = b + (1 if i0 == 0 else 3 * i0)
                    act.wait_ge(pe_done, loc + 1 + 3 * (i - i0))
                    nc.scalar.activation(act_g, bank[4][:], ACT.Silu).then_inc(g_act, 1)

                def step(i, i0):
                    n = b + 3 * i0 - 1
                    conv_at(0, filled(n) + 16 * (i - i0), before(n) + 3 * (i - i0))
                    evac(i - 1, i0 - 1)
                    conv_at(1, filled(n + 1) + 16 * (i - i0), before(n + 1) + 3 * (i - i0))
                    split_h(hb + i - 1, before(n + 2) + 3 * (i - i0))
                    conv_at(2, filled(n + 2) + 16 * (i - i0), before(n + 2) + 3 * (i - i0))

                nc.scalar.preload_act_table_set(SILU)
                step(1, 1)
                step(2, 2)
                with act.Fori(3, FFN_N) as i:
                    step(i, 3)
                conv(b + 3 * FFN_N - 1)
                evac(FFN_N - 1, FFN_N - 1)
                split_h(hb + FFN_N - 1, None, last=True)
                conv(b + 3 * FFN_N)

            ffn("ffn0")
            n = START["pool"]
            conv(n + 1)
            nc.scalar.preload_act_table_set(LN_EXP)
            square_x(5, 4)
            take_root(5)
            for k in range(KT):
                act.wait_ge(pool_normed, k + 1)
                nc.scalar.activation(pool_a[:, k, 16:], full[:, k, :], ACT.Identity,
                                     bias=mods[:, 3, k:k + 1]).then_inc(pool_shifted, 1)
            for k in range(KT):
                act.wait_ge(pool_full, k // 2 + 1)
                nc.scalar.activation(uhi[:, k, :], full[:, k, :], ACT.Identity,
                                     bias=scal[:, NEG_SHIFT, k:k + 1]).then_inc(pool_hi, 1)
            square_x(6, 5)
            conv(n + 2)
            take_root(6)
            split_u(3, n + 1, mods[:, 6, :])
            ffn("ffn1")
            b = START["kv"]
            conv(b + 1)
            nc.scalar.preload_act_table_set(LN_EXP)
            square_x(7, 6)
            take_root(7)
            split_u(4, b, mods[:, 18, :])
            conv(b + 2)

            def rotary(r, done, scalar, dst):
                for q in range(4):
                    act.wait_ge(pe_done, done - 3 + q)
                    nc.scalar.activation(dst[:, 2 * q:2 * q + 2, :], bank[q][:], ACT.Copy, scale=scalar).then_inc(r_copy, 1)
                    nc.scalar.activation(hroot[:, 2 * q:2 * q + 2, :], bank[q][:], ACT.Square).then_inc(r_copy, 1)
                    conv_next(r, q)

            def conv_next(r, q):
                n = (START["kv"] if r == 0 else START["wq"]) + 3 + q
                if r == 1 and q == 3:
                    return
                conv(n)

            def rotary_root(r):
                for q in range(4):
                    act.wait_ge(r_ss, 4 * r + q + 1)
                    h = hroot[:, 2 * q:2 * q + 2, :]
                    link(nc.scalar.activation(h, bank[q][:], ACT.Ln, bias=eps[:], scale=1.0 / P))
                    nc.scalar.activation(h, h, ACT.Exp, scale=-0.5).then_inc(r_root, 1)

            def take_v(n):
                act.wait_ge(pe_done, b + 5 + n)
                nc.scalar.activation(v2[:, :, 256 * n:256 * n + 256], bank[4 + n % 2][:], ACT.Copy).then_inc(v2_taken, 1)

            rotary(0, b + 4, vec[:, VEC["k_norm"]:VEC["k_norm"] + 1], tmp2)
            take_v(0)
            conv(b + 7)
            rotary_root(0)
            for n in range(1, 4):
                take_v(n)
                if n == 2:
                    conv(START["ffn2"])
            split_u(5, b + 8, mods[:, 9, :])
            conv(START["ffn2"] + 1)
            act.wait_ge(r_done, 4)
            ffn("ffn2")
            b = START["wq"]
            conv(b + 1)
            nc.scalar.preload_act_table_set(LN_EXP)
            square_x(8, 7)
            take_root(8)
            split_u(6, b, mods[:, 12, :])
            conv(b + 2)
            rotary(1, b + 4, scal[:, QSC, 0:1], q2)
            rotary_root(1)
            conv(b + 6)
            attention(8, NU, lambda u: None)
            act.wait_ge(s_pv, NU + 8)
            for q in range(4):
                nc.scalar.activation(uhi[:, 2 * q:2 * q + 2, :], bank[q][:], ACT.Copy).then_inc(o_hi, 1)
            conv(b + 7)
            b = START["ffn3"]
            square_x(9, 8)
            conv(b)
            take_root(9)
            conv(b + 1)
            split_u(7, b, mods[:, 15, :])
            ffn("ffn3")
            for t in range(2):
                for c in range(2):
                    act.wait_ge(out_turned, 2 * t + c + 1)
                    nc.scalar.activation(xin[:, t, c * 512:(c + 1) * 512], bank[4 + 2 * t + c][:],
                                         ACT.Copy).then_inc(out_copied, 1)

        @block.vector
        def _(dve):
            own = [0]

            def link(ins):
                own[0] += 1
                ins.then_inc(dve_own, 1)
                dve.wait_ge(dve_own, own[0])

            def conv_at(pos, hi_at):
                dve.wait_ge(hi_done, hi_at)
                nc.vector.tensor_tensor(wlo[:, pos, :], raw[:, pos, :], whi[:, pos, :].bitcast(F32),
                                        ALU.subtract).then_inc(lo_done, 1)

            def conv(n):
                if n == len(RING):
                    return
                if n in QSLOTS:
                    dve.wait_ge(hi_done, n + 1)
                    nc.vector.tensor_tensor(split_views(wlo, n), raw_view(n), split_views(whi, n).bitcast(F32),
                                            ALU.subtract).then_inc(lo_done, 1)
                    return
                conv_at(RING[n], n + 1)

            def ada_add(s, a, k, k0):
                w = len(ADA_SESSIONS[s])
                m = ADA_START[s] + k0 * w + a
                step = 0 if isinstance(k, int) else w
                buf = ADA_BUF[m]
                per = sum(1 for q in range(w) if q % 2 == buf)
                if step == 0:
                    dve.wait_ge(ada_loaded[buf], ada_filled(m))
                else:
                    dve.wait_ge(ada_loaded[buf], ada_filled(m) + 16 * per * (k - k0))
                if isinstance(k, int) and k == 0:
                    if s > 0:
                        dve.wait_ge(ada_sum, s)
                    nc.vector.tensor_scalar(acc[:, a, :], ada[:, buf, :], csilu[:, 0:1], None,
                                            ALU.mult).then_inc(ada_used, 1)
                    return
                dve.wait_ge(ada_used, ada_acc_before(m) + step * (k - k0))
                c = csilu[:, k:k + 1] if isinstance(k, int) else csilu[:, bass.ds(k, 1)]
                nc.vector.scalar_tensor_tensor(out=acc[:, a, :], in0=ada[:, buf, :], scalar=c, in1=acc[:, a, :],
                                               op0=ALU.mult, op1=ALU.add).then_inc(ada_used, 1)

            def take_mods(s):
                dve.wait_ge(ada_sum, s + 1)
                w = ADA_SESSIONS[s]
                for a, pair in enumerate(w):
                    for i, m in enumerate(PAIR_MODS[pair]):
                        c = 16 * a + 8 * i
                        ins = nc.vector.tensor_tensor(mods[:, m, :], bank[7][:, c:c + 8], adab[:, 8 * m:8 * m + 8], ALU.add)
                ins.then_inc(mods_done, 1)
                dve.wait_ge(mods_done, s + 1)

            def gain(i, m, g):
                link(nc.vector.scalar_tensor_tensor(out=scal[:, i, :], in0=mods[:, m, :], scalar=1.0, in1=g,
                                                    op0=ALU.add, op1=ALU.mult))

            def weight(i, m, w):
                link(nc.vector.tensor_scalar(scal[:, i, :], mods[:, m, :], 1.0, w, ALU.add, ALU.mult))

            def norm_g(layer, sub):
                a = VEC["norm_g"] + 8 * (3 * layer + sub)
                return vec[:, a:a + 8]

            def make_u(e, p, a, shift=None):
                dve.wait_ge(root_done, e + 1)
                if p > 0:
                    dve.wait_ge(u_lo, 8 * p)
                for kk in range(KT + 2):
                    if kk < KT:
                        nc.vector.scalar_tensor_tensor(out=full[:, kk, :], in0=xT[:, kk, :], scalar=a[:, kk:kk + 1],
                                                       in1=root[:], op0=ALU.mult, op1=ALU.mult).then_inc(u_full, 1)
                    k = kk - 2
                    if k < 0:
                        continue
                    dve.wait_ge(u_hi, 8 * p + k + 1)
                    if shift is None:
                        nc.vector.tensor_tensor(ulo[:, k, :], full[:, k, :], uhi[:, k, :].bitcast(F32),
                                                ALU.subtract).then_inc(u_lo, 1)
                    else:
                        nc.vector.scalar_tensor_tensor(out=ulo[:, k, :], in0=full[:, k, :], scalar=shift[:, k:k + 1],
                                                       in1=uhi[:, k, :].bitcast(F32), op0=ALU.add,
                                                       op1=ALU.subtract).then_inc(u_lo, 1)

            def add_normed(e, g, version):
                dve.wait_ge(root_done, e + 1)
                for q in range(5):
                    if q < 4:
                        for k in (2 * q, 2 * q + 1):
                            ins = nc.vector.scalar_tensor_tensor(
                                out=full[:, k, :], in0=bank[k // 2][:, (k % 2) * T:(k % 2 + 1) * T],
                                scalar=g[:, k:k + 1], in1=root[:], op0=ALU.mult, op1=ALU.mult)
                        ins.then_inc(f_normed, 1)
                    if q > 0:
                        dve.wait_ge(f_normed, 4 * (version - 2) + q)
                        s = slice(2 * q - 2, 2 * q)
                        nc.vector.tensor_tensor(xT[:, s, :], xT[:, s, :], full[:, s, :], ALU.add).then_inc(x_ready, 1)
                dve.wait_ge(x_ready, 4 * version)

            def add_scaled(c, version, name):
                for k in range(KT):
                    if k % 2 == 0:
                        wait_bank(dve, name, k // 2)
                    ins = nc.vector.scalar_tensor_tensor(out=xT[:, k, :], in0=bank[k // 2][:, (k % 2) * T:(k % 2 + 1) * T],
                                                         scalar=c[:, k:k + 1], in1=xT[:, k, :], op0=ALU.mult, op1=ALU.add)
                    if k % 2:
                        ins.then_inc(x_ready, 1)
                dve.wait_ge(x_ready, 4 * version)

            nc.vector.memset(eps[:], EPS)
            for q in range(4):
                dve.wait_ge(x_turned, q + 1)
                nc.vector.tensor_copy(xT[:, 2 * q:2 * q + 2, :], bank[q][:]).then_inc(x_ready, 1)
            dve.wait_ge(mix_pre_t, 1)
            nc.vector.tensor_copy(vec[:, 0:8], bank[7][:, 384:392]).then_inc(mix_pre_done, 1)
            conv(0)
            dve.wait_ge(x_ready, 4)
            dve.wait_ge(mix_pre_done, 1)
            conv(1)
            dve.wait_ge(vec_t, 1)
            nc.vector.tensor_copy(vec[:, 8:NVEC], bank[7][:, 392:384 + NVEC]).then_inc(vec_done, 1)
            make_u(0, 0, vec[:, vrow("mix_pre")])
            conv(2)
            dve.wait_ge(late_t, 1)
            nc.vector.tensor_copy(adab[:], bank[6][:, 128:288])
            nc.vector.tensor_copy(posx[:].rearrange("p a b -> p (a b)"), bank[6][:, 288:320]).then_inc(late_done, 1)
            dve.wait_ge(bvec_mm, 1)
            nc.vector.tensor_tensor(bvec, bank[7][0:16, 0:384], dmask, ALU.add).then_inc(bvec_done, 1)
            dve.wait_ge(c_ready, 1)

            def conv_and_ada(n):
                conv(n)
                if n >= 4:
                    ada_add(0, n % 2, (n - 4) // 2, (n - 4) // 2)

            for n in range(3, 8):
                conv_and_ada(n)

            dve.wait_ge(kvx_in, 64)
            for a in range(2):
                entries = blk[:, a, :].rearrange("p (i g j) -> p i g j", i=16, g=2)
                for g in range(2):
                    tok = kvx[:, a, g, :].rearrange("p (j i r) -> p i j r", i=8, r=2)
                    for s in range(2):
                        ins = nc.vector.tensor_tensor(
                            entries[:, 8 * s:8 * s + 8, g, :], tok[:, :, s:s + NCMP, 0],
                            posx[:, a, 8 * s:8 * s + 8].unsqueeze(2).to_broadcast([P, 8, NCMP]), ALU.add)
                ins.then_inc(blk_full, 1)

            def entries_lo(a):
                dve.wait_ge(blk_hi, a + 1)
                nc.vector.tensor_tensor(bpart_lo, blk[:, a, :], bpart_hi.bitcast(F32), ALU.subtract).then_inc(blk_lo, 1)

            entries_lo(0)
            link(nc.vector.tensor_scalar(scal[:, QSC, 0:1], vec[:, VEC["q_norm"]:VEC["q_norm"] + 1], P ** -0.5, None, ALU.mult))
            for n in range(START["cmp"], START["gate"] + 3):
                if n == START["gate"]:
                    entries_lo(1)
                conv_and_ada(n)

            E = cmpE[:, :, :, 0:NCMP]
            S = [cmpS[:, i, :].rearrange("p (t h) -> p t h", t=2) for i in range(3)]

            def over_blocks(a):
                return a.unsqueeze(3).to_broadcast([P, 2, 8, NCMP])

            dve.wait_ge(cs_mm, 1)
            mask = const("cmpmask").rearrange("p (t n) -> p t n", t=2)
            for t in range(2):
                for g in range(2):
                    sc = bank[4 + g][:, t * 64:(t + 1) * 64].rearrange("p (h n) -> p h n", h=4)[:, :, 0:NCMP]
                    ins = nc.vector.tensor_tensor(E[:, t, 4 * g:4 * g + 4, :], sc,
                                                  mask[:, t:t + 1, 0:NCMP].to_broadcast([P, 4, NCMP]), ALU.add)
            ins.then_inc(cs_dve, 1)
            dve.wait_ge(cs_dve, 1)
            link(nc.vector.tensor_reduce(S[0], E, AX.X, ALU.max))
            link(nc.vector.tensor_scalar(S[0], S[0], FLOOR, None, ALU.max))
            nc.vector.tensor_tensor(E, E, over_blocks(S[0]), ALU.subtract).then_inc(cs_dve, 1)
            conv_and_ada(START["gate"] + 3)
            dve.wait_ge(cs_exp, 1)
            link(nc.vector.tensor_reduce(S[1], E, AX.X, ALU.add))
            link(nc.vector.tensor_scalar(S[1], S[1], 1e-30, None, ALU.max))
            link(nc.vector.reciprocal(S[2], S[1]))
            dve.wait_ge(gate_done, 1)
            link(nc.vector.tensor_tensor(S[2], S[2], gate3[:].rearrange("p t (h c) -> p t h c", c=3)[:, :, :, 0], ALU.mult))
            nc.vector.tensor_tensor(E, E, over_blocks(S[2]), ALU.mult).then_inc(cs_prob, 1)
            for n in range(START["gate"] + 4, START["gate"] + 6):
                conv_and_ada(n)

            def conv_between(u):
                for i, at in enumerate((1, 4)):
                    n = START["gate"] + 6 + i
                    if u == at:
                        conv(n)
                    if u == at + 1:
                        ada_add(0, n % 2, (n - 4) // 2, (n - 4) // 2)
                for j, at in GATE_TAKEN.items():
                    if u == at + 1:
                        conv(START["gate"] + 3 + j)

            def attention(count, base, bias_of, sink_of, gate_of, between=None):
                for u in range(count + 1):
                    if u < count:
                        w = base + u
                        sm = small[:, w % 3, :]
                        pr = prob[w % 3]
                        dve.wait_ge(s_mm, w + 1)
                        if w >= 3:
                            dve.wait_ge(s_turned, w - 2)
                        b = bias_of(u)
                        nc.vector.tensor_tensor(pr[:, 0:P], bank[4 + w % 2][:, 0:P], b[:, P:T], ALU.add)
                        link(nc.vector.tensor_tensor(pr[:, P:384], bank[4 + w % 2][:, P:384], b, ALU.add))
                        nc.vector.tensor_reduce(sm[:, 6:7], pr[:, 0:P], AX.X, ALU.max)
                        link(nc.vector.tensor_reduce(sm[:, 7:8], pr[:, P:384], AX.X, ALU.max))
                        if sink_of(u) is not None:
                            link(nc.vector.tensor_tensor(sm[:, 6:8], sm[:, 6:8], sink_of(u).to_broadcast([P, 2]), ALU.max))
                        nc.vector.tensor_scalar(sm[:, 0:2], sm[:, 6:8], -1.0, None, ALU.mult).then_inc(s_max, 1)
                    v = u - 1
                    if 0 <= v < count:
                        w = base + v
                        sm = small[:, w % 3, :]
                        pr = prob[w % 3]
                        dve.wait_ge(s_exp, w + 1)
                        if sink_of(v) is not None:
                            link(nc.vector.tensor_tensor(sm[:, 2:4], sm[:, 2:4], sm[:, 4:6], ALU.add))
                        link(nc.vector.reciprocal(sm[:, 8:10], sm[:, 2:4]))
                        if gate_of(v) is not None:
                            link(nc.vector.tensor_tensor(sm[:, 8:10], sm[:, 8:10], gate_of(v), ALU.mult))
                        nc.vector.tensor_scalar(pr[:, 0:P], pr[:, 0:P], sm[:, 8:9], None, ALU.mult)
                        nc.vector.tensor_scalar(pr[:, P:384], pr[:, P:384], sm[:, 9:10], None, ALU.mult).then_inc(s_prob, 1)
                    if between is not None:
                        between(u)

            def split_o(done):
                for q in range(4):
                    dve.wait_ge(o_hi, done + q + 1)
                    s = slice(2 * q, 2 * q + 2)
                    nc.vector.tensor_tensor(ulo[:, s, :], bank[q][:].rearrange("p (a b) -> p a b", a=2),
                                            uhi[:, s, :].bitcast(F32), ALU.subtract).then_inc(o_lo, 1)

            def bias_of(u):
                kind, h = units[u]
                return bias_swa[h // 6][:, h % 6, :] if kind == 2 else bias_nsa[:, h, :]

            dve.wait_ge(bias_in, 48)
            attention(NU, 0,
                      bias_of,
                      lambda u: sinks[:, units[u][1]:units[u][1] + 1] if units[u][0] == 2 else None,
                      lambda u: None if units[u][0] == 2 else gate3[:, :, 3 * units[u][1] + 1 + units[u][0]], conv_between)
            for i, q in enumerate((2, 3, 0, 1)):
                dve.wait_ge(o_hi, i + 1)
                s = slice(2 * q, 2 * q + 2)
                o = bank[q][:].rearrange("p (a b) -> p a b", a=2) if q < 2 else o_swa[:, 2 * q - 4:2 * q - 2, :]
                nc.vector.tensor_tensor(ulo[:, s, :], o, uhi[:, s, :].bitcast(F32), ALU.subtract).then_inc(o_lo, 1)
            conv(START["up"] + 2)

            for q in range(4):
                n = START["up"] + q
                dve.wait_ge(pe_done, n + 1)
                if q == 2:
                    dve.wait_ge(gates_ready, 1)
                for m in range(2):
                    t = 4 * q + 2 * m
                    ins = nc.vector.tensor_tensor(gates[:, t:t + 2, :], gates[:, t:t + 2, :],
                                                  bank[[4, 6, 0, 2][q] + m][:].rearrange("p (a b) -> p a b", a=2), ALU.mult)
                ins.then_inc(y_taken, 1)
                conv(n + 3)
            dve.wait_ge(y_taken, 4)
            for q in range(2):
                s = slice(4 * q, 4 * q + 4)
                nc.vector.tensor_tensor(full[:, s, :], gates[:, s, :], gates[:, 8 + 4 * q:12 + 4 * q, :], ALU.add).then_inc(y_full, 1)
            for q in range(2):
                s = slice(4 * q, 4 * q + 4)
                dve.wait_ge(y_hi, q + 1)
                nc.vector.tensor_tensor(ulo[:, s, :], full[:, s, :], uhi[:, s, :].bitcast(F32), ALU.subtract).then_inc(y_lo, 1)
            take_mods(0)
            gain(SA["ffn0"], 1, norm_g(0, 0))
            weight(SC["ffn0"], 2, 0.5)
            conv(START["out"] + 3)
            conv(START["mlp"])
            add_normed(1, vec[:, vrow("mix_post")], 2)
            conv(START["mlp"] + 1)
            make_u(2, 1, vec[:, vrow("mlp_pre")])

            b = START["mlp"]

            def split_h(i, last=False):
                dve.wait_ge(h_hi, i + 1)
                hi, lo = (uhi_flat[:, 0:512], ulo_flat[:, 0:512]) if last else (hhi, hlo)
                nc.vector.tensor_tensor(lo, hfull, hi.bitcast(F32), ALU.subtract).then_inc(h_lo, 1)

            def sub(i, i0, piece, j, j0, conv_in=True):
                dve.wait_ge(g_act, i + 1)
                if not isinstance(i, int) or i > 0:
                    dve.wait_ge(h_lo, i)
                nc.vector.tensor_tensor(hfull, act_g, act_g, ALU.mult).then_inc(h_full, 1)
                split_h(i, last=isinstance(i, int) and i == MLP_N - 1)
                n = b + o_local(i0)
                conv_at(RING[n], n + 1 + 2 * (i - i0))
                ada_add(1, piece, j, j0)
                if conv_in:
                    n = b + i_local(i0 + 2)
                    conv_at(RING[n], n + 1 + 2 * (i - i0))

            def pair(j, j0, conv_in=True):
                sub(2 * j, 2 * j0, 0, j, j0, conv_in)
                sub(2 * j + 1, 2 * j0 + 1, 1, j, j0, conv_in)

            pair(0, 0)
            pair(1, 1)
            with dve.Fori(2, MLP_N // 2 - 1) as j:
                pair(j, 2)
            pair(MLP_N // 2 - 1, MLP_N // 2 - 1, conv_in=False)

            b0 = START["ffn0"]
            conv(b0)
            add_normed(3, vec[:, vrow("mlp_post")], 3)
            conv(b0 + 1)
            make_u(4, 2, scal[:, SA["ffn0"], :], mods[:, 0, :])
            take_mods(1)
            gain(SA["pool"], 4, norm_g(0, 1))
            link(nc.vector.scalar_tensor_tensor(out=scal[:, SC["pool"], :], in0=mods[:, 5, :], scalar=1.0,
                                                in1=vec[:, vrow("pool_scale")], op0=ALU.add, op1=ALU.mult))
            gain(SA["ffn1"], 7, norm_g(0, 2))

            def ffn(name):
                b = START[name]
                hb = H_BASE[name]
                s = SESSION[name]

                def times_up(i):
                    dve.wait_ge(g_act, hb + i + 1)
                    dve.wait_ge(h_lo, hb + i)
                    nc.vector.tensor_tensor(hfull, act_g, bank[5][:], ALU.mult).then_inc(h_full, 1)

                def step(i, i0, with_ada):
                    n = b + 3 * i0 - 1
                    conv_at(0, n + 1 + 3 * (i - i0))
                    if with_ada:
                        ada_add(s, 0, i - 1, i0 - 1)
                    times_up(i - 1)
                    conv_at(1, n + 2 + 3 * (i - i0))
                    split_h(hb + i - 1)
                    conv_at(2, n + 3 + 3 * (i - i0))
                    if with_ada and len(ADA_SESSIONS[s]) > 1:
                        ada_add(s, 1, i - 1, i0 - 1)

                step(1, 1, s is not None)
                step(2, 2, s is not None)
                with dve.Fori(3, KT + 1) as i:
                    step(i, 3, s is not None)
                with dve.Fori(KT + 1, FFN_N) as i:
                    step(i, KT + 1, False)
                conv(b + 3 * FFN_N - 1)
                times_up(FFN_N - 1)
                split_h(hb + FFN_N - 1, last=True)
                conv(b + 3 * FFN_N)

            ffn("ffn0")
            n = START["pool"]
            add_scaled(scal[:, SC["ffn0"], :], 4, "ffn0")
            conv(n + 1)
            nc.vector.memset(pool_a[:, :, 0:16], 0.0)
            nc.vector.memset(pool_b[:, :, 0:16], 0.0)
            dve.wait_ge(root_done, 6)
            for k in range(KT):
                nc.vector.scalar_tensor_tensor(out=full[:, k, :], in0=xT[:, k, :], scalar=scal[:, SA["pool"], k:k + 1],
                                               in1=root[:], op0=ALU.mult, op1=ALU.mult).then_inc(pool_normed, 1)
            link(nc.vector.tensor_scalar(scal[:, NEG_SHIFT, :], mods[:, 3, :], -1.0, None, ALU.mult))
            dve.wait_ge(pool_shifted, 8)
            src, dst = pool_a, pool_b
            for g in range(4):
                s = 1 << g
                link(nc.vector.tensor_tensor(dst[:, 2 * g:, 16:], src[:, 2 * g:, 16:], src[:, 2 * g:, 16 - s:272 - s], ALU.add))
                own_tiles = dst[:, 2 * g:2 * g + 2, 16:]
                rc = const("poolrc")[:, g * 16:(g + 1) * 16].unsqueeze(1).to_broadcast([P, 2, 16])
                h = full[:, 2 * g:2 * g + 2, :]
                spare = src[:, 2 * g:2 * g + 2, 16:32]
                link(nc.vector.tensor_tensor(spare, own_tiles[:, :, 0:16], rc, ALU.mult))
                nc.vector.tensor_tensor(h[:, :, 0:16], spare, h[:, :, 0:16], ALU.subtract)
                nc.vector.scalar_tensor_tensor(out=h[:, :, 16:], in0=own_tiles[:, :, 16:], scalar=0.5 / s, in1=h[:, :, 16:],
                                               op0=ALU.mult, op1=ALU.subtract).then_inc(pool_full, 1)
                src, dst = dst, src
            for k in range(KT):
                dve.wait_ge(pool_hi, k + 1)
                nc.vector.scalar_tensor_tensor(out=ulo[:, k, :], in0=full[:, k, :], scalar=scal[:, NEG_SHIFT, k:k + 1],
                                               in1=uhi[:, k, :].bitcast(F32), op0=ALU.add,
                                               op1=ALU.subtract).then_inc(pool_lo, 1)
            add_scaled(scal[:, SC["pool"], :], 5, "pool")
            conv(n + 2)
            make_u(6, 3, scal[:, SA["ffn1"], :], mods[:, 6, :])
            take_mods(2)
            weight(SC["ffn1"], 8, 0.5)
            weight(SC["ffn3"], 17, 0.5)
            gain(SA["kv"], 19, vec[:, vrow("kv_norm")])
            ffn("ffn1")
            b = START["kv"]
            add_scaled(scal[:, SC["ffn1"], :], 6, "ffn1")
            conv(b + 1)
            make_u(7, 4, scal[:, SA["kv"], :], mods[:, 18, :])
            conv(b + 2)

            cos = const("cos").unsqueeze(1).to_broadcast([P, 2, T])
            sin = const("sin").unsqueeze(1).to_broadcast([P, 2, T])

            dve.wait_ge(rotary_in, 16)

            def rotary(r, src, turned, dst):
                for q in range(4):
                    s = slice(2 * q, 2 * q + 2)
                    dve.wait_ge(r_root, 4 * r + q + 1)
                    dve.wait_ge(r_swap, 4 * r + q + 1)
                    nc.vector.tensor_tensor(src[:, s, :], src[:, s, :], cos, ALU.mult)
                    link(nc.vector.tensor_tensor(turned[:, s, :], bank[q][:].rearrange("p (a b) -> p a b", a=2), sin, ALU.mult))
                    link(nc.vector.tensor_tensor(dst[:, s, :], src[:, s, :], turned[:, s, :], ALU.add))
                    nc.vector.tensor_tensor(dst[:, s, :], dst[:, s, :], hroot[:, s, :], ALU.mult).then_inc(r_done, 1)
                dve.wait_ge(r_done, 4 * r + 4)

            for q in range(5):
                conv(b + 3 + q)
            take_mods(3)
            gain(SA["ffn2"], 10, norm_g(1, 0))
            weight(SC["ffn2"], 11, 0.5)
            rotary(0, tmp2, k2, k2)
            conv(START["ffn2"])
            make_u(7, 5, scal[:, SA["ffn2"], :], mods[:, 9, :])
            conv(START["ffn2"] + 1)
            ffn("ffn2")
            b = START["wq"]
            add_scaled(scal[:, SC["ffn2"], :], 7, "ffn2")
            take_mods(4)
            gain(SA["moba"], 13, norm_g(1, 1))
            conv(b + 1)
            make_u(8, 6, scal[:, SA["moba"], :], mods[:, 12, :])
            conv(b + 2)
            for q in range(3):
                conv(b + 3 + q)
            weight(SC["moba"], 14, 1.0)
            gain(SA["ffn3"], 16, norm_g(1, 2))
            rotary(1, q2, tmp2, q2)
            attention(8, NU, lambda u: const("causal"), lambda u: None, lambda u: None)
            split_o(4)
            conv(b + 6)
            conv(b + 7)
            b = START["ffn3"]
            add_scaled(scal[:, SC["moba"], :], 8, "wo")
            conv(b)
            make_u(9, 7, scal[:, SA["ffn3"], :], mods[:, 15, :])
            conv(b + 1)
            ffn("ffn3")
            add_scaled(scal[:, SC["ffn3"], :], 9, "ffn3")


def kernel(**inputs):
    import concourse.bacc as bacc
    from concourse.bass_utils import run_bass_kernel_spmd

    nc = bacc.Bacc("TRN2", target_bir_lowering=False, num_devices=1)
    tables = dict(zip(("table_cst", "table_onehot", "table_mask"), shape_constants()))
    arrays, aps = {}, {}
    for name in NAMES:
        a = np.ascontiguousarray(inputs[name])
        arrays["in_" + name] = a
        aps[name] = nc.dram_tensor("in_" + name, a.shape, mybir.dt.from_np(a.dtype), kind="ExternalInput").ap()
    tabs = []
    for name, a in tables.items():
        arrays[name] = a
        tabs.append(nc.dram_tensor(name, a.shape, F32, kind="ExternalInput").ap())
    bias_rows = nc.dram_tensor("bias_rows", (P, 16, 384), F32, kind="Internal").ap()
    out = nc.dram_tensor("out_0", (1, T, D), F32, kind="ExternalOutput").ap()
    build(nc, aps, *tabs, bias_rows, out)
    r = run_bass_kernel_spmd(nc, [arrays], core_ids=[0])
    return r.results[0]["out_0"]
```
